# Optimizing a Trainium2 kernel written in Bass

```python
import math
import jax, jax.numpy as jnp
from jax import lax
import numpy as np

D_MODEL = 1024
BATCH = 1
SEQ = 256
DEPTH = 2

MIX_WIDTH = D_MODEL
RWKV_WIDTH = MIX_WIDTH // 2
HEAD_SIZE = 64
RWKV_HEADS = RWKV_WIDTH // HEAD_SIZE
DECAY_LORA = 64
AAA_LORA = 64
MV_LORA = 32
GATE_LORA = 128
RWKV_COLS = 3 * RWKV_WIDTH + DECAY_LORA + AAA_LORA + GATE_LORA
POOL_WIDTH = MIX_WIDTH - RWKV_WIDTH
POOL_WINDOWS = (2, 4, 8, 16)
POOL_GROUP = POOL_WIDTH // len(POOL_WINDOWS)
IN_COLS = RWKV_COLS + POOL_WIDTH
GN_EPS = 64e-5
NORM_EPS = 1e-6
N_KEYS = 128
N_EXPERTS = N_KEYS * N_KEYS
PEER_HEADS = 8
PEER_QDIM = 256
PEER_HALF = PEER_QDIM // 2
PEER_TOPK = 16
TOK_BLOCK = 128


def rmsnorm(x, g):
    x32 = x.astype(jnp.float32)
    y = x32 * lax.rsqrt(jnp.mean(x32 * x32, axis=-1, keepdims=True) + NORM_EPS)
    return (y * g.astype(jnp.float32)).astype(x.dtype)

def modulate(h, shift, scale):
    return h * (1 + scale[:, None, :]) + shift[:, None, :]

def token_shift(z, mu):
    prev = jnp.pad(z, ((0, 0), (1, 0), (0, 0)))[:, :-1]
    return z + (prev - z) * mu

def rwkv7_step(state, inp):
    r_t, w_t, k_t, v_t, kk_t, a_t = inp
    sa = jnp.einsum('bhvk,bhk->bhv', state, -kk_t)
    state = (state * w_t[:, :, None, :]
             + sa[..., None] * (kk_t * a_t)[:, :, None, :]
             + v_t[..., None] * k_t[:, :, None, :])
    y = jnp.einsum('bhvk,bhk->bhv', state, r_t)
    return state, y

def rwkv7_mix(r, k, v, wd, ad, gd, w0, w_up, a0, a_up, g_up, k_k, k_a, r_k, lnx_g, lnx_b):
    B, S, _ = r.shape
    f32 = jnp.float32
    w = -jax.nn.softplus(-(w0 + jnp.tanh(wd) @ w_up)) - 0.5
    decay = jnp.exp(-jnp.exp(w.astype(f32)))
    a = jax.nn.sigmoid(a0 + ad @ a_up)
    g = jax.nn.sigmoid(gd) @ g_up

    def heads(t):
        return t.reshape(B, S, RWKV_HEADS, HEAD_SIZE).astype(f32)

    kk = heads(k * k_k)
    kk = kk / jnp.maximum(jnp.sqrt(jnp.sum(kk * kk, axis=-1, keepdims=True)), 1e-12)
    k = k * (1 + (a - 1) * k_a)
    rh, kh, vh, ah, wh = heads(r), heads(k), heads(v), heads(a), heads(decay)
    tm = lambda t: jnp.moveaxis(t, 1, 0)
    s0 = jnp.zeros((B, RWKV_HEADS, HEAD_SIZE, HEAD_SIZE), f32)
    _, ys = lax.scan(rwkv7_step, s0, (tm(rh), tm(wh), tm(kh), tm(vh), tm(kk), tm(ah)))
    y = jnp.moveaxis(ys, 0, 1)
    mean = jnp.mean(y, axis=-1, keepdims=True)
    var = jnp.mean(jnp.square(y - mean), axis=-1, keepdims=True)
    yn = ((y - mean) * lax.rsqrt(var + GN_EPS)).reshape(B, S, RWKV_WIDTH)
    yn = yn * lnx_g.astype(f32) + lnx_b.astype(f32)
    bonus = jnp.sum(rh * kh * r_k.astype(f32), axis=-1, keepdims=True) * vh
    out = (yn + bonus.reshape(B, S, RWKV_WIDTH)) * g.astype(f32)
    return out.astype(r.dtype)

def multiscale_pool(p, pool_w, pool_scale):
    B, S, _ = p.shape
    f32 = jnp.float32
    p32 = p.astype(f32)
    cs = jnp.cumsum(p32, axis=1)
    pos = jnp.arange(1, S + 1, dtype=f32)
    groups = []
    for j, win in enumerate(POOL_WINDOWS):
        sl = slice(j * POOL_GROUP, (j + 1) * POOL_GROUP)
        csj = cs[..., sl]
        lag = jnp.pad(csj, ((0, 0), (win, 0), (0, 0)))[:, :S]
        mean = (csj - lag) / jnp.minimum(pos, float(win))[None, :, None]
        groups.append(mean - p32[..., sl])
    d = jnp.stack(groups, axis=2)
    out = jnp.einsum('bsgc,gcd->bsgd', d, pool_w.astype(f32)).reshape(B, S, POOL_WIDTH)
    return (out * pool_scale.astype(f32)).astype(p.dtype)

def peer_ffn(h, peer_q, peer_keys, peer_u, peer_v):
    B, S, D = h.shape
    q = (h @ peer_q).reshape(B, S, PEER_HEADS, 2, PEER_HALF)
    scores = jnp.einsum('bshpd,hpkd->bshpk', q, peer_keys)
    s, i = lax.top_k(scores, PEER_TOPK)
    cand_s = (s[..., 0, :, None] + s[..., 1, None, :]).reshape(B, S, PEER_HEADS, PEER_TOPK * PEER_TOPK)
    cand_i = (i[..., 0, :, None] * N_KEYS + i[..., 1, None, :]).reshape(B, S, PEER_HEADS, PEER_TOPK * PEER_TOPK)
    top_s, sel = lax.top_k(cand_s, PEER_TOPK)
    idx = jnp.take_along_axis(cand_i, sel, axis=-1)
    gate = jax.nn.softmax(top_s.astype(jnp.float32), axis=-1)
    T = B * S
    E = PEER_HEADS * PEER_TOPK
    nb = T // TOK_BLOCK
    hb = h.reshape(nb, TOK_BLOCK, D)
    ib = idx.reshape(nb, TOK_BLOCK, E)
    gb = gate.astype(h.dtype).reshape(nb, TOK_BLOCK, E)

    def block(args):
        hx, ix, gx = args
        u_sel = jnp.take(peer_u, ix, axis=0)
        v_sel = jnp.take(peer_v, ix, axis=0)
        act = jax.nn.gelu(jnp.einsum('td,ted->te', hx, u_sel), approximate=False)
        return jnp.einsum('te,ted->td', gx * act, v_sel)

    out = lax.map(block, (hb, ib, gb))
    return out.reshape(B, S, D)

def first_inputs(seed: int = 0) -> dict:
    key = jax.random.key(seed)
    ks = jax.random.split(key, 32)
    nrm = lambda k, shape, s: jax.random.normal(k, shape, jnp.float32) * s
    L, Lr = DEPTH, DEPTH - 1
    return {
        "x": nrm(ks[0], (BATCH, SEQ, D_MODEL), 1.0),
        "c": nrm(ks[1], (BATCH, D_MODEL), 1.0),
        "ada_w": nrm(ks[2], (L, D_MODEL, 6 * D_MODEL), 0.5 * D_MODEL ** -0.5),
        "ada_b": nrm(ks[3], (L, 6 * D_MODEL), 0.01),
        "ln1_g": 1.0 + nrm(ks[4], (L, D_MODEL), 0.01),
        "w_in": nrm(ks[5], (L, D_MODEL, IN_COLS), D_MODEL ** -0.5),
        "mu_shift": jax.random.uniform(ks[6], (L, RWKV_COLS), jnp.float32),
        "w0": nrm(ks[7], (L, RWKV_WIDTH), 0.5),
        "w_up": nrm(ks[8], (L, DECAY_LORA, RWKV_WIDTH), 0.1 * DECAY_LORA ** -0.5),
        "a0": nrm(ks[9], (L, RWKV_WIDTH), 0.1),
        "a_up": nrm(ks[10], (L, AAA_LORA, RWKV_WIDTH), 0.1 * AAA_LORA ** -0.5),
        "g_up": nrm(ks[11], (L, GATE_LORA, RWKV_WIDTH), GATE_LORA ** -0.5),
        "vres_down": nrm(ks[12], (Lr, D_MODEL, MV_LORA), D_MODEL ** -0.5),
        "vres_mu": jax.random.uniform(ks[13], (Lr, MV_LORA), jnp.float32),
        "vres_v0": 1.0 + nrm(ks[14], (Lr, RWKV_WIDTH), 0.1),
        "vres_up": nrm(ks[15], (Lr, MV_LORA, RWKV_WIDTH), 0.1 * MV_LORA ** -0.5),
        "k_k": 0.85 + nrm(ks[16], (L, RWKV_WIDTH), 0.02),
        "k_a": 1.0 + nrm(ks[17], (L, RWKV_WIDTH), 0.02),
        "r_k": -0.04 + nrm(ks[18], (L, RWKV_HEADS, HEAD_SIZE), 0.02),
        "lnx_g": 1.0 + nrm(ks[19], (L, RWKV_WIDTH), 0.01),
        "lnx_b": nrm(ks[20], (L, RWKV_WIDTH), 0.01),
        "pool_w": nrm(ks[21], (L, len(POOL_WINDOWS), POOL_GROUP, POOL_GROUP), POOL_GROUP ** -0.5),
        "pool_scale": 1.0 + nrm(ks[22], (L, POOL_WIDTH), 0.01),
        "w_out": nrm(ks[23], (L, MIX_WIDTH, D_MODEL), MIX_WIDTH ** -0.5),
        "ln2_g": 1.0 + nrm(ks[24], (L, D_MODEL), 0.01),
        "peer_q": nrm(ks[25], (L, D_MODEL, PEER_HEADS * PEER_QDIM), D_MODEL ** -0.5),
        "peer_keys": nrm(ks[26], (L, PEER_HEADS, 2, N_KEYS, PEER_HALF), PEER_HALF ** -0.5),
        "peer_u": nrm(ks[27], (L, N_EXPERTS, D_MODEL), D_MODEL ** -0.5),
        "peer_v": nrm(ks[28], (L, N_EXPERTS, D_MODEL), PEER_HEADS ** -0.5),
        "lnf_g": 1.0 + nrm(ks[29], (D_MODEL,), 0.01),
    }

def first_block(x, c, ada_w, ada_b, ln1_g, w_in, mu_shift, w0, w_up, a0, a_up, g_up,
              vres_down, vres_mu, vres_v0, vres_up, k_k, k_a, r_k, lnx_g, lnx_b,
              pool_w, pool_scale, w_out, ln2_g, peer_q, peer_keys, peer_u, peer_v, lnf_g):
    split_pts = [RWKV_WIDTH, 2 * RWKV_WIDTH, 3 * RWKV_WIDTH,
                 3 * RWKV_WIDTH + DECAY_LORA, 3 * RWKV_WIDTH + DECAY_LORA + AAA_LORA]
    c_act = jax.nn.silu(c)
    v_first = None
    for l in range(DEPTH):
        mod = c_act @ ada_w[l] + ada_b[l]
        sh1, sc1, g1, sh2, sc2, g2 = jnp.split(mod, 6, axis=-1)

        h = modulate(rmsnorm(x, ln1_g[l]), sh1, sc1)
        w_full = w_in[l] if l == 0 else jnp.concatenate([w_in[l], vres_down[l - 1]], axis=1)
        proj = h @ w_full
        rw = token_shift(proj[..., :RWKV_COLS], mu_shift[l])
        r, k, v, wd, ad, gd = jnp.split(rw, split_pts, axis=-1)
        pool_in = proj[..., RWKV_COLS:RWKV_COLS + POOL_WIDTH]
        if l == 0:
            v_first = v
        else:
            vd = token_shift(proj[..., RWKV_COLS + POOL_WIDTH:], vres_mu[l - 1])
            v = v + (v_first - v) * jax.nn.sigmoid(vres_v0[l - 1] + vd @ vres_up[l - 1])
        y_rwkv = rwkv7_mix(r, k, v, wd, ad, gd, w0[l], w_up[l], a0[l], a_up[l], g_up[l],
                           k_k[l], k_a[l], r_k[l], lnx_g[l], lnx_b[l])
        y_pool = multiscale_pool(pool_in, pool_w[l], pool_scale[l])
        mix = jnp.concatenate([y_rwkv, y_pool], axis=-1) @ w_out[l]
        x = x + g1[:, None, :] * mix

        h2 = modulate(rmsnorm(x, ln2_g[l]), sh2, sc2)
        x = x + g2[:, None, :] * peer_ffn(h2, peer_q[l], peer_keys[l], peer_u[l], peer_v[l])
    return rmsnorm(x, lnf_g)


N_A_LAYERS = DEPTH // 2
N_B_LAYERS = DEPTH - N_A_LAYERS
D_RNN = D_MODEL
LRU_HEADS = 4
LRU_BLOCK = D_RNN // LRU_HEADS
CONV_WIDTH = 4
LRU_C = 8.0
MLA_HEADS = 16
QK_NOPE = 64
QK_ROPE = 32
V_HEAD = 64
Q_LORA = 384
KV_LORA = 256
ROPE_THETA = 10000.0
Q_BLOCK = 128
ATTN_SCALE = 1.0 / math.sqrt(QK_NOPE + QK_ROPE)
N_EXPERTS_2 = N_KEYS * N_KEYS
PEER_HALF_2 = PEER_QDIM // 2
PEER_CHUNK = 128
RMS_EPS = 1e-6
NEG_INF = -1e30


def rmsnorm_2(x, g):
    xf = x.astype(jnp.float32)
    y = xf * lax.rsqrt(jnp.mean(xf * xf, axis=-1, keepdims=True) + RMS_EPS)
    return (y * g.astype(jnp.float32)).astype(x.dtype)

def rope(x, positions):
    half = QK_ROPE // 2
    freqs = ROPE_THETA ** (-jnp.arange(half, dtype=jnp.float32) / half)
    ang = positions.astype(jnp.float32)[..., None] * freqs
    ang = ang.reshape(ang.shape[:2] + (1,) * (x.ndim - 3) + (half,))
    cos, sin = jnp.cos(ang), jnp.sin(ang)
    xf = x.astype(jnp.float32)
    x1, x2 = xf[..., :half], xf[..., half:]
    out = jnp.concatenate([x1 * cos - x2 * sin, x1 * sin + x2 * cos], axis=-1)
    return out.astype(x.dtype)

def _lru_combine(left, right):
    a1, b1 = left
    a2, b2 = right
    return a1 * a2, a2 * b1 + b2

def rglru_block(h, w_in, conv_w, conv_b, wa, ba, wx, bx, lam, w_out):
    B, S, _ = h.shape
    gate_in, rec_in = jnp.split(h @ w_in, 2, axis=-1)
    gate = jax.nn.gelu(gate_in, approximate=False)
    xp = jnp.pad(rec_in, ((0, 0), (CONV_WIDTH - 1, 0), (0, 0)))
    xc = conv_b
    for k in range(CONV_WIDTH):
        xc = xc + xp[:, k:k + S] * conv_w[k]
    xb = xc.reshape(B, S, LRU_HEADS, LRU_BLOCK)
    r = jax.nn.sigmoid(jnp.einsum('bshi,hij->bshj', xb, wa).reshape(B, S, D_RNN) + ba)
    i = jax.nn.sigmoid(jnp.einsum('bshi,hij->bshj', xb, wx).reshape(B, S, D_RNN) + bx)
    log_a = -LRU_C * r.astype(jnp.float32) * jax.nn.softplus(-lam.astype(jnp.float32))
    a = jnp.exp(log_a)
    b = jnp.sqrt(-jnp.expm1(2.0 * log_a)) * (i * xc).astype(jnp.float32)
    _, hs = lax.associative_scan(_lru_combine, (a, b), axis=1)
    return (gate * hs.astype(h.dtype)) @ w_out

def shared_kv(x, c, kv_ada_w, kv_ada_b, kv_norm_g, w_dkv, w_kr, kv_latent_g, w_uk, w_uv, positions):
    B, S, _ = x.shape
    shift, scale = jnp.split((jax.nn.silu(c) @ kv_ada_w + kv_ada_b)[:, None, :], 2, axis=-1)
    h = rmsnorm_2(x, kv_norm_g) * (1.0 + scale) + shift
    c_kv = rmsnorm_2(h @ w_dkv, kv_latent_g)
    k_rope = rope(h @ w_kr, positions)
    k_nope = (c_kv @ w_uk).reshape(B, S, MLA_HEADS, QK_NOPE)
    v = (c_kv @ w_uv).reshape(B, S, MLA_HEADS, V_HEAD)
    return k_nope, k_rope, v

def _to_blocks(t, block):
    B, S = t.shape[:2]
    return jnp.moveaxis(t.reshape((B, S // block, block) + t.shape[2:]), 1, 0)

def _from_blocks(t):
    nb, B, blk = t.shape[:3]
    return jnp.moveaxis(t, 0, 1).reshape((B, nb * blk) + t.shape[3:])

def mla_block(h, w_dq, q_latent_g, w_uq, w_o, k_nope, k_rope, v, positions):
    B, S, _ = h.shape
    q_lat = rmsnorm_2(h @ w_dq, q_latent_g)
    q = (q_lat @ w_uq).reshape(B, S, MLA_HEADS, QK_NOPE + QK_ROPE)
    q_nope = q[..., :QK_NOPE]
    q_rope = rope(q[..., QK_NOPE:], positions)

    def attend(args):
        qn, qr, qpos = args
        s = (jnp.einsum('bqhd,bkhd->bhqk', qn, k_nope)
             + jnp.einsum('bqhr,bkr->bhqk', qr, k_rope)).astype(jnp.float32) * ATTN_SCALE
        mask = positions[:, None, None, :] <= qpos[:, None, :, None]
        p = jax.nn.softmax(jnp.where(mask, s, NEG_INF), axis=-1).astype(v.dtype)
        return jnp.einsum('bhqk,bkhd->bqhd', p, v)

    out = lax.map(attend, (_to_blocks(q_nope, Q_BLOCK), _to_blocks(q_rope, Q_BLOCK),
                           _to_blocks(positions, Q_BLOCK)))
    out = _from_blocks(out).reshape(B, S, MLA_HEADS * V_HEAD)
    return out @ w_o

def peer(h, w_q, sub_keys, u_tab, v_tab):
    B, S, _ = h.shape
    q = (h @ w_q).reshape(B, S, PEER_HEADS, 2, PEER_HALF_2)
    s = jnp.einsum('bshpd,hpnd->bshpn', q, sub_keys).astype(jnp.float32)
    v1, i1 = lax.top_k(s[..., 0, :], PEER_TOPK)
    v2, i2 = lax.top_k(s[..., 1, :], PEER_TOPK)
    cand = (v1[..., :, None] + v2[..., None, :]).reshape(B, S, PEER_HEADS, PEER_TOPK * PEER_TOPK)
    cv, ci = lax.top_k(cand, PEER_TOPK)
    e1 = jnp.take_along_axis(i1, ci // PEER_TOPK, axis=-1)
    e2 = jnp.take_along_axis(i2, ci % PEER_TOPK, axis=-1)
    idx = e1 * N_KEYS + e2
    g = jax.nn.softmax(cv, axis=-1).astype(h.dtype)

    def experts(args):
        hc, ic, gc = args
        act = jax.nn.gelu(jnp.einsum('bcd,bchkd->bchk', hc, u_tab[ic]), approximate=False)
        return jnp.einsum('bchk,bchkd->bcd', gc * act, v_tab[ic])

    out = lax.map(experts, (_to_blocks(h, PEER_CHUNK), _to_blocks(idx, PEER_CHUNK),
                            _to_blocks(g, PEER_CHUNK)))
    return _from_blocks(out)

def _normal(key, shape, fan_in):
    return jax.random.normal(key, shape, jnp.float32) * (fan_in ** -0.5)

def _gain(key, shape):
    return 1.0 + 0.02 * jax.random.normal(key, shape, jnp.float32)

def _bias(key, shape):
    return 0.02 * jax.random.normal(key, shape, jnp.float32)

def second_inputs(seed: int = 0) -> dict:
    key = jax.random.key(seed)
    ks = iter(jax.random.split(key, 40))
    D = D_MODEL
    x = jax.random.normal(next(ks), (BATCH, SEQ, D), jnp.float32)
    c = jax.random.normal(next(ks), (BATCH, D), jnp.float32)
    offset = jax.random.randint(next(ks), (BATCH, 1), 0, 1024, dtype=jnp.int32)
    positions = offset + jnp.arange(SEQ, dtype=jnp.int32)[None, :]
    u = jax.random.uniform(next(ks), (N_A_LAYERS, D_RNN), jnp.float32, 0.9, 0.999)
    a0 = u ** (1.0 / LRU_C)
    lru_lambda = jnp.log(a0) - jnp.log1p(-a0)
    return {
        'x': x, 'c': c, 'positions': positions,
        'ada_w': _normal(next(ks), (DEPTH, D, 6 * D), D),
        'ada_b': _bias(next(ks), (DEPTH, 6 * D)),
        'norm_mix_g': _gain(next(ks), (DEPTH, D)),
        'norm_ffn_g': _gain(next(ks), (DEPTH, D)),
        'lru_w_in': _normal(next(ks), (N_A_LAYERS, D, 2 * D_RNN), D),
        'lru_conv_w': _normal(next(ks), (N_A_LAYERS, CONV_WIDTH, D_RNN), CONV_WIDTH),
        'lru_conv_b': _bias(next(ks), (N_A_LAYERS, D_RNN)),
        'lru_wa': _normal(next(ks), (N_A_LAYERS, LRU_HEADS, LRU_BLOCK, LRU_BLOCK), LRU_BLOCK),
        'lru_ba': _bias(next(ks), (N_A_LAYERS, D_RNN)),
        'lru_wx': _normal(next(ks), (N_A_LAYERS, LRU_HEADS, LRU_BLOCK, LRU_BLOCK), LRU_BLOCK),
        'lru_bx': _bias(next(ks), (N_A_LAYERS, D_RNN)),
        'lru_lambda': lru_lambda,
        'lru_w_out': _normal(next(ks), (N_A_LAYERS, D_RNN, D), D_RNN),
        'kv_ada_w': _normal(next(ks), (D, 2 * D), D),
        'kv_ada_b': _bias(next(ks), (2 * D,)),
        'kv_norm_g': _gain(next(ks), (D,)),
        'mla_w_dkv': _normal(next(ks), (D, KV_LORA), D),
        'mla_w_kr': _normal(next(ks), (D, QK_ROPE), D),
        'mla_kv_latent_g': _gain(next(ks), (KV_LORA,)),
        'mla_w_uk': _normal(next(ks), (KV_LORA, MLA_HEADS * QK_NOPE), KV_LORA),
        'mla_w_uv': _normal(next(ks), (KV_LORA, MLA_HEADS * V_HEAD), KV_LORA),
        'mla_w_dq': _normal(next(ks), (N_B_LAYERS, D, Q_LORA), D),
        'mla_q_latent_g': _gain(next(ks), (N_B_LAYERS, Q_LORA)),
        'mla_w_uq': _normal(next(ks), (N_B_LAYERS, Q_LORA, MLA_HEADS * (QK_NOPE + QK_ROPE)), Q_LORA),
        'mla_w_o': _normal(next(ks), (N_B_LAYERS, MLA_HEADS * V_HEAD, D), MLA_HEADS * V_HEAD),
        'peer_w_q': _normal(next(ks), (DEPTH, D, PEER_HEADS * PEER_QDIM), D),
        'peer_sub_keys': _normal(next(ks), (DEPTH, PEER_HEADS, 2, N_KEYS, PEER_HALF_2), PEER_HALF_2),
        'peer_u': _normal(next(ks), (DEPTH, N_EXPERTS_2, D), D),
        'peer_v': _normal(next(ks), (DEPTH, N_EXPERTS_2, D), PEER_HEADS),
        'final_g': _gain(next(ks), (D,)),
    }

def second_block(x, c, positions, ada_w, ada_b, norm_mix_g, norm_ffn_g,
              lru_w_in, lru_conv_w, lru_conv_b, lru_wa, lru_ba, lru_wx, lru_bx, lru_lambda, lru_w_out,
              kv_ada_w, kv_ada_b, kv_norm_g, mla_w_dkv, mla_w_kr, mla_kv_latent_g, mla_w_uk, mla_w_uv,
              mla_w_dq, mla_q_latent_g, mla_w_uq, mla_w_o,
              peer_w_q, peer_sub_keys, peer_u, peer_v, final_g):
    k_nope = k_rope = v = None
    for l in range(DEPTH):
        if l == N_A_LAYERS:
            k_nope, k_rope, v = shared_kv(x, c, kv_ada_w, kv_ada_b, kv_norm_g, mla_w_dkv, mla_w_kr,
                                          mla_kv_latent_g, mla_w_uk, mla_w_uv, positions)
        mod = (jax.nn.silu(c) @ ada_w[l] + ada_b[l])[:, None, :]
        sh1, sc1, g1, sh2, sc2, g2 = jnp.split(mod, 6, axis=-1)
        h = rmsnorm_2(x, norm_mix_g[l]) * (1.0 + sc1) + sh1
        if l < N_A_LAYERS:
            y = rglru_block(h, lru_w_in[l], lru_conv_w[l], lru_conv_b[l], lru_wa[l], lru_ba[l],
                            lru_wx[l], lru_bx[l], lru_lambda[l], lru_w_out[l])
        else:
            j = l - N_A_LAYERS
            y = mla_block(h, mla_w_dq[j], mla_q_latent_g[j], mla_w_uq[j], mla_w_o[j],
                          k_nope, k_rope, v, positions)
        x = x + g1 * y
        h = rmsnorm_2(x, norm_ffn_g[l]) * (1.0 + sc2) + sh2
        x = x + g2 * peer(h, peer_w_q[l], peer_sub_keys[l], peer_u[l], peer_v[l])
    return rmsnorm_2(x, final_g)


def setup_inputs(seed=0):
    out = dict(first_inputs(seed))
    for name, value in second_inputs(seed + 1).items():
        if name != "x":
            out[name + "_2"] = value
    return out


def reference(
    x, c, ada_w, ada_b, ln1_g, w_in, mu_shift, w0, w_up, a0, a_up, g_up, vres_down, vres_mu,
    vres_v0, vres_up, k_k, k_a, r_k, lnx_g, lnx_b, pool_w, pool_scale, w_out, ln2_g, peer_q,
    peer_keys, peer_u, peer_v, lnf_g, c_2, positions_2, ada_w_2, ada_b_2, norm_mix_g_2,
    norm_ffn_g_2, lru_w_in_2, lru_conv_w_2, lru_conv_b_2, lru_wa_2, lru_ba_2, lru_wx_2,
    lru_bx_2, lru_lambda_2, lru_w_out_2, kv_ada_w_2, kv_ada_b_2, kv_norm_g_2, mla_w_dkv_2,
    mla_w_kr_2, mla_kv_latent_g_2, mla_w_uk_2, mla_w_uv_2, mla_w_dq_2, mla_q_latent_g_2,
    mla_w_uq_2, mla_w_o_2, peer_w_q_2, peer_sub_keys_2, peer_u_2, peer_v_2, final_g_2,
):
    x = first_block(
        x, c, ada_w, ada_b, ln1_g, w_in, mu_shift, w0, w_up, a0, a_up, g_up, vres_down, vres_mu,
        vres_v0, vres_up, k_k, k_a, r_k, lnx_g, lnx_b, pool_w, pool_scale, w_out, ln2_g, peer_q,
        peer_keys, peer_u, peer_v, lnf_g,
    )
    return second_block(
        x, c_2, positions_2, ada_w_2, ada_b_2, norm_mix_g_2, norm_ffn_g_2, lru_w_in_2,
        lru_conv_w_2, lru_conv_b_2, lru_wa_2, lru_ba_2, lru_wx_2, lru_bx_2, lru_lambda_2,
        lru_w_out_2, kv_ada_w_2, kv_ada_b_2, kv_norm_g_2, mla_w_dkv_2, mla_w_kr_2,
        mla_kv_latent_g_2, mla_w_uk_2, mla_w_uv_2, mla_w_dq_2, mla_q_latent_g_2, mla_w_uq_2,
        mla_w_o_2, peer_w_q_2, peer_sub_keys_2, peer_u_2, peer_v_2, final_g_2,
    )


_drawn_inputs = setup_inputs


def setup_inputs(seed=0):
    import zlib

    import numpy as np

    out = dict(_drawn_inputs(seed))
    spreads = {}
    factors = {'ln1_g': 4.77,
     'w_up': 5.05,
     'a0': 3.014,
     'a_up': 3.254,
     'vres_down': 5.455,
     'vres_mu': 6.845,
     'vres_v0': 5.183,
     'vres_up': 5.301,
     'k_k': 43.416,
     'k_a': 4.692,
     'r_k': 3.383,
     'lnx_g': 23.485,
     'lnx_b': 21.514,
     'pool_scale': 5.471,
     'ln2_g': 3.833,
     'lnf_g': 3.636,
     'norm_mix_g_2': 2.712,
     'norm_ffn_g_2': 3.09,
     'lru_ba_2': 8.0,
     'lru_bx_2': 5.598,
     'kv_ada_b_2': 5.929,
     'kv_norm_g_2': 8.0,
     'mla_kv_latent_g_2': 7.328,
     'mla_q_latent_g_2': 8.0,
     'final_g_2': 7.761}
    for name, (base, spread) in spreads.items():
        noise = np.random.default_rng([zlib.crc32(name.encode()), seed]).standard_normal(out[name].shape)
        drawn = base * np.exp(spread * noise) if base else spread * noise
        out[name] = __import__('jax').numpy.asarray(drawn.astype(out[name].dtype))
    for name, factor in factors.items():
        out[name] = (out[name] * factor).astype(out[name].dtype)
    return out
```

```python
from contextlib import ExitStack, contextmanager

import numpy as np

import concourse.bass as bass
from concourse import mybir

F32 = mybir.dt.float32
F32R = mybir.dt.float32r
U32 = mybir.dt.uint32
I32 = mybir.dt.int32
ALU = mybir.AluOpType
ACT = mybir.ActivationFunctionType
AX = mybir.AxisListType

P = 128
T = 256
D = 1024
DC = D // P
TT = T // P
RW = 512
G4 = RW // P
CH = 64
NCH = T // CH
HEADS = 8
TOPK = 16
KEYS = 128
EXPERTS = KEYS * KEYS
GN_EPS = 64e-5
EPS = 1e-6
DECAY = float(np.exp(-0.5))
WINDOWS = (2, 4, 8, 16)
AH = 16
ATT_SCALE = 1.0 / float(np.sqrt(96.0))
NEG = -1e30
LOWEST = -3.0e38

RAW = 4
SPL = 2

PCOLS = {}


def _cols(name, n):
    PCOLS[name] = (sum(k for _, k in PCOLS.values()), n)


_cols("c0", 8)
_cols("c1", 8)
for _l in range(4):
    _cols(f"ada_b{_l}", 48)
    _cols(f"mix_g{_l}", 8)
    _cols(f"ffn_g{_l}", 8)
for _l in range(2):
    _cols(f"mu{_l}", 15)
    for _n in ("w0", "a0", "k_k", "k_a", "r_k", "lnx_g", "lnx_b", "pool_scale"):
        _cols(f"{_n}{_l}", 4)
_cols("vres_v0", 4)
_cols("lnf_g", 8)
_cols("conv_w", 32)
for _n in ("conv_b", "ba", "bx", "lam", "kv_g", "final_g"):
    _cols(_n, 8)
_cols("kv_ada_b", 16)
_cols("ckv_g", 2)
_cols("cq_g", 3)
_cols("freq", 1)
_cols("sign", 1)
NPAR = sum(k for _, k in PCOLS.values())

SEGS = {}


def _plan():
    n = w = 0
    for l in range(4):
        mix = [[("in0", 18), ("out0", 8)], [("in1", 19), ("out1", 8)],
               [("lgate", 8), ("lrec", 8), ("lout", 8)],
               [("kvada", 16), ("dkv", 4), ("dq", 3), ("wo", 8)]][l]
        for name, count in [(f"ada{l}", 48), *mix, (f"q{l}", 16)]:
            SEGS[name] = (n, count, "w", w)
            n, w = n + count, w + count
        SEGS[f"u{l}"] = (n, KEYS, "u", l)
        n += KEYS
        SEGS[f"v{l}"] = (n, KEYS, "v", l)
        n += KEYS
    return w


NW = _plan()
TAKEN = {}
_e = 0
for _name in SEGS:
    TAKEN[_name] = _e
    if _name[0] not in "v" and not _name.startswith("ada") and _name != "kvada":
        _e += SEGS[_name][1]

SMALL = {"mix0": 48, "mix1": 96, "mix2": 112, "mix3": 192}
HSPLIT = {"ffn0": 3, "ffn1": 6, "ffn2": 9, "ffn3": 13}
CHUNK_STEPS = 31
CHUNK_OUTS = 32
MASKS = 10


def tiles_in_loops(eng, first, count, body):
    k = 0
    while k < count and first + k < RAW:
        body(first + k, first + k, k, None)
        k += 1
    turns = (count - k) // 4
    if turns >= 2:
        with eng.Fori(0, turns) as i:
            for j in range(4):
                body(first + k + j + i * 4, first + k + j, k + j + i * 4, i)
        k += 4 * turns
    while k < count:
        body(first + k, first + k, k, None)
        k += 1


class Seen:

    def __init__(self, eng, chain):
        self.eng, self.chain_sem, self.base, self.here = eng, chain, {}, None

    def __call__(self, sem, k=1):
        if self.here is None:
            self.base[sem.name] = self.base.get(sem.name, 0) + k
            self.eng.wait_ge(sem, self.base[sem.name])
        else:
            i, per, got = self.here
            got[sem.name] = got.get(sem.name, 0) + k
            at = self.base.get(sem.name, 0) + got[sem.name]
            self.eng.wait_ge(sem, at if i is None else i * per[sem.name] + at)

    def link(self, ins, sem=None):
        sem = sem or self.chain_sem
        ins.then_inc(sem, 1)
        self(sem)

    @contextmanager
    def loop(self, turns, per):
        per = {s.name: k for s, k in per.items()}
        with self.eng.Fori(0, turns) as i:
            self.here = (i, per, {})
            yield i
            got = self.here[2]
        assert got == per, (got, per)
        self.here = None
        for s, k in per.items():
            self.base[s] = self.base.get(s, 0) + turns * k


def build(nc, x_in_dram, w_tiles, u_tiles, v_tiles, params, consts, lora, lru_w, mla_w, mla_uv, keys_t, pool_inv,
          positions, out):
    with ExitStack() as ctx:
        def sb(name, shape, dt=F32):
            return ctx.enter_context(nc.sbuf_tensor(name, shape, dt))

        def sem(name):
            return ctx.enter_context(nc.semaphore(name))

        arena = sb("arena", [P, KEYS * T])
        raw = sb("raw", [P, RAW, D])
        t_hi = sb("t_hi", [P, SPL, D], F32R)
        t_lo = sb("t_lo", [P, SPL, D], F32R)
        x = sb("x", [P, DC, T])
        h_hi = sb("h_hi", [P, DC, T], F32R)
        h_lo = sb("h_lo", [P, DC, T], F32R)
        par = sb("par", [P, NPAR])
        cst = sb("cst", [P, 4, P])
        mod = sb("mod", [P, 48])
        mod_kv = sb("mod_kv", [P, 16])
        gain = sb("gain", [P, DC])
        c_act = sb("c_act", [P, 2, DC])
        c_spl = sb("c_spl", [P, 2, DC, 2], F32R)
        v_first = sb("v_first", [P, G4, T])
        sel = sb("sel", [P, 3, T])
        ps = ctx.enter_context(nc.psum_tensor("ps", [P, 8, 512], F32))

        ident, ones, head_ones, iota = (cst[:, k, :] for k in range(4))

        def pcol(name):
            a, n = PCOLS[name]
            return par[:, a:a + n]

        def carve(spec):
            at, got = 0, {}
            for name, shape in spec:
                size = int(np.prod(shape))
                v = arena[:, at:at + size]
                if len(shape) > 1:
                    names = " ".join(f"a{k}" for k in range(len(shape)))
                    v = v.rearrange(f"p ({names}) -> p {names}", **{f"a{k}": s for k, s in enumerate(shape)})
                got[name] = v
                at += size
            assert at <= KEYS * T, at
            return got

        act_all = arena[:, :].rearrange("p (e t) -> p e t", t=T)
        quad = (G4, T)
        rk = carve([("A", quad), ("B", quad), ("z", (19, T + 1)), ("rw", (15, T)), ("dec", quad), ("d1", quad),
                    ("Pinv", quad), ("Pprev", quad), ("kk", quad), ("kp", quad), ("tmp", quad), ("Pc", quad),
                    ("a", quad), ("gate", quad), ("K", quad), ("R", quad), ("bonus", quad), ("y", quad),
                    ("lora", (20, P)), ("masks", (MASKS, P)), ("pa", (4, T + 16)), ("pb", (4, T + 16)),
                    ("inv", quad)])
        wide = carve([("w", (DC, T))])["w"]
        chunk_at = {}
        at_rw = 2048 + 19 * (T + 1)
        free = [2048 + 512 * k for k in range(9)] + [at_rw + 512 * k for k in range(4)] \
            + [at_rw + 15 * T + 512 * k for k in range(14)]
        for name in ("Abd", "Bbd", "Kbd", "Rbd", "Vbd", "LT", "L2T", "T1T", "T2T", "At", "Bt", "Kt", "Vt", "Gm",
                     "X0", "X1", "XT0", "XT1", "Z", "U0", "XA", "RpT", "Q", "S0"):
            a = free.pop(0)
            chunk_at[name] = arena[:, a:a + 512].rearrange("p (g k) -> p g k", g=4)
        lr = carve([("w", (DC, T)), ("gate", (DC, T)), ("rp", (DC, T + 3)), ("xc", (DC, T)), ("rg", (DC, T)),
                    ("ig", (DC, T)), ("la", (DC, T)), ("a", (DC, T)), ("tau", (DC, T)), ("hs", (DC, T)),
                    ("wts", (32, P)), ("sp", (4, DC))])
        ml = carve([("w", (DC, T)), ("ck", (2, T)), ("krz", (2, T)), ("cq", (3, T)), ("uq", (48, P)),
                    ("uk", (16, P)), ("uv", (2, D)), ("kn", (DC, T)), ("kr", (T,)), ("qn", (DC, T)),
                    ("qr", (4, T)), ("qs", (4, T)), ("cos", (T,)), ("sin", (T,)), ("ang", (T,)), ("tmp", (4, T)),
                    ("vpad", (TT, AH, P)), ("mask", (TT, T)), ("mbias", (TT, T)), ("s", (TT, T)),
                    ("p", (TT, T)), ("pT", (TT, T)), ("posi", (T,)), ("posf", (T,)), ("posq", (TT,)),
                    ("posqi", (TT,)), ("st", (8,)), ("sq", (3, T)), ("rinv", (T,))])
        def ml_at(name):
            return {"uq": DC * T + 7 * T}[name]

        tk = carve([("w", (DC, T)), ("keys", (16, P)), ("q", (16, T)), ("sc", (TT, 16, P)), ("s2", (16, P)),
                    ("cand", (HEADS, 256)), ("c2", (HEADS, 256)), ("eq", (HEADS, TOPK, TOPK)),
                    ("val", (16, TOPK)), ("idx", (16, TOPK)), ("idf", (16, TOPK)), ("cs", (HEADS, TOPK)),
                    ("ci", (HEADS, TOPK)), ("hat", (2, HEADS, TOPK)), ("hatu", (2, HEADS, TOPK)),
                    ("e", (3, HEADS, TOPK)), ("den", (2, HEADS)),
                    ("rinv", (T,))])
        sum_sb = carve([("w", (DC, T)), ("keys", (16, P)), ("sum", (TT, D))])["sum"]
        oh1 = sb("oh1", [P, 2, 4, P])
        ms_all = oh1[:, 0, 0:2, :].rearrange("p a k -> p (a k)")
        rinv_all = oh1[:, 0, 2:4, :].rearrange("p a k -> p (a k)")
        oh2 = sb("oh2", [P, 2, 4, P])
        wa_hi = sb("wa_hi", [P, 2, T], F32R)
        wa_lo = sb("wa_lo", [P, 2, T], F32R)

        loaded = [sem(f"loaded{k}") for k in range(RAW)]
        hi_done = sem("hi_done")
        lo_done = sem("lo_done")
        tile_used = sem("tile_used")
        taken = sem("taken")
        par_in = sem("par_in")
        x_in = sem("x_in")
        small_in = sem("small_in")
        c_ready = sem("c_ready")
        csplit = sem("csplit")
        chains = {e: sem(f"chain_{e}") for e in ("act", "dve", "pool")}
        squares = sem("squares")
        sumsq = sem("sumsq")
        ms_ready = sem("ms_ready")
        root = sem("root")
        normed = sem("normed")
        h_full = sem("h_full")
        h_up = sem("h_up")
        h_split = sem("h_split")
        arena_free = sem("arena_free")
        shifted = sem("shifted")
        lora_in = sem("lora_in")
        lora_mm = sem("lora_mm")
        lora_out = sem("lora_out")
        hsum_in = sem("hsum_in")
        hsum = sem("hsum")
        hroot = sem("hroot")
        blocks_in = sem("blocks_in")
        pe_blk = sem("pe_blk")
        blk_out = sem("blk_out")
        pool_ready = sem("pool_ready")
        pool_mm = sem("pool_mm")
        z_free = sem("z_free")
        mix_ready = sem("mix_ready")
        xc_ready = sem("xc_ready")
        gates_mm = sem("gates_mm")
        gates_out = sem("gates_out")
        la_ready = sem("la_ready")
        ea_ready = sem("ea_ready")
        beta_in = sem("beta_in")
        beta = sem("beta")
        sp_a = sem("sp_a")
        sp_b = sem("sp_b")
        ang_ready = sem("ang_ready")
        trig = sem("trig")
        lat_in = sem("lat_in")
        kv_mm = sem("kv_mm")
        kv_out = sem("kv_out")
        sc_mm = sem("sc_mm")
        sc_ready = sem("sc_ready")
        exp_done = sem("exp_done")
        p_ready = sem("p_ready")
        pt_mm = sem("pt_mm")
        pt_out = sem("pt_out")
        av_mm = sem("av_mm")
        av_out = sem("av_out")
        keys_in = sem("keys_in")
        score_mm = sem("score_mm")
        score_out = sem("score_out")
        sm_in = sem("sm_in")
        sm_exp = sem("sm_exp")
        chosen = sem("chosen")
        chosen_t = sem("chosen_t")
        sel_ready = sem("sel_ready")
        hot = sem("hot")
        gates_t = sem("gates_t")
        gated = sem("gated")
        wah = sem("wah")
        wal = sem("wal")
        moe_out = sem("moe_out")
        moe_t = sem("moe_t")
        x_ready = sem("x_ready")
        fin = sem("fin")
        out_done = sem("out_done")

        block = ctx.enter_context(nc.Block())

        @block.sync
        def _(sp):
            sp.dma_start(par[:, :], params).then_inc(par_in, 16)
            sp.dma_start(cst[:, :, :], consts[:, 0:4, :]).then_inc(par_in, 16)
            sp.dma_start(x[:, :, :], x_in_dram).then_inc(x_in, 16)
            for name, (first, count, source, s0) in SEGS.items():
                def load(n, j, k, i, source=source, s0=s0):
                    if j >= RAW:
                        sp.wait_ge(lo_done, n - RAW + 1)
                    slot = j % RAW
                    if source == "w":
                        src = w_tiles[bass.ds(s0 + k, 1)].rearrange("a p n -> p (a n)")
                    elif source == "u":
                        src = u_tiles[bass.ds(s0 * KEYS + k, 1)].rearrange("a p n -> p (a n)")
                    else:
                        src = v_tiles[s0, :, bass.ds(k, 1), :].rearrange("p a n -> p (a n)")
                    sp.dma_start(raw[:, slot, :], src).then_inc(loaded[slot], 16)
                tiles_in_loops(sp, first, count, load)
            sp.wait_ge(fin, 1)
            sp.dma_start(out, wide).then_inc(out_done, 16)
            sp.wait_ge(out_done, 16)

        @block.gpsimd
        def _(pool):
            seen = Seen(pool, chains["pool"])

            def pooling(l):
                pool.wait_ge(small_in, SMALL[f"mix{l}"])
                seen(z_free)
                pa, pb, z = rk["pa"], rk["pb"], rk["z"]
                seen.link(pool.memset(pa[:, :, 0:16], 0.0))
                seen.link(pool.memset(pb[:, :, 0:16], 0.0))
                seen.link(pool.tensor_copy(pa[:, :, 16:], z[:, 14:18, 1:]))
                bufs = [pa, pb]
                for k, win in enumerate(WINDOWS):
                    src, dst, back = bufs[k % 2], bufs[(k + 1) % 2], win // 2
                    seen.link(pool.tensor_tensor(dst[:, k:, 16:], src[:, k:, 16:], src[:, k:, 16 - back:16 + T - back],
                                                 ALU.add))
                    seen.link(pool.tensor_tensor(dst[:, k, 16:], dst[:, k, 16:], rk["inv"][:, k, :], ALU.mult))
                    last = pool.tensor_tensor(dst[:, k, 16:], dst[:, k, 16:], z[:, 14 + k, 1:], ALU.subtract)
                    if k < len(WINDOWS) - 1:
                        seen.link(last)
                last.then_inc(pool_ready, 1)

            for l in range(4):
                if l:
                    seen(arena_free)
                if l < 2:
                    pool.dma_start(rk["lora"], lora[l]).then_inc(small_in, 16)
                    pool.dma_start(rk["masks"], consts[:, 4:4 + MASKS, :]).then_inc(small_in, 16)
                    pool.dma_start(rk["inv"], pool_inv).then_inc(small_in, 16)
                    pooling(l)
                elif l == 2:
                    pool.dma_start(lr["wts"], lru_w).then_inc(small_in, 16)
                else:
                    a = ml_at("uq")
                    pool.dma_start(arena[:, a:a + 64 * P].rearrange("p (m k) -> p m k", k=P), mla_w).then_inc(small_in, 16)
                    pool.dma_start(ml["uv"], mla_uv).then_inc(small_in, 16)
                    pool.dma_start(ml["posi"].bitcast(I32), positions[0:1, :].broadcast_to([P, T])).then_inc(small_in, 16)
                    for tt in range(TT):
                        pool.dma_start(ml["posqi"][:, tt:tt + 1].bitcast(I32),
                                       positions[0:1, tt * P:(tt + 1) * P].rearrange("a p -> p a")).then_inc(small_in, 16)
                pool.wait_ge(h_split, HSPLIT[f"ffn{l}"])
                pool.dma_start(tk["keys"], keys_t[l]).then_inc(keys_in, 16)

        @block.scalar
        def _(act):
            seen = Seen(act, chains["act"])

            def upper(n, j, i):
                turn = (j // RAW + 1) if i is None else i + (j // RAW + 1)
                act.wait_ge(loaded[j % RAW], turn * 16)
                if j >= SPL:
                    act.wait_ge(tile_used, n - SPL + 1)
                act.copy(t_hi[:, j % SPL, :], raw[:, j % RAW, :]).then_inc(hi_done, 1)

            def uppers(name):
                tiles_in_loops(act, *SEGS[name][:2], lambda n, j, k, i: upper(n, j, i))

            def project(name, take_out):
                first, count = SEGS[name][:2]
                upper(first, first, None)

                def step(n, j, k, i):
                    upper(n, j, i)
                    act.wait_ge(tile_used, n)
                    take_out(k, (j - 1) % 2).then_inc(taken, 1)
                tiles_in_loops(act, first + 1, count - 1, step)
                act.wait_ge(tile_used, first + count)
                take_out(count - 1, (first + count - 1) % 2).then_inc(taken, 1)

            def at(k):
                return bass.ds(k, 1) if not isinstance(k, int) else slice(k, k + 1)

            def norm():
                seen(ms_ready)
                act.activation(rinv_all, ms_all, ACT.Sqrt).then_inc(root, 1)

            def modulate(shift):
                seen(normed)
                for c in range(DC):
                    ins = act.activation(wide[:, c, :], wide[:, c, :], ACT.Identity, bias=shift[:, c:c + 1],
                                         scale=gain[:, c:c + 1])
                seen.link(ins)
                ins = act.copy(h_hi[:, :, :], wide)
                ins.then_inc(h_up, 1)

            def split_upper(ready, k=1):
                seen(ready, k)
                act.copy(h_hi[:, :, :], wide).then_inc(h_up, 1)

            def rwkv(l):
                rw = rk["rw"]
                project(f"in{l}", lambda k, b: act.copy(rk["z"][:, at(k), 1:], ps[:, b:b + 1, 0:T]))
                seen(shifted)
                act.activation(rw[0:64, 12, :], rw[0:64, 12, :], ACT.Tanh).then_inc(lora_in, 1)
                act.activation(rw[:, 13, :], rw[:, 13, :], ACT.Sigmoid).then_inc(lora_in, 1)
                seen(lora_mm)
                for g in range(G4):
                    lo, hi = ps[:, 2 + g // 2, (g % 2) * T:(g % 2 + 1) * T], ps[:, 4 + g // 2, (g % 2) * T:(g % 2 + 1) * T]
                    d = act.activation(rk["dec"][:, g, :], lo, ACT.Sigmoid, bias=pcol(f"w0{l}")[:, g:g + 1])
                    act.activation(rk["a"][:, g, :], hi, ACT.Sigmoid, bias=pcol(f"a0{l}")[:, g:g + 1])
                for g in range(G4):
                    ins = act.copy(rk["gate"][:, g, :], ps[:, 6 + g // 2, (g % 2) * T:(g % 2 + 1) * T])
                if l:
                    for g in range(G4):
                        ins = act.activation(rk["tmp"][:, g, :], ps[:, g // 2, (g % 2) * T:(g % 2 + 1) * T], ACT.Sigmoid,
                                             bias=pcol("vres_v0")[:, g:g + 1])
                seen.link(ins)
                act.activation(rk["dec"], rk["dec"], ACT.Exp, scale=-DECAY).then_inc(lora_out, 1)
                seen(hsum)
                act.activation(rk["tmp"].rearrange("p (b g) t -> p b (g t)", b=2), ps[:, 2:4, :], ACT.Sqrt)\
                    .then_inc(hroot, 1)
                seen(hsum_in, 4)
                act.activation(rk["tmp"], rk["tmp"], ACT.Sqrt).then_inc(hroot, 1)
                seen(hsum, 3)
                split_upper(mix_ready)

            def lru():
                project("lgate", lambda k, b: act.activation(lr["gate"][:, at(k), :], ps[:, b:b + 1, 0:T], ACT.Gelu))
                project("lrec", lambda k, b: act.copy(lr["rp"][:, at(k), 3:], ps[:, b:b + 1, 0:T]))
                seen(sp_a)
                seen.link(act.activation(lr["sp"][:, 1, :], lr["sp"][:, 0, :], ACT.Exp, scale=-1.0))
                act.activation(lr["sp"][:, 1, :], lr["sp"][:, 1, :], ACT.Ln, bias=ones[:, 0:1]).then_inc(sp_b, 1)
                seen(gates_mm)
                for c in range(DC):
                    bank, half = c // 2, slice((c % 2) * T, (c % 2 + 1) * T)
                    act.activation(lr["rg"][:, c, :], ps[:, bank, half], ACT.Sigmoid, bias=pcol("ba")[:, c:c + 1])
                    ins = act.activation(lr["ig"][:, c, :], ps[:, 4 + bank, half], ACT.Sigmoid,
                                         bias=pcol("bx")[:, c:c + 1])
                ins.then_inc(gates_out, 1)
                seen(la_ready)
                act.activation(lr["tau"], lr["la"], ACT.Tanh, scale=-1.0).then_inc(ea_ready, 1)
                act.activation(lr["a"], lr["la"], ACT.Exp).then_inc(ea_ready, 1)
                seen(beta_in)
                act.activation(lr["tau"], lr["tau"], ACT.Sqrt, scale=2.0).then_inc(beta, 1)
                split_upper(mix_ready)

            def attention():
                project("dkv", lambda k, b: act.copy(
                    ml["ck"][:, k, :] if k < 2 else ml["krz"][:, k - 2, :], ps[:, b, 0:T]))
                modulate_for("mix3")
                project("dq", lambda k, b: act.copy(ml["cq"][:, k, :], ps[:, b, 0:T]))
                seen(ang_ready, 2)
                act.activation(ml["cos"], ml["cos"], ACT.Sin)
                act.activation(ml["sin"], ml["sin"], ACT.Sin).then_inc(trig, 1)
                for _ in range(2):
                    seen(ms_ready)
                    act.activation(ml["rinv"], ml["rinv"], ACT.Sqrt).then_inc(root, 1)
                for h in range(AH):
                    seen(sc_ready)
                    for q in range(TT):
                        ins = act.activation(ml["p"][:, q, :], ml["s"][:, q, :], ACT.Exp, bias=ml["st"][:, q:q + 1],
                                             accum_out=ml["st"][:, 2 + q:3 + q])
                    ins.then_inc(exp_done, 1)
                split_upper(av_out, AH // 2)

            def modulate_for(which):
                norm()
                if which == "kv":
                    modulate(mod_kv[:, 0:8])
                elif which.startswith("mix"):
                    modulate(mod[:, 0:8])
                else:
                    modulate(mod[:, 24:32])

            def peer(l):
                project(f"q{l}", lambda k, b: act.copy(tk["q"][:, at(k), :], ps[:, b:b + 1, 0:T]))
                for tt in range(TT):
                    for b in range(4):
                        seen(score_mm)
                        act.copy(tk["sc"][:, tt, 4 * b:4 * b + 4, :].rearrange("p a k -> p (a k)"),
                                 ps[:, 2 + b, :]).then_inc(score_out, 1)
                for tt in range(TT):
                    seen(sm_in)
                    act.activation(tk["e"][:, 2], tk["e"][:, 2], ACT.Exp).then_inc(sm_exp, 1)
                act.wait_ge(sel_ready, TT * (l + 1))
                project(f"u{l}", lambda k, b: act.activation(act_all[:, at(k), :], ps[:, b:b + 1, 0:T], ACT.Gelu))
                first = SEGS[f"v{l}"][0]
                act.wait_ge(gated, (T // 4) * (l + 1))

                def step(n, j, k, i):
                    upper(n, j, i)
                    act.copy(wa_hi[:, j % 2:j % 2 + 1, :], act_all[:, at(k), :]).then_inc(wah, 1)
                tiles_in_loops(act, first, KEYS, step)

            act.wait_ge(par_in, 32)
            act.activation(c_act[:, 0, :], pcol("c0"), ACT.Silu).then_inc(c_ready, 1)
            act.activation(c_act[:, 1, :], pcol("c1"), ACT.Silu).then_inc(c_ready, 1)
            for l in range(4):
                uppers(f"ada{l}")
                if l == 3:
                    uppers("kvada")
                    modulate_for("kv")
                    attention()
                else:
                    modulate_for(f"mix{l}")
                    if l < 2:
                        rwkv(l)
                    else:
                        lru()
                uppers(("out0", "out1", "lout", "wo")[l])
                modulate_for(f"ffn{l}")
                peer(l)
                if l % 2:
                    norm()

        @block.vector
        def _(dve):
            seen = Seen(dve, chains["dve"])
            link = seen.link
            tts, ts, stt, cp = dve.tensor_tensor, dve.tensor_scalar, dve.scalar_tensor_tensor, dve.tensor_copy

            def lower(n, j, k=None, i=None):
                dve.wait_ge(hi_done, n + 1)
                tts(t_lo[:, j % SPL, :], raw[:, j % RAW, :], t_hi[:, j % SPL, :].bitcast(F32),
                    ALU.subtract).then_inc(lo_done, 1)

            def lowers(name):
                tiles_in_loops(dve, *SEGS[name][:2], lower)

            def at(k):
                return bass.ds(k, 1) if not isinstance(k, int) else slice(k, k + 1)

            def add_products(name, gate):
                first, count = SEGS[name][:2]
                lower(first, first)

                def take_out(k, b):
                    return stt(x[:, k, :], ps[:, b, 0:T], gate[:, k:k + 1], x[:, k, :], ALU.mult, ALU.add)

                for k in range(1, count):
                    lower(first + k, first + k)
                    dve.wait_ge(tile_used, first + k)
                    take_out(k - 1, (first + k - 1) % 2).then_inc(taken, 1)
                dve.wait_ge(tile_used, first + count)
                take_out(count - 1, (first + count - 1) % 2).then_inc(taken, 1)
                dve.wait_ge(taken, TAKEN[name] + count)

            def modulation(l):
                lowers(f"ada{l}")
                dve.wait_ge(tile_used, SEGS[f"ada{l}"][0] + 48)
                link(dve.tensor_reduce(mod[:, :], ps[:, 2, 0:96].rearrange("p (m two) -> p m two", two=2), AX.X, ALU.add))
                link(tts(mod[:, :], mod[:, :], pcol(f"ada_b{l}"), ALU.add))
                if l == 3:
                    lowers("kvada")
                    dve.wait_ge(tile_used, SEGS["kvada"][0] + 16)
                    link(dve.tensor_reduce(mod_kv[:, :], ps[:, 3, 0:32].rearrange("p (m two) -> p m two", two=2),
                                           AX.X, ALU.add))
                    link(tts(mod_kv[:, :], mod_kv[:, :], pcol("kv_ada_b"), ALU.add))

            def norm_x():
                tts(wide, x[:, :, :], x[:, :, :], ALU.mult).then_inc(squares, 1)
                seen(sumsq)
                ts(ms_all, ps[:, 2, 0:T], 1.0 / D, EPS, ALU.mult, ALU.add).then_inc(ms_ready, 1)
                seen(root)
                link(dve.reciprocal(rinv_all, rinv_all))
                return tts(wide, x[:, :, :], rinv_all.unsqueeze(1).broadcast_to([P, DC, T]), ALU.mult)

            def norm(g, scale):
                link(stt(gain[:, :], scale, 1.0, g, ALU.add, ALU.mult))
                norm_x().then_inc(normed, 1)
                split_lower()

            def split_lower():
                seen(h_up)
                tts(h_lo[:, :, :], wide, h_hi[:, :, :].bitcast(F32), ALU.subtract).then_inc(h_split, 1)

            def rwkv(l):
                z, rw, kk, kp, a, v = rk["z"], rk["rw"], rk["kk"], rk["kp"], rk["a"], rk["rw"][:, 8:12, :]
                r, k, tmp, tmp2 = rw[:, 0:4, :], rw[:, 4:8, :], rk["tmp"], rk["d1"]
                name = f"in{l}"
                first, count = SEGS[name][:2]
                link(dve.memset(z[:, :, 0:1], 0.0))
                lowers(name)
                dve.wait_ge(taken, TAKEN[name] + count)
                link(tts(rw[:, 0:14, :], z[:, 0:14, 0:T], z[:, 0:14, 1:T + 1], ALU.subtract), z_free)
                if l:
                    link(tts(rw[:, 14, :], z[:, 18, 0:T], z[:, 18, 1:T + 1], ALU.subtract))
                for m in range(14 + l):
                    ins = stt(rw[:, m, :], rw[:, m, :], pcol(f"mu{l}")[:, m:m + 1], z[:, m + 4 * (m == 14), 1:],
                              ALU.mult, ALU.add)
                link(ins, shifted)
                if not l:
                    cp(v_first[:, :, :], v)
                for g in range(G4):
                    ins = ts(kk[:, g, :], k[:, g, :], pcol(f"k_k{l}")[:, g:g + 1], None, ALU.mult)
                link(ins)
                seen(lora_out)
                if l:
                    link(tts(v_first[:, :, :], v_first[:, :, :], v, ALU.subtract))
                    link(tts(v_first[:, :, :], v_first[:, :, :], tmp, ALU.mult))
                    link(tts(v, v, v_first[:, :, :], ALU.add))
                tts(tmp2, kk, kk, ALU.mult).then_inc(hsum_in, 1)
                link(ts(gain[:, 0:4], pcol(f"k_a{l}"), -1.0, 1.0, ALU.mult, ALU.add))
                for g in range(G4):
                    ins = ts(kp[:, g, :], a[:, g, :], pcol(f"k_a{l}")[:, g:g + 1], gain[:, g:g + 1], ALU.mult, ALU.add)
                link(ins)
                link(tts(kp, kp, k, ALU.mult))
                dec, Pc, Pinv, Pprev = rk["dec"], rk["Pc"], rk["Pinv"], rk["Pprev"]
                starts = lambda b: b.rearrange("p g (c t) -> p (g c) t", t=CH)
                seen(hsum)
                link(dve.memset(tmp2, 0.0))
                link(cp(starts(tmp2)[:, :, 0:1], starts(dec)[:, :, 0:1]))
                link(dve.memset(starts(dec)[:, :, 0:1], 0.0))
                flat = lambda b: b.rearrange("p g t -> p (g t)")
                link(dve.tensor_tensor_scan(flat(Pc), flat(dec), flat(tmp2), 0.0, ALU.mult, ALU.add))
                link(dve.reciprocal(Pinv, Pc))
                dve.memset(starts(Pprev)[:, :, 0:1], 1.0)
                link(cp(starts(Pprev)[:, :, 1:], starts(Pc)[:, :, 0:CH - 1]))
                seen(hroot)
                link(ts(tmp, tmp, 1e-12, None, ALU.max))
                link(dve.reciprocal(tmp, tmp))
                link(tts(kk, kk, tmp, ALU.mult))
                link(tts(rk["R"], r, kp, ALU.mult))
                for g in range(G4):
                    ins = ts(tmp[:, g, :], rk["R"][:, g, :], pcol(f"r_k{l}")[:, g:g + 1], None, ALU.mult)
                ins.then_inc(hsum_in, 1)
                link(stt(rk["A"], kk, -1.0, Pprev, ALU.mult, ALU.mult))
                link(tts(rk["B"], kk, a, ALU.mult))
                link(tts(rk["B"], rk["B"], Pinv, ALU.mult))
                link(tts(rk["K"], kp, Pinv, ALU.mult))
                link(tts(rk["R"], r, Pc, ALU.mult))
                seen(hsum)
                link(tts(rk["bonus"].rearrange("p (b g) t -> p b (g t)", b=2), ps[:, 4:6, :],
                         v.rearrange("p (b g) t -> p b (g t)", b=2), ALU.mult))
                dve.wait_ge(pool_ready, l + 1)
                c_ = chunk_at
                for n in ("Abd", "Bbd", "Kbd", "Rbd", "Vbd", "S0"):
                    ins = dve.memset(c_[n], 0.0)
                link(ins)
                masks = rk["masks"]
                SU, SL, IU, M1T, M1 = (masks[:, k, :] for k in range(5))
                bc = lambda m: m.unsqueeze(1).broadcast_to([P, G4, P])
                out4 = lambda b: ps[:, b, :].rearrange("p (g k) -> p g k", g=4)
                with seen.loop(NCH, {chains["dve"]: 2, pe_blk: CHUNK_STEPS, blocks_in: 1, blk_out: CHUNK_OUTS}) as c:
                    tok = bass.ds(c * CH, CH)
                    pairs = (("Abd", rk["A"]), ("Bbd", rk["B"]), ("Kbd", rk["K"]), ("Rbd", rk["R"]), ("Vbd", v))
                    for n, src in pairs:
                        cp(c_[n][0:64, :, 0:64], src[0:64, :, tok])
                        ins = cp(c_[n][64:128, :, 64:128], src[64:128, :, tok])
                    link(ins, blocks_in)

                    def out_of(bank, dst, mask=None, plus=None):
                        seen(pe_blk)
                        if mask is not None:
                            return tts(dst, out4(bank), bc(mask), ALU.mult)
                        if plus is not None:
                            return tts(dst, out4(bank), plus, ALU.add)
                        return cp(dst, out4(bank))

                    def done(ins):
                        link(ins, blk_out)

                    done(out_of(2, c_["LT"], SU))
                    done(out_of(3, c_["X0"], M1))
                    done(out_of(4, c_["L2T"], SU))
                    done(out_of(5, c_["T1T"], IU))
                    done(out_of(6, c_["T2T"], IU))
                    done(out_of(7, c_["At"]))
                    done(out_of(2, c_["Bt"]))
                    done(out_of(3, c_["Kt"]))
                    done(out_of(4, c_["Vt"]))
                    link(tts(c_["XT0"], c_["LT"], bc(M1T), ALU.mult))
                    link(tts(c_["X0"], c_["X0"], bc(ident), ALU.add))
                    done(tts(c_["XT0"], c_["XT0"], bc(ident), ALU.add))
                    for lev in range(5):
                        cur, nxt = lev % 2, (lev + 1) % 2
                        done(out_of(5, c_["Z"], masks[:, 5 + lev, :]))
                        done(out_of(6, c_[f"X{nxt}"], plus=c_[f"X{cur}"]))
                        done(out_of(7, c_[f"XT{nxt}"], plus=c_[f"XT{cur}"]))
                    done(out_of(2, c_["Gm"]))
                    done(out_of(3, c_["XA"]))
                    done(out_of(4, c_["U0"]))
                    done(out_of(5, c_["RpT"], plus=c_["Rbd"]))
                    done(out_of(6, c_["Q"]))
                    seen(pe_blk)
                    cp(rk["y"][0:64, :, tok], out4(7)[0:64, :, 0:64])
                    done(cp(rk["y"][64:128, :, tok], out4(7)[64:128, :, 64:128]))
                    seen(pe_blk)
                    end = rk["Pc"].rearrange("p g (c t) -> p g c t", t=CH)[:, :, bass.ds(c, 1), CH - 1]
                    done(tts(c_["S0"], out4(2), end.broadcast_to([P, G4, P]), ALU.mult))
                y = rk["y"]
                seen(hsum)
                halves = lambda b: b.rearrange("p (b g) t -> p b (g t)", b=2)
                link(stt(halves(y), ps[:, 2:4, :], -1.0 / 64, halves(y), ALU.mult, ALU.add))
                tts(tmp, y, y, ALU.mult).then_inc(hsum_in, 1)
                seen(hsum)
                ts(halves(tmp), ps[:, 4:6, :], 1.0 / 64, GN_EPS, ALU.mult, ALU.add).then_inc(hsum_in, 1)
                seen(hroot)
                link(dve.reciprocal(tmp, tmp))
                link(tts(y, y, tmp, ALU.mult))
                for g in range(G4):
                    ins = ts(y[:, g, :], y[:, g, :], pcol(f"lnx_g{l}")[:, g:g + 1], pcol(f"lnx_b{l}")[:, g:g + 1],
                             ALU.mult, ALU.add)
                link(ins)
                link(tts(y, y, rk["bonus"], ALU.add))
                tts(wide[:, 0:4, :], y, rk["gate"], ALU.mult)
                seen(pool_mm)
                for g in range(G4):
                    ins = ts(wide[:, 4 + g, :], ps[:, 6 + g // 2, (g % 2) * T:(g % 2 + 1) * T],
                             pcol(f"pool_scale{l}")[:, g:g + 1], None, ALU.mult)
                ins.then_inc(mix_ready, 1)
                split_lower()

            def lru():
                rp, xc = lr["rp"], lr["xc"]
                lowers("lgate")
                link(dve.memset(rp[:, :, 0:3], 0.0))
                lowers("lrec")
                link(ts(lr["sp"][:, 0, :], pcol("lam"), -1.0, None, ALU.mult))
                tts(lr["sp"][:, 0, :], lr["sp"][:, 0, :], pcol("lam"), ALU.max).then_inc(sp_a, 1)
                dve.wait_ge(taken, TAKEN["lrec"] + 8)
                w = lambda k, c: pcol("conv_w")[:, 8 * k + c:8 * k + c + 1]
                for c in range(DC):
                    ins = ts(xc[:, c, :], rp[:, c, 0:T], w(0, c), pcol("conv_b")[:, c:c + 1], ALU.mult, ALU.add)
                link(ins)
                for k in range(1, 4):
                    for c in range(DC):
                        ins = stt(xc[:, c, :], rp[:, c, k:k + T], w(k, c), xc[:, c, :], ALU.mult, ALU.add)
                    if k < 3:
                        link(ins)
                ins.then_inc(xc_ready, 1)
                link(ts(lr["sp"][:, 2, :], pcol("lam"), -1.0, 0.0, ALU.mult, ALU.max))
                seen(sp_b)
                link(tts(lr["sp"][:, 2, :], lr["sp"][:, 2, :], lr["sp"][:, 1, :], ALU.add))
                link(ts(lr["sp"][:, 3, :], lr["sp"][:, 2, :], -8.0, None, ALU.mult))
                seen(gates_out)
                for c in range(DC):
                    ins = ts(lr["la"][:, c, :], lr["rg"][:, c, :], lr["sp"][:, 3, c:c + 1], None, ALU.mult)
                ins.then_inc(la_ready, 1)
                link(tts(lr["ig"], lr["ig"], xc, ALU.mult))
                seen(ea_ready)
                link(ts(lr["rg"], lr["tau"], 1.0, None, ALU.add))
                link(dve.reciprocal(lr["rg"], lr["rg"]))
                tts(lr["tau"], lr["tau"], lr["rg"], ALU.mult).then_inc(beta_in, 1)
                seen(beta)
                link(tts(lr["ig"], lr["ig"], lr["tau"], ALU.mult))
                seen(ea_ready)
                for c in range(DC):
                    ins = dve.tensor_tensor_scan(lr["hs"][:, c, :], lr["a"][:, c, :], lr["ig"][:, c, :], 0.0,
                                                 ALU.mult, ALU.add)
                link(ins)
                tts(wide, lr["gate"], lr["hs"], ALU.mult).then_inc(mix_ready, 1)
                split_lower()

            def attention():
                lowers("dkv")
                norm(pcol("mix_g3"), mod[:, 8:16])
                lowers("dq")
                dve.wait_ge(taken, TAKEN["dq"] + 3)
                dve.wait_ge(small_in, SMALL["mix3"])
                posf, ang, cos, sin, tmp = ml["posf"], ml["ang"], ml["cos"], ml["sin"], ml["tmp"]
                cp(ml["posq"], ml["posqi"].bitcast(I32))
                link(cp(posf, ml["posi"].bitcast(I32)))
                for tt in range(TT):
                    ins = ts(ml["mask"][:, tt, :], posf, ml["posq"][:, tt:tt + 1], None, ALU.is_le)
                link(ins)
                link(ts(ml["mbias"], ml["mask"], -1.0, -NEG, ALU.add, ALU.mult))
                link(ts(ang, posf, pcol("freq"), None, ALU.mult))
                MAGIC = 12582912.0
                C1, C2 = 6.28125, 0.0019350051879882812
                C3 = 2.0 * np.pi - C1 - C2
                for dst, quarter, add in ((sin, 0.0, 0.0), (cos, 0.25, float(np.pi / 2))):
                    link(ts(tmp[:, 0, :], ang, float(1 / (2 * np.pi)), quarter, ALU.mult, ALU.add))
                    link(ts(tmp[:, 1, :], tmp[:, 0, :], MAGIC, None, ALU.add))
                    link(ts(tmp[:, 1, :], tmp[:, 1, :], MAGIC, None, ALU.subtract))
                    link(stt(dst, tmp[:, 1, :], -C1, ang, ALU.mult, ALU.add))
                    link(stt(dst, tmp[:, 1, :], -C2, dst, ALU.mult, ALU.add))
                    link(stt(dst, tmp[:, 1, :], -float(C3), dst, ALU.mult, ALU.add))
                    if add:
                        link(ts(dst, dst, add, None, ALU.add))
                    link(ts(dst, dst, 3.1415925, -3.1415925, ALU.min, ALU.max), ang_ready)
                seen(trig)
                link(ts(sin, sin, pcol("sign"), None, ALU.mult))
                for lat, n, g in (("ck", 2, "ckv_g"), ("cq", 3, "cq_g")):
                    tts(ml["sq"][:, 0:n, :], ml[lat], ml[lat], ALU.mult).then_inc(squares, 1)
                    seen(sumsq)
                    ts(ml["rinv"], ps[:, 2, 0:T], 1.0 / (n * P), EPS, ALU.mult, ALU.add).then_inc(ms_ready, 1)
                    seen(root)
                    link(dve.reciprocal(ml["rinv"], ml["rinv"]))
                    for c in range(n):
                        ins = stt(ml[lat][:, c, :], ml[lat][:, c, :], pcol(g)[:, c:c + 1], ml["rinv"], ALU.mult, ALU.mult)
                    link(ins)
                link(tts(ml["kr"], ml["krz"][:, 0, :], cos, ALU.mult))
                link(tts(tmp[:, 0, :], ml["krz"][:, 1, :], sin, ALU.mult))
                link(tts(ml["kr"], ml["kr"], tmp[:, 0, :], ALU.add))
                link(dve.memset(ml["vpad"], 0.0), lat_in)
                pair = lambda v, a: v[:, a:a + 2, :].rearrange("p a t -> p (a t)")
                dsts = [pair(ml["kn"], a) for a in (0, 2, 4, 6)] + [pair(ml["qn"], a) for a in (0, 2, 4, 6)] \
                    + [pair(ml["qr"], a) for a in (0, 2)] + [pair(ml["qs"], a) for a in (0, 2)]
                for n, dst in enumerate(dsts):
                    seen(kv_mm)
                    link(cp(dst, ps[:, n % 8, :]), kv_out)
                for kt in range(TT):
                    for half in range(2):
                        seen(kv_mm)
                        src = ps[:, 4 + 2 * kt + half, :].rearrange("p (h two k) -> p h two k", two=2, k=64)
                        dst = ml["vpad"][:, kt, 8 * half:8 * half + 8, :].rearrange("p (h two) k -> p h two k", two=2)
                        cp(dst[:, :, 0, 0:64], src[:, :, 0, :])
                        link(cp(dst[:, :, 1, 64:128], src[:, :, 1, :]), kv_out)
                bc4 = lambda v: v.unsqueeze(1).broadcast_to([P, 4, T])
                link(tts(ml["qr"], ml["qr"], bc4(cos), ALU.mult))
                link(tts(ml["qs"], ml["qs"], bc4(sin), ALU.mult))
                link(tts(ml["qr"], ml["qr"], ml["qs"], ALU.add), lat_in)
                s, p, st = ml["s"], ml["p"], ml["st"]
                for h in range(AH):
                    seen(sc_mm)
                    link(stt(s, ps[:, 2 + h % 2, :].rearrange("p (q k) -> p q k", q=2), ATT_SCALE, ml["mask"],
                             ALU.mult, ALU.mult))
                    link(tts(s, s, ml["mbias"], ALU.add))
                    link(dve.tensor_reduce(st[:, 4:6], s, AX.X, ALU.max))
                    ts(st[:, 0:2], st[:, 4:6], -1.0, None, ALU.mult).then_inc(sc_ready, 1)
                    seen(exp_done)
                    link(dve.reciprocal(st[:, 6:8], st[:, 2:4]))
                    for q in range(TT):
                        ins = ts(p[:, q, :], p[:, q, :], st[:, 6 + q:7 + q], None, ALU.mult)
                    ins.then_inc(p_ready, 1)
                    seen(pt_mm)
                    cp(ml["pT"].rearrange("p a t -> p (a t)"), ps[:, 4 + h % 2, :]).then_inc(pt_out, 1)
                    if h % 2:
                        seen(av_mm)
                        cp(wide[:, h // 2, :], ps[:, 6, 0:T]).then_inc(av_out, 1)
                split_lower()

            def top16(src, other, val, idx, width):
                link(dve.max(val[:, 0:8], src))
                dve.max_index(idx[:, 0:8], val[:, 0:8], src)
                link(dve.match_replace(other, val[:, 0:8], src, LOWEST))
                link(dve.max(val[:, 8:16], other))
                return dve.max_index(idx[:, 8:16], val[:, 8:16], other)

            def choose(l):
                lowers(f"q{l}")
                val, idx, idf, cs, ci = tk["val"], tk["idx"].bitcast(U32), tk["idf"], tk["cs"], tk["ci"].bitcast(U32)
                hat, hatu, e, eq = tk["hat"], tk["hatu"].bitcast(U32), tk["e"], tk["eq"]
                for tt in range(TT):
                    for hp in range(16):
                        if hp % 4 == 0:
                            seen(score_out)
                        ins = top16(tk["sc"][:, tt, hp, :], tk["s2"][:, hp, :], val[:, hp, :], idx[:, hp, :], KEYS)
                    link(ins)
                    link(cp(idf, idx))
                    two = lambda v, w: v.rearrange("p (h two) k -> p two h k", two=2)[:, w]
                    full = [P, HEADS, TOPK, TOPK]
                    link(tts(tk["cand"].rearrange("p h (i j) -> p h i j", i=TOPK),
                             two(val, 0).unsqueeze(3).broadcast_to(full),
                             two(val, 1).unsqueeze(2).broadcast_to(full), ALU.add))
                    for h in range(HEADS):
                        ins = top16(tk["cand"][:, h, :], tk["c2"][:, h, :], cs[:, h, :], ci[:, h, :], 256)
                    link(ins)
                    tts(e[:, 2], cs, cs[:, :, 0:1].broadcast_to([P, HEADS, TOPK]), ALU.subtract).then_inc(sm_in, 1)
                    ts(hatu[:, 0], ci, 4, None, ALU.logical_shift_right)
                    link(ts(hatu[:, 1], ci, TOPK - 1, None, ALU.bitwise_and))
                    link(cp(hat, hatu))
                    for w in range(2):
                        link(tts(eq, hat[:, w].unsqueeze(3).broadcast_to(full),
                                 iota[:, 0:TOPK].unsqueeze(1).unsqueeze(1).broadcast_to(full), ALU.is_equal))
                        link(tts(eq, eq, two(idf, w).unsqueeze(2).broadcast_to(full), ALU.mult))
                        link(dve.tensor_reduce(e[:, w], eq, AX.X, ALU.add))
                    seen(sm_exp)
                    link(dve.tensor_reduce(tk["den"][:, 0, :], e[:, 2], AX.X, ALU.add))
                    link(dve.reciprocal(tk["den"][:, 1, :], tk["den"][:, 0, :]))
                    tts(e[:, 2], e[:, 2], tk["den"][:, 1, :].unsqueeze(2).broadcast_to([P, HEADS, TOPK]),
                        ALU.mult).then_inc(chosen, 1)
                    seen(chosen_t)
                    cp(sel[:, :, tt * P:(tt + 1) * P], ps[:, 6 + tt, 0:3 * P].rearrange("p (w t) -> p w t", w=3))\
                        .then_inc(sel_ready, 1)

            def gates(l):
                def hots(g, b):
                    for q in range(4):
                        col = lambda w: sel[:, w, bass.ds(g * 4 + q, 1)] if not isinstance(g, int) \
                            else sel[:, w, 4 * g + q:4 * g + q + 1]
                        ts(oh1[:, b, q, :], iota, col(0), None, ALU.is_equal)
                        ins = ts(oh2[:, b, q, :], iota, col(1), col(2), ALU.is_equal, ALU.mult)
                    ins.then_inc(hot, 1)

                def gate(g, b):
                    view = act_all[:, :, bass.ds(g * 4, 4)] if not isinstance(g, int) else act_all[:, :, 4 * g:4 * g + 4]
                    view = view.rearrange("p e t -> p t e")
                    return tts(view, ps[:, b, :].rearrange("p (t e) -> p t e", t=4), view, ALU.mult).then_inc(gated, 1)

                dve.wait_ge(sel_ready, TT * (l + 1))
                dve.wait_ge(taken, TAKEN[f"u{l}"] + KEYS)
                n = T // 4
                hots(0, 0)
                with seen.loop(n // 2 - 1, {gates_t: 2}) as i:
                    hots(i * 2 + 1, 1)
                    seen(gates_t)
                    gate(i * 2, 0)
                    hots(i * 2 + 2, 0)
                    seen(gates_t)
                    gate(i * 2 + 1, 1)
                hots(n - 1, 1)
                seen(gates_t)
                gate(n - 2, 0)
                seen(gates_t)
                gate(n - 1, 1)

            def experts_out(l):
                first = SEGS[f"v{l}"][0]
                g2 = mod[:, 40:48]

                def step(n, j, k, i):
                    lower(n, j)
                    dve.wait_ge(wah, (k if i is None else k) + (1 + KEYS * l))
                    tts(wa_lo[:, j % 2:j % 2 + 1, :], act_all[:, at(k), :], wa_hi[:, j % 2:j % 2 + 1, :].bitcast(F32),
                        ALU.subtract).then_inc(wal, 1)
                tiles_in_loops(dve, first, KEYS, step)
                dve.wait_ge(tile_used, first + KEYS)
                for tt in range(TT):
                    for half in range(2):
                        ins = cp(sum_sb[:, tt, half * 512:(half + 1) * 512], ps[:, 2 + 2 * tt + half, :])
                ins.then_inc(moe_out, 1)
                for m in range(4):
                    seen(moe_t)
                    for c in range(2):
                        ins = stt(x[:, 2 * m + c, :], ps[:, [6, 7, 0, 1][m], c * T:(c + 1) * T], g2[:, 2 * m + c:2 * m + c + 1],
                                  x[:, 2 * m + c, :], ALU.mult, ALU.add)
                if l in (1, 3):
                    link(ins)
                return ins

            dve.wait_ge(par_in, 32)
            seen(c_ready, 2)
            link(cp(c_spl[:, :, :, 0], c_act[:, :, :]))
            tts(c_spl[:, :, :, 1], c_act[:, :, :], c_spl[:, :, :, 0].bitcast(F32), ALU.subtract).then_inc(csplit, 1)
            for l in range(4):
                modulation(l)
                if l == 0:
                    dve.wait_ge(x_in, 16)
                if l == 3:
                    norm(pcol("kv_g"), mod_kv[:, 8:16])
                    attention()
                else:
                    norm(pcol(f"mix_g{l}"), mod[:, 8:16])
                    if l < 2:
                        rwkv(l)
                    else:
                        lru()
                add_products(("out0", "out1", "lout", "wo")[l], mod[:, 16:24])
                norm(pcol(f"ffn_g{l}"), mod[:, 32:40])
                choose(l)
                lowers(f"u{l}")
                gates(l)
                ins = experts_out(l)
                if l == 1 or l == 3:
                    link(norm_x())
                    g = pcol("lnf_g" if l == 1 else "final_g")
                    for c in range(DC):
                        dst = x if l == 1 else wide
                        ins = ts(dst[:, c, :], wide[:, c, :], g[:, c:c + 1], None, ALU.mult)
                link(ins, arena_free if l < 3 else fin)

        @block.tensor
        def _(pe):
            seen = Seen(pe, None)
            mm = pe.matmul

            def products(name):
                first, count = SEGS[name][:2]

                def step(n, j, k, i):
                    pe.wait_ge(lo_done, n + 1)
                    if not (TAKEN[name] == 0 and i is None and k < 2):
                        pe.wait_ge(taken, k + (TAKEN[name] - 1))
                    o = ps[:, j % 2, 0:T]
                    hi = t_hi[:, j % SPL, :].rearrange("p (c m) -> p c m", c=DC)
                    lo = t_lo[:, j % SPL, :].rearrange("p (c m) -> p c m", c=DC)
                    for c in range(DC):
                        mm(o, hi[:, c, :], h_hi[:, c, :], start=(c == 0), stop=False)
                        mm(o, hi[:, c, :], h_lo[:, c, :], start=False, stop=False)
                        ins = mm(o, lo[:, c, :], h_hi[:, c, :], start=False, stop=(c == DC - 1))
                    ins.then_inc(tile_used, 1)
                if TAKEN[name] == 0:
                    for k in range(2):
                        step(first + k, first + k, k, None)

                    tiles_in_loops(pe, first + 2, count - 2, lambda n, j, k, i: step(n, j, k + 2, i))
                else:
                    tiles_in_loops(pe, first, count, step)

            def modulation(name, who, bank):
                def step(n, j, k, i):
                    pe.wait_ge(lo_done, n + 1)
                    o = ps[:, bank, bass.ds(k * 2, 2)] if i is not None else ps[:, bank, 2 * k:2 * k + 2]
                    for part in (t_hi, t_lo):
                        w = part[:, j % SPL, :].rearrange("p (c m) -> p c m", c=DC)
                        for c in range(DC):
                            ins = mm(o, w[:, c, :], c_spl[:, who, c, :], start=(part is t_hi and c == 0),
                                     stop=(part is t_lo and c == DC - 1))
                    ins.then_inc(tile_used, 1)
                tiles_in_loops(pe, *SEGS[name][:2], step)

            def sum_squares(src, n):
                seen(squares)
                for c in range(n):
                    ins = mm(ps[:, 2, 0:T], ones, src[:, c, :], start=(c == 0), stop=(c == n - 1))
                ins.then_inc(sumsq, 1)

            def head_sum(src, bank, wait=True):
                if wait:
                    seen(hsum_in)
                for b in range(2):
                    ins = mm(ps[:, bank + b, :], head_ones, src[:, 2 * b:2 * b + 2, :].rearrange("p g t -> p (g t)"),
                             start=True, stop=True)
                ins.then_inc(hsum, 1)

            def rwkv(l):
                rw, lw = rk["rw"], rk["lora"]
                products(f"in{l}")
                pe.wait_ge(small_in, SMALL[f"mix{l}"])
                seen(lora_in, 2)
                for m in range(8):
                    mm(ps[:, 2 + m // 2, (m % 2) * T:(m % 2 + 1) * T], lw[:, m, :], rw[:, 12, :], start=True, stop=True)
                for m in range(4):
                    ins = mm(ps[:, 6 + m // 2, (m % 2) * T:(m % 2 + 1) * T], lw[:, 8 + m, :], rw[:, 13, :],
                             start=True, stop=True)
                if l:
                    pe.wait_ge(taken, TAKEN["in1"] + 19)
                    for m in range(4):
                        ins = mm(ps[:, m // 2, (m % 2) * T:(m % 2 + 1) * T], lw[:, 12 + m, :], rw[:, 14, :],
                                 start=True, stop=True)
                ins.then_inc(lora_mm, 1)
                head_sum(rk["d1"], 2)
                head_sum(rk["tmp"], 4)
                c_ = chunk_at
                out4 = lambda b, g: ps[:, b, g * P:(g + 1) * P]
                with seen.loop(NCH, {blocks_in: 1, blk_out: CHUNK_OUTS}) as c:
                    def four(bank, *terms):
                        for g in range(G4):
                            for n, (lhs, rhs) in enumerate(terms):
                                lhs_ = lhs[:, g, :] if not lhs is ident else ident
                                ins = mm(out4(bank, g), lhs_, rhs[:, g, :], start=(n == 0), stop=(n == len(terms) - 1))
                        ins.then_inc(pe_blk, 1)

                    def turn(bank, src):
                        for g in range(G4):
                            ins = pe.transpose(out4(bank, g), src[:, g, :], ident)
                        ins.then_inc(pe_blk, 1)

                    A, B, K, R = c_["Abd"], c_["Bbd"], c_["Kbd"], c_["Rbd"]
                    seen(blocks_in)
                    four(2, (B, A))
                    four(3, (A, B))
                    four(4, (K, A))
                    four(5, (B, R))
                    four(6, (K, R))
                    turn(7, A)
                    seen(blk_out)
                    turn(2, B)
                    seen(blk_out)
                    turn(3, K)
                    seen(blk_out)
                    turn(4, c_["Vbd"])
                    seen(blk_out, 7)
                    for lev in range(5):
                        cur = lev % 2
                        four(5, (c_["LT"], c_[f"X{cur}"]))
                        seen(blk_out)
                        four(6, (c_[f"XT{cur}"], c_["Z"]))
                        four(7, (c_["Z"], c_[f"XT{cur}"]))
                        seen(blk_out, 2)
                    XT = c_["XT1"]
                    four(2, (c_["L2T"], c_["Vt"]))
                    four(3, (XT, c_["At"]))
                    seen(blk_out)
                    four(4, (XT, c_["Gm"]))
                    seen(blk_out)
                    four(5, (c_["XA"], c_["T1T"]))
                    four(6, (c_["XA"], c_["Bt"]))
                    seen(blk_out, 3)
                    S = c_["S0"]
                    four(7, (c_["U0"], c_["T1T"]), (c_["Vt"], c_["T2T"]), (S, c_["RpT"]))
                    four(2, (c_["Bt"], c_["U0"]), (c_["Kt"], c_["Vt"]), (c_["Q"], S), (ident, S))
                    seen(blk_out, 2)
                head_sum(rk["y"], 2, wait=False)
                head_sum(rk["tmp"], 4)
                seen(hsum_in)
                pe.wait_ge(pool_ready, l + 1)
                for g in range(G4):
                    src = rk["pb"] if g % 2 == 0 else rk["pa"]
                    ins = mm(ps[:, 6 + g // 2, (g % 2) * T:(g % 2 + 1) * T], lw[:, 16 + g, :], src[:, g, 16:],
                             start=True, stop=True)
                ins.then_inc(pool_mm, 1)

            def lru():
                products("lgate")
                products("lrec")
                pe.wait_ge(small_in, SMALL["mix2"])
                seen(xc_ready)
                pe.wait_ge(taken, TAKEN["lrec"] + 8)
                for gate in range(2):
                    for h in range(4):
                        for jt in range(2):
                            c = 2 * h + jt
                            for ic in range(2):
                                ins = mm(ps[:, 4 * gate + c // 2, (c % 2) * T:(c % 2 + 1) * T],
                                         lr["wts"][:, ((gate * 4 + h) * 2 + ic) * 2 + jt, :], lr["xc"][:, 2 * h + ic, :],
                                         start=(ic == 0), stop=(ic == 1))
                ins.then_inc(gates_mm, 1)

            def attention():
                products("dkv")
                sum_squares(wide, DC)
                seen(h_split)
                products("dq")
                sum_squares(ml["sq"], 2)
                sum_squares(ml["sq"], 3)
                pe.wait_ge(small_in, SMALL["mix3"])
                seen(lat_in)
                pe.wait_ge(taken, TAKEN["dq"] + 3)
                jobs = [(ml["uk"], 2, ml["ck"], m) for m in range(8)] + [(ml["uq"], 3, ml["cq"], m) for m in range(16)]
                for n in range(0, len(jobs), 2):
                    bank = (n // 2) % 8
                    if n // 2 >= 8:
                        seen(kv_out)
                    for half in range(2):
                        w, kc, rhs, m = jobs[n + half]
                        for c in range(kc):
                            ins = mm(ps[:, bank, half * T:(half + 1) * T], w[:, m * kc + c, :], rhs[:, c, :],
                                     start=(c == 0), stop=(c == kc - 1))
                    ins.then_inc(kv_mm, 1)
                for kt in range(TT):
                    for half in range(2):
                        seen(kv_out)
                        for c in range(2):
                            ins = mm(ps[:, 4 + 2 * kt + half, :], ml["ck"][:, c, kt * P:(kt + 1) * P],
                                     ml["uv"][:, c, half * 512:(half + 1) * 512], start=(c == 0), stop=(c == 1))
                        ins.then_inc(kv_mm, 1)
                seen(kv_out, 8)
                seen(lat_in)
                for h in range(AH):
                    a, r = 64 * (h % 2), 32 * (h % 4)
                    for q in range(TT):
                        o = ps[:, 2 + h % 2, q * T:(q + 1) * T]
                        mm(o, ml["qn"][a:a + 64, h // 2, q * P:(q + 1) * P], ml["kn"][a:a + 64, h // 2, :],
                           start=True, stop=False)
                        ins = mm(o, ml["qr"][r:r + 32, h // 4, q * P:(q + 1) * P], ml["kr"][r:r + 32, :],
                                 start=False, stop=True)
                    ins.then_inc(sc_mm, 1)
                    seen(p_ready)
                    for kt in range(TT):
                        for q in range(TT):
                            ins = pe.transpose(ps[:, 4 + h % 2, kt * T + q * P:kt * T + (q + 1) * P],
                                               ml["p"][:, q, kt * P:(kt + 1) * P], ident)
                    ins.then_inc(pt_mm, 1)
                    seen(pt_out)
                    if h % 2 == 0 and h:
                        seen(av_out)
                    for kt in range(TT):
                        ins = mm(ps[:, 6, 0:T], ml["vpad"][:, kt, h, :], ml["pT"][:, kt, :],
                                 start=(h % 2 == 0 and kt == 0), stop=(h % 2 == 1 and kt == 1))
                    if h % 2:
                        ins.then_inc(av_mm, 1)

            def peer(l):
                products(f"q{l}")
                pe.wait_ge(keys_in, 16 * (l + 1))
                pe.wait_ge(taken, TAKEN[f"q{l}"] + 16)
                for tt in range(TT):
                    for b in range(4):
                        if tt:
                            seen(score_out)
                        for k in range(4):
                            hp = 4 * b + k
                            ins = mm(ps[:, 2 + b, k * P:(k + 1) * P], tk["q"][:, hp, tt * P:(tt + 1) * P],
                                     tk["keys"][:, hp, :], start=True, stop=True)
                        ins.then_inc(score_mm, 1)
                seen(score_out, 4)
                for tt in range(TT):
                    seen(chosen)
                    for w in range(3):
                        ins = pe.transpose(ps[:, 6 + tt, w * P:(w + 1) * P], tk["e"][:, w].rearrange("p h k -> p (h k)"), ident)
                    ins.then_inc(chosen_t, 1)
                products(f"u{l}")
                pe.wait_ge(taken, TAKEN[f"u{l}"] + KEYS)
                turns = T // 8

                def gate(b):
                    for q in range(4):
                        ins = mm(ps[:, b, q * P:(q + 1) * P], oh1[:, b, q, :], oh2[:, b, q, :], start=True, stop=True)
                    ins.then_inc(gates_t, 1)
                for b in range(2):
                    seen(hot)
                    gate(b)
                with seen.loop(turns - 1, {hot: 2, gated: 2}) as i:
                    for b in range(2):
                        seen(hot)
                        seen(gated)
                        gate(b)
                seen(gated, 2)
                first = SEGS[f"v{l}"][0]

                def step(n, j, k, i):
                    pe.wait_ge(lo_done, n + 1)
                    pe.wait_ge(wal, k + (1 + KEYS * l))
                    b = j % 2
                    one, last = (i is None and k == 0), (i is None and k == KEYS - 1)
                    for tt in range(TT):
                        up = wa_hi[:, b, tt * P:(tt + 1) * P]
                        down = wa_lo[:, b, tt * P:(tt + 1) * P]
                        for half in range(2):
                            cols = slice(half * 512, (half + 1) * 512)
                            o = ps[:, 2 + 2 * tt + half, :]
                            mm(o, up, t_hi[:, j % SPL, cols], start=one, stop=False)
                            mm(o, up, t_lo[:, j % SPL, cols], start=False, stop=False)
                            ins = mm(o, down, t_hi[:, j % SPL, cols], start=False, stop=last)
                    ins.then_inc(tile_used, 1)
                step(first, first, 0, None)
                tiles_in_loops(pe, first + 1, KEYS - 1, lambda n, j, k, i: step(n, j, k + 1, i))
                seen(moe_out)
                for m in range(4):
                    for c in range(2):
                        for tt in range(TT):
                            ins = pe.transpose(ps[:, [6, 7, 0, 1][m], c * T + tt * P:c * T + (tt + 1) * P],
                                               sum_sb[:, tt, (2 * m + c) * P:(2 * m + c + 1) * P], ident)
                    ins.then_inc(moe_t, 1)

            pe.wait_ge(par_in, 32)
            seen(csplit)
            for l in range(4):
                modulation(f"ada{l}", l // 2, 2)
                if l == 3:
                    modulation("kvada", 1, 3)
                sum_squares(wide, DC)
                seen(h_split)
                if l < 2:
                    rwkv(l)
                elif l == 2:
                    lru()
                else:
                    attention()
                seen(h_split)
                products(("out0", "out1", "lout", "wo")[l])
                sum_squares(wide, DC)
                seen(h_split)
                peer(l)
                if l % 2:
                    sum_squares(wide, DC)


def _by_chunk(a, n):
    a = np.asarray(a)
    return np.moveaxis(a.reshape(*a.shape[:-1], n, P), -1, 0)


def _tiles(w, pad=0):
    w = np.asarray(w)
    if pad:
        w = np.concatenate([w, np.zeros((w.shape[0], pad), w.dtype)], axis=1)
    m = w.shape[1] // P
    return w.reshape(DC, P, m, P).transpose(2, 1, 0, 3).reshape(m, P, D)


def _constants():
    i = np.arange(P)
    row, col = i[:, None], i[None, :]
    same = row // 64 == col // 64
    out = [row == col, np.ones((P, P)), same, np.broadcast_to(col, (P, P)),
           same & (row < col), same & (row > col), same & (row <= col),
           (row // 2 == col // 2) & (row < col), (row // 2 == col // 2) & (row > col)]
    for n in (2, 4, 8, 16, 32):
        out.append((row // (2 * n) == col // (2 * n)) & (row // n > col // n))
    return np.stack([np.asarray(m, np.float32) for m in out], axis=1)


def _layout(i):
    f = np.float32
    par = np.zeros((P, NPAR), f)

    def put(name, v):
        a, n = PCOLS[name]
        par[:, a:a + n] = np.asarray(v).reshape(P, n)

    put("c0", _by_chunk(i["c"], 8))
    put("c1", _by_chunk(i["c_2"], 8))
    for l in range(4):
        b = l // 2
        put(f"ada_b{l}", _by_chunk(i["ada_b_2" if b else "ada_b"][l % 2], 48))
        put(f"mix_g{l}", _by_chunk(i["norm_mix_g_2" if b else "ln1_g"][l % 2], 8))
        put(f"ffn_g{l}", _by_chunk(i["norm_ffn_g_2" if b else "ln2_g"][l % 2], 8))
    for l in range(2):
        mu = np.zeros((15 * P,), f)
        mu[:14 * P] = i["mu_shift"][l]
        if l:
            mu[14 * P:14 * P + 32] = i["vres_mu"][0]
        put(f"mu{l}", _by_chunk(mu, 15))
        for n in ("w0", "a0", "k_k", "k_a", "lnx_g", "lnx_b", "pool_scale"):
            put(f"{n}{l}", _by_chunk(i[n][l], 4))
        put(f"r_k{l}", _by_chunk(np.asarray(i["r_k"][l]).reshape(-1), 4))
    put("vres_v0", _by_chunk(i["vres_v0"][0], 4))
    put("lnf_g", _by_chunk(i["lnf_g"], 8))
    put("conv_w", _by_chunk(i["lru_conv_w_2"][0], 8))
    for n, src in (("conv_b", "lru_conv_b_2"), ("ba", "lru_ba_2"), ("bx", "lru_bx_2"), ("lam", "lru_lambda_2")):
        put(n, _by_chunk(i[src][0], 8))
    put("kv_g", _by_chunk(i["kv_norm_g_2"], 8))
    put("final_g", _by_chunk(i["final_g_2"], 8))
    put("kv_ada_b", _by_chunk(i["kv_ada_b_2"], 16))
    put("ckv_g", _by_chunk(i["mla_kv_latent_g_2"], 2))
    put("cq_g", _by_chunk(i["mla_q_latent_g_2"][0], 3))
    freq = np.float32(10000.0) ** (-np.arange(16, dtype=f) / np.float32(16))
    put("freq", freq[np.arange(P) % 16])
    put("sign", np.where(np.arange(P) % 32 < 16, -1.0, 1.0).astype(f))

    swap = np.r_[16:32, 0:16]
    kr = np.asarray(i["mla_w_kr_2"])
    w = []
    for l in range(4):
        w.append(_tiles(i["ada_w_2" if l > 1 else "ada_w"][l % 2]))
        if l == 0:
            w += [_tiles(i["w_in"][0]), _tiles(i["w_out"][0])]
        elif l == 1:
            w += [_tiles(i["w_in"][1]), _tiles(i["vres_down"][0], pad=96), _tiles(i["w_out"][1])]
        elif l == 2:
            w += [_tiles(i["lru_w_in_2"][0]), _tiles(i["lru_w_out_2"][0])]
        else:
            w += [_tiles(i["kv_ada_w_2"]), _tiles(i["mla_w_dkv_2"]), _tiles(np.tile(kr, (1, 4))),
                  _tiles(np.tile(kr[:, swap], (1, 4))), _tiles(i["mla_w_dq_2"][0]), _tiles(i["mla_w_o_2"][0])]
        w.append(_tiles(i["peer_w_q_2" if l > 1 else "peer_q"][l % 2]))
    w = np.concatenate(w)

    u = np.concatenate([np.asarray(i[n][l]).reshape(KEYS, KEYS, DC, P).transpose(1, 3, 2, 0).reshape(KEYS, P, D)
                        for n in ("peer_u", "peer_u_2") for l in range(2)])
    v = np.concatenate([np.asarray(i[n]).reshape(2, KEYS, KEYS, D) for n in ("peer_v", "peer_v_2")])

    lora = np.zeros((2, P, 20, P), f)
    for l in range(2):
        lora[l, :64, 0:4] = np.asarray(i["w_up"][l]).reshape(64, 4, P)
        lora[l, 64:, 4:8] = np.asarray(i["a_up"][l]).reshape(64, 4, P)
        lora[l, :, 8:12] = np.asarray(i["g_up"][l]).reshape(P, 4, P)
        if l:
            lora[l, :32, 12:16] = np.asarray(i["vres_up"][0]).reshape(32, 4, P)
        lora[l, :, 16:20] = np.asarray(i["pool_w"][l]).transpose(1, 0, 2)

    lru = np.stack([np.asarray(i[n][0]).reshape(4, 2, P, 2, P) for n in ("lru_wa_2", "lru_wx_2")])
    lru = lru.transpose(3, 0, 1, 2, 4, 5).reshape(P, 32, P)

    uq = np.asarray(i["mla_w_uq_2"][0]).reshape(3, P, AH, 96)
    rope = uq[..., 64:]
    parts = [uq[..., :64].reshape(3, P, 8, P), rope.reshape(3, P, 4, P), rope[..., swap].reshape(3, P, 4, P)]
    uq = np.concatenate(parts, axis=2).transpose(1, 2, 0, 3).reshape(P, 48, P)
    uk = np.asarray(i["mla_w_uk_2"]).reshape(2, P, 8, P).transpose(1, 2, 0, 3).reshape(P, 16, P)
    mla = np.concatenate([uq, uk], axis=1)
    uv = np.asarray(i["mla_w_uv_2"]).reshape(2, P, D).transpose(1, 0, 2)

    keys = np.concatenate([np.asarray(i[n]) for n in ("peer_keys", "peer_sub_keys_2")])
    keys = keys.reshape(4, 16, KEYS, P).transpose(0, 3, 1, 2)

    pos = np.arange(1, T + 1, dtype=f)
    inv = np.stack([1.0 / np.minimum(pos, f(win)) for win in WINDOWS]).astype(f)
    inv = np.broadcast_to(inv, (P, 4, T))
    xt = _by_chunk(i["x"][0], 8).transpose(0, 2, 1)
    return {"x_in": xt, "w_tiles": w, "u_tiles": u, "v_tiles": v, "params": par, "consts": _constants(),
            "lora": lora, "lru_w": lru, "mla_w": mla, "mla_uv": uv, "keys_t": keys, "pool_inv": inv,
            "positions": np.asarray(i["positions_2"])}


def kernel(**inputs):
    import concourse.bacc as bacc
    from concourse.bass_utils import run_bass_kernel_spmd as run

    arrays = {n: np.ascontiguousarray(a) for n, a in _layout({n: np.asarray(a) for n, a in inputs.items()}).items()}
    nc = bacc.Bacc("TRN2", target_bir_lowering=False, num_devices=1)
    args = [nc.dram_tensor(n, a.shape, mybir.dt.from_np(a.dtype), kind="ExternalInput").ap() for n, a in arrays.items()]
    out = nc.dram_tensor("out_xt", (P, DC, T), F32, kind="ExternalOutput").ap()
    build(nc, *args, out)
    r = run(nc, [arrays], core_ids=[0])
    got = np.asarray(r.results[0]["out_xt"])
    return np.ascontiguousarray(got.transpose(2, 1, 0)).reshape(1, T, D)
```

```python
from contextlib import ExitStack, contextmanager

import numpy as np

import concourse.bass as bass
from concourse import mybir

F32 = mybir.dt.float32
F32R = mybir.dt.float32r
U32 = mybir.dt.uint32
I32 = mybir.dt.int32
ALU = mybir.AluOpType
ACT = mybir.ActivationFunctionType
AX = mybir.AxisListType

P = 128
T = 256
D = 1024
DC = D // P
TT = T // P
RW = 512
G4 = RW // P
CH = 64
NCH = T // CH
HEADS = 8
TOPK = 16
KEYS = 128
EXPERTS = KEYS * KEYS
GN_EPS = 64e-5
EPS = 1e-6
DECAY = float(np.exp(-0.5))
WINDOWS = (2, 4, 8, 16)
AH = 16
ATT_SCALE = 1.0 / float(np.sqrt(96.0))
NEG = -1e30
LOWEST = -3.0e38

RAW = 4
SPL = 2

PCOLS = {}


def _cols(name, n):
    PCOLS[name] = (sum(k for _, k in PCOLS.values()), n)


_cols("c0", 8)
_cols("c1", 8)
for _l in range(4):
    _cols(f"ada_b{_l}", 48)
    _cols(f"mix_g{_l}", 8)
    _cols(f"ffn_g{_l}", 8)
for _l in range(2):
    _cols(f"mu{_l}", 15)
    for _n in ("w0", "a0", "k_k", "k_a", "r_k", "lnx_g", "lnx_b", "pool_scale"):
        _cols(f"{_n}{_l}", 4)
_cols("vres_v0", 4)
_cols("lnf_g", 8)
_cols("conv_w", 32)
for _n in ("conv_b", "ba", "bx", "lam", "kv_g", "final_g"):
    _cols(_n, 8)
_cols("kv_ada_b", 16)
_cols("ckv_g", 2)
_cols("cq_g", 3)
_cols("freq", 1)
_cols("sign", 1)
NPAR = sum(k for _, k in PCOLS.values())

SEGS = {}


def _plan():
    n = w = 0
    for l in range(4):
        mix = [[("in0", 18), ("out0", 8)], [("in1", 19), ("out1", 8)],
               [("lgate", 8), ("lrec", 8), ("lout", 8)],
               [("dkv", 4), ("dq", 3), ("wo", 8)]][l]
        for name, count in [("ada0", 48)] * (l == 0) + mix + [(f"q{l}", 16)]:
            SEGS[name] = (n, count, "w", w)
            n, w = n + count, w + count
        SEGS[f"u{l}"] = (n, KEYS, "u", l)
        n += KEYS
        if l < 3:
            count = 48 + 16 * (l == 2)
            SEGS[f"ada{l + 1}"] = (n, count, "w", w)
            n, w = n + count, w + count
        SEGS[f"v{l}"] = (n, KEYS, "v", l)
        n += KEYS
    return w


NW = _plan()
TAKEN = {}
WHOLE = {}
_e = _w = 0
for _name in SEGS:
    TAKEN[_name], WHOLE[_name] = _e, _w
    if _name.startswith("ada"):
        _w += SEGS[_name][1]
    elif _name[0] != "v":
        _e += SEGS[_name][1]
RANK_KEYS, PAIRS, RANK_PAIRS, SOFT, LOOK_UP, CHOSEN = 0, 16, 18, 34, 35, 47
STEPS = 48
ROWS = [0, 6, 12, 18]

SMALL = {"mix0": 48, "mix1": 96, "mix2": 112, "mix3": 192}
HSPLIT = {"ffn0": 3, "ffn1": 6, "ffn2": 9, "ffn3": 13}
CHUNK_STEPS = 31
CHUNK_OUTS = 32
MASKS = 10


def in_loops(eng, name, a, b, body):
    tiles_in_loops(eng, SEGS[name][0] + a, b - a, lambda n, j, k, i: body(n, j, k + a, i))


def tiles_in_loops(eng, first, count, body):
    k = 0
    while k < count and first + k < RAW:
        body(first + k, first + k, k, None)
        k += 1
    turns = (count - k) // 4
    if turns >= 2:
        with eng.Fori(0, turns) as i:
            for j in range(4):
                body(first + k + j + i * 4, first + k + j, k + j + i * 4, i)
        k += 4 * turns
    while k < count:
        body(first + k, first + k, k, None)
        k += 1


class Seen:

    def __init__(self, eng, chain):
        self.eng, self.chain_sem, self.base, self.here = eng, chain, {}, None

    def __call__(self, sem, k=1):
        if self.here is None:
            self.base[sem.name] = self.base.get(sem.name, 0) + k
            self.eng.wait_ge(sem, self.base[sem.name])
        else:
            i, per, got = self.here
            got[sem.name] = got.get(sem.name, 0) + k
            at = self.base.get(sem.name, 0) + got[sem.name]
            self.eng.wait_ge(sem, at if i is None else i * per[sem.name] + at)

    def link(self, ins, sem=None):
        sem = sem or self.chain_sem
        ins.then_inc(sem, 1)
        self(sem)

    @contextmanager
    def loop(self, turns, per):
        per = {s.name: k for s, k in per.items()}
        with self.eng.Fori(0, turns) as i:
            self.here = (i, per, {})
            yield i
            got = self.here[2]
        assert got == per, (got, per)
        self.here = None
        for s, k in per.items():
            self.base[s] = self.base.get(s, 0) + turns * k


def build(nc, x_in_dram, w_tiles, u_tiles, v_tiles, params, consts, lora, lru_w, mla_w, mla_uv, keys_t, pool_inv,
          positions, out):
    with ExitStack() as ctx:
        def sb(name, shape, dt=F32):
            return ctx.enter_context(nc.sbuf_tensor(name, shape, dt))

        def sem(name):
            return ctx.enter_context(nc.semaphore(name))

        arena = sb("arena", [P, KEYS * T])
        raw = sb("raw", [P, RAW, D])
        t_hi = sb("t_hi", [P, SPL, D], F32R)
        t_lo = sb("t_lo", [P, SPL, D], F32R)
        x = sb("x", [P, DC, T])
        h_hi = sb("h_hi", [P, DC, T], F32R)
        h_lo = sb("h_lo", [P, DC, T], F32R)
        par = sb("par", [P, NPAR])
        cst = sb("cst", [P, 4, P])
        mods = sb("mods", [P, 2, 48])
        mod_kv = sb("mod_kv", [P, 16])
        gain = sb("gain", [P, DC])
        c_act = sb("c_act", [P, 2, DC])
        mod_row = sb("mod_row", [1, D])
        v_first = sb("v_first", [P, G4, T])
        sel = sb("sel", [P, 3, T])
        ps = ctx.enter_context(nc.psum_tensor("ps", [P, 8, 512], F32))

        ident, ones, head_ones, iota = (cst[:, k, :] for k in range(4))

        def pcol(name):
            a, n = PCOLS[name]
            return par[:, a:a + n]

        def carve(spec):
            at, got = 0, {}
            for name, shape in spec:
                size = int(np.prod(shape))
                v = arena[:, at:at + size]
                if len(shape) > 1:
                    names = " ".join(f"a{k}" for k in range(len(shape)))
                    v = v.rearrange(f"p ({names}) -> p {names}", **{f"a{k}": s for k, s in enumerate(shape)})
                got[name] = v
                at += size
            assert at <= KEYS * T, at
            return got

        act_all = arena[:, :].rearrange("p (e t) -> p e t", t=T)
        quad = (G4, T)
        rk = carve([("A", quad), ("B", quad), ("z", (19, T + 1)), ("rw", (15, T)), ("dec", quad), ("d1", quad),
                    ("Pinv", quad), ("Pprev", quad), ("kk", quad), ("kp", quad), ("tmp", quad), ("Pc", quad),
                    ("a", quad), ("gate", quad), ("K", quad), ("R", quad), ("bonus", quad), ("y", quad),
                    ("lora", (20, P)), ("masks", (MASKS, P)), ("pa", (4, T + 16)), ("pb", (4, T + 16)),
                    ("inv", quad)])
        wide = carve([("w", (DC, T))])["w"]
        chunk_at = {}
        at_rw = 2048 + 19 * (T + 1)
        free = [2048 + 512 * k for k in range(9)] + [at_rw + 512 * k for k in range(4)] \
            + [at_rw + 15 * T + 512 * k for k in range(14)]
        for name in ("Abd", "Bbd", "Kbd", "Rbd", "Vbd", "LT", "L2T", "T1T", "T2T", "At", "Bt", "Kt", "Vt", "Gm",
                     "X0", "X1", "XT0", "XT1", "Z", "U0", "XA", "RpT", "Q", "S0"):
            a = free.pop(0)
            chunk_at[name] = arena[:, a:a + 512].rearrange("p (g k) -> p g k", g=4)
        lr = carve([("w", (DC, T)), ("gate", (DC, T)), ("rp", (DC, T + 3)), ("xc", (DC, T)), ("rg", (DC, T)),
                    ("ig", (DC, T)), ("la", (DC, T)), ("a", (DC, T)), ("tau", (DC, T)), ("hs", (DC, T)),
                    ("wts", (32, P)), ("sp", (4, DC))])
        ml = carve([("w", (DC, T)), ("ck", (2, T)), ("krz", (2, T)), ("cq", (3, T)), ("uq", (48, P)),
                    ("uk", (16, P)), ("uv", (2, D)), ("kn", (DC, T)), ("kr", (T,)), ("qn", (DC, T)),
                    ("qr", (4, T)), ("qs", (4, T)), ("cos", (T,)), ("sin", (T,)), ("ang", (T,)), ("tmp", (4, T)),
                    ("vpad", (TT, AH, P)), ("mask", (TT, T)), ("mbias", (TT, T)), ("s", (TT, T)),
                    ("p", (TT, T)), ("pT", (TT, T)), ("posi", (T,)), ("posf", (T,)), ("posq", (TT,)),
                    ("posqi", (TT,)), ("st", (8,)), ("sq", (3, T)), ("rinv", (T,))])
        def ml_at(name):
            return {"uq": DC * T + 7 * T}[name]

        choice = [("s2", (P,)), ("cand", (HEADS, 256)), ("c2", (256,)), ("eq", (HEADS // 2, TOPK, TOPK)),
                  ("val", (16, TOPK)), ("idx", (16, TOPK)), ("idf", (16, TOPK)), ("cs", (HEADS, TOPK)),
                  ("ci", (HEADS, TOPK)), ("hat", (2, HEADS, TOPK)), ("hatu", (2, HEADS, TOPK)),
                  ("e", (3, HEADS, TOPK)), ("den", (2, HEADS))]
        TK_SLOT = KEYS - -(-sum(int(np.prod(shape)) for _, shape in choice) // T)
        SC_SLOT = TK_SLOT - TT * 16 * P // T
        assert SC_SLOT > STEPS + PAIRS + 2 and TK_SLOT > TT * STEPS + 6
        tk = carve([("w", (DC, T)), ("keys", (16, P)), ("q", (16, T)), ("gap", (SC_SLOT * T - 8192,)),
                    ("sc", (TT, 16, P)), *choice])
        sum_sb = carve([("w", (DC, T)), ("keys", (16, P)), ("sum", (TT, D))])["sum"]
        oh1 = sb("oh1", [P, 2, 4, P])
        ms_all = oh1[:, 0, 0:2, :].rearrange("p a k -> p (a k)")
        rinv_all = oh1[:, 0, 2:4, :].rearrange("p a k -> p (a k)")
        oh2 = sb("oh2", [P, 2, 4, P])
        wa_hi, wa_lo = h_hi, h_lo

        loaded = [sem(f"loaded{k}") for k in range(RAW)]
        hi_done = sem("hi_done")
        lo_done = sem("lo_done")
        tile_used = sem("tile_used")
        taken = sem("taken")
        par_in = sem("par_in")
        x_in = sem("x_in")
        small_in = sem("small_in")
        c_ready = sem("c_ready")
        row_out = sem("row_out")
        row_turned = sem("row_turned")
        mod_ready = sem("mod_ready")
        chains = {e: sem(f"chain_{e}") for e in ("act", "dve", "pool")}
        squares = sem("squares")
        sumsq = sem("sumsq")
        ms_ready = sem("ms_ready")
        root = sem("root")
        normed = sem("normed")
        h_full = sem("h_full")
        h_up = sem("h_up")
        h_split = sem("h_split")
        arena_free = sem("arena_free")
        shifted = sem("shifted")
        lora_in = sem("lora_in")
        lora_mm = sem("lora_mm")
        lora_out = sem("lora_out")
        hsum_in = sem("hsum_in")
        hsum = sem("hsum")
        hroot = sem("hroot")
        blocks_in = sem("blocks_in")
        pe_blk = sem("pe_blk")
        blk_out = sem("blk_out")
        pool_ready = sem("pool_ready")
        pool_mm = sem("pool_mm")
        z_free = sem("z_free")
        mix_ready = sem("mix_ready")
        xc_ready = sem("xc_ready")
        gates_mm = sem("gates_mm")
        gates_out = sem("gates_out")
        la_ready = sem("la_ready")
        ea_ready = sem("ea_ready")
        beta_in = sem("beta_in")
        beta = sem("beta")
        sp_a = sem("sp_a")
        sp_b = sem("sp_b")
        ang_ready = sem("ang_ready")
        trig = sem("trig")
        lat_in = sem("lat_in")
        kv_mm = sem("kv_mm")
        kv_out = sem("kv_out")
        sc_mm = sem("sc_mm")
        sc_ready = sem("sc_ready")
        exp_done = sem("exp_done")
        p_ready = sem("p_ready")
        pt_mm = sem("pt_mm")
        pt_out = sem("pt_out")
        av_mm = sem("av_mm")
        av_out = sem("av_out")
        keys_in = sem("keys_in")
        score_mm = sem("score_mm")
        score_out = sem("score_out")
        sm_in = sem("sm_in")
        sm_exp = sem("sm_exp")
        chosen = sem("chosen")
        chosen_t = sem("chosen_t")
        sel_ready = sem("sel_ready")
        ranked = sem("ranked")
        hot = sem("hot")
        gates_t = sem("gates_t")
        gated = sem("gated")
        wah = sem("wah")
        wal = sem("wal")
        moe_out = sem("moe_out")
        moe_t = sem("moe_t")
        x_ready = sem("x_ready")
        fin = sem("fin")
        out_done = sem("out_done")

        block = ctx.enter_context(nc.Block())

        @block.sync
        def _(sp):
            sp.dma_start(par[:, :], params).then_inc(par_in, 16)
            sp.dma_start(cst[:, :, :], consts[:, 0:4, :]).then_inc(par_in, 16)
            sp.dma_start(x[:, :, :], x_in_dram).then_inc(x_in, 16)
            for name, (first, count, source, s0) in SEGS.items():
                def load(n, j, k, i, name=name, source=source, s0=s0):
                    if j >= RAW:
                        last = name
                        if i is None and n - RAW < SEGS[name][0]:
                            last = [s for s in SEGS if SEGS[s][0] <= n - RAW][-1]
                        if last.startswith("ada"):
                            sp.wait_ge(tile_used, n - RAW + 1)
                        else:
                            sp.wait_ge(lo_done, n + (1 - RAW - WHOLE[last]))
                    slot = j % RAW
                    if source == "w":
                        src = w_tiles[bass.ds(s0 + k, 1)].rearrange("a p n -> p (a n)")
                    elif source == "u":
                        src = u_tiles[bass.ds(s0 * KEYS + k, 1)].rearrange("a p n -> p (a n)")
                    else:
                        src = v_tiles[s0, :, bass.ds(k, 1), :].rearrange("p a n -> p (a n)")
                    sp.dma_start(raw[:, slot, :], src).then_inc(loaded[slot], 16)
                for k in range(min(RAW, count)):
                    load(first + k, first + k, k, None)
                in_loops(sp, name, RAW, count, load) if count > RAW else None
            sp.wait_ge(fin, 1)
            sp.dma_start(out, wide).then_inc(out_done, 16)
            sp.wait_ge(out_done, 16)

        @block.gpsimd
        def _(pool):
            seen = Seen(pool, chains["pool"])

            def pooling(l):
                pool.wait_ge(small_in, SMALL[f"mix{l}"])
                seen(z_free)
                pa, pb, z = rk["pa"], rk["pb"], rk["z"]
                seen.link(pool.memset(pa[:, :, 0:16], 0.0))
                seen.link(pool.memset(pb[:, :, 0:16], 0.0))
                seen.link(pool.tensor_copy(pa[:, :, 16:], z[:, 14:18, 1:]))
                bufs = [pa, pb]
                for k, win in enumerate(WINDOWS):
                    src, dst, back = bufs[k % 2], bufs[(k + 1) % 2], win // 2
                    seen.link(pool.tensor_tensor(dst[:, k:, 16:], src[:, k:, 16:], src[:, k:, 16 - back:16 + T - back],
                                                 ALU.add))
                    seen.link(pool.tensor_tensor(dst[:, k, 16:], dst[:, k, 16:], rk["inv"][:, k, :], ALU.mult))
                    last = pool.tensor_tensor(dst[:, k, 16:], dst[:, k, 16:], z[:, 14 + k, 1:], ALU.subtract)
                    if k < len(WINDOWS) - 1:
                        seen.link(last)
                last.then_inc(pool_ready, 1)

            for l in range(4):
                if l:
                    seen(arena_free)
                if l < 2:
                    pool.dma_start(rk["lora"], lora[l]).then_inc(small_in, 16)
                    pool.dma_start(rk["masks"], consts[:, 4:4 + MASKS, :]).then_inc(small_in, 16)
                    pool.dma_start(rk["inv"], pool_inv).then_inc(small_in, 16)
                    pooling(l)
                elif l == 2:
                    pool.dma_start(lr["wts"], lru_w).then_inc(small_in, 16)
                else:
                    a = ml_at("uq")
                    pool.dma_start(arena[:, a:a + 64 * P].rearrange("p (m k) -> p m k", k=P), mla_w).then_inc(small_in, 16)
                    pool.dma_start(ml["uv"], mla_uv).then_inc(small_in, 16)
                    pool.dma_start(ml["posi"].bitcast(I32), positions[0:1, :].broadcast_to([P, T])).then_inc(small_in, 16)
                    for tt in range(TT):
                        pool.dma_start(ml["posqi"][:, tt:tt + 1].bitcast(I32),
                                       positions[0:1, tt * P:(tt + 1) * P].rearrange("a p -> p a")).then_inc(small_in, 16)
                pool.wait_ge(h_split, HSPLIT[f"ffn{l}"])
                pool.dma_start(tk["keys"], keys_t[l]).then_inc(keys_in, 16)

        @block.scalar
        def _(act):
            seen = Seen(act, chains["act"])

            def upper(n, j, i, name):
                turn = (j // RAW + 1) if i is None else i + (j // RAW + 1)
                act.wait_ge(loaded[j % RAW], turn * 16)
                if j >= SPL:
                    act.wait_ge(tile_used, n - SPL + 1)
                act.copy(t_hi[:, j % SPL, :], raw[:, j % RAW, :]).then_inc(hi_done, 1)

            def uppers(name):
                tiles_in_loops(act, *SEGS[name][:2], lambda n, j, k, i: upper(n, j, i, name))

            def project(name, take_out):
                first, count = SEGS[name][:2]
                upper(first, first, None, name)
                upper(first + 1, first + 1, None, name)

                def step(n, j, k, i):
                    upper(n, j, i, name)
                    take_out(k, j % 2).then_inc(taken, 1)
                tiles_in_loops(act, first + 2, count - 2, step)
                for k in (count - 2, count - 1):
                    act.wait_ge(tile_used, first + k + 1)
                    take_out(k, (first + k) % 2).then_inc(taken, 1)

            def at(k):
                return bass.ds(k, 1) if not isinstance(k, int) else slice(k, k + 1)

            def rows(l):
                first, count = SEGS[f"ada{l}"][:2]

                def take_out(g):
                    act.wait_ge(tile_used, first + 8 + g * 8)
                    if not (l == 0 and isinstance(g, int)):
                        act.wait_ge(row_turned, g + ROWS[l])
                    act.copy(mod_row[0:1, :], ps[0:1, 6:8, :].rearrange("p a k -> p (a k)")).then_inc(row_out, 1)
                take_out(0)
                with act.Fori(1, count // 8) as g:
                    take_out(g)

            def norm():
                seen(ms_ready)
                act.activation(rinv_all, ms_all, ACT.Sqrt).then_inc(root, 1)

            def modulate(shift):
                seen(normed)
                for c in range(DC):
                    ins = act.activation(wide[:, c, :], wide[:, c, :], ACT.Identity, bias=shift[:, c:c + 1],
                                         scale=gain[:, c:c + 1])
                seen.link(ins)
                ins = act.copy(h_hi[:, :, :], wide)
                ins.then_inc(h_up, 1)

            def split_upper(ready, k=1):
                seen(ready, k)
                act.copy(h_hi[:, :, :], wide).then_inc(h_up, 1)

            def rwkv(l):
                rw = rk["rw"]
                project(f"in{l}", lambda k, b: act.copy(rk["z"][:, at(k), 1:], ps[:, b:b + 1, 0:T]))
                seen(shifted)
                act.activation(rw[0:64, 12, :], rw[0:64, 12, :], ACT.Tanh).then_inc(lora_in, 1)
                act.activation(rw[:, 13, :], rw[:, 13, :], ACT.Sigmoid).then_inc(lora_in, 1)
                seen(lora_mm)
                for g in range(G4):
                    lo, hi = ps[:, 2 + g // 2, (g % 2) * T:(g % 2 + 1) * T], ps[:, 4 + g // 2, (g % 2) * T:(g % 2 + 1) * T]
                    d = act.activation(rk["dec"][:, g, :], lo, ACT.Sigmoid, bias=pcol(f"w0{l}")[:, g:g + 1])
                    act.activation(rk["a"][:, g, :], hi, ACT.Sigmoid, bias=pcol(f"a0{l}")[:, g:g + 1])
                for g in range(G4):
                    ins = act.copy(rk["gate"][:, g, :], ps[:, 6 + g // 2, (g % 2) * T:(g % 2 + 1) * T])
                if l:
                    for g in range(G4):
                        ins = act.activation(rk["tmp"][:, g, :], ps[:, g // 2, (g % 2) * T:(g % 2 + 1) * T], ACT.Sigmoid,
                                             bias=pcol("vres_v0")[:, g:g + 1])
                seen.link(ins)
                act.activation(rk["dec"], rk["dec"], ACT.Exp, scale=-DECAY).then_inc(lora_out, 1)
                seen(hsum)
                act.activation(rk["tmp"].rearrange("p (b g) t -> p b (g t)", b=2), ps[:, 2:4, :], ACT.Sqrt)\
                    .then_inc(hroot, 1)
                seen(hsum_in, 4)
                act.activation(rk["tmp"], rk["tmp"], ACT.Sqrt).then_inc(hroot, 1)
                seen(hsum, 3)
                split_upper(mix_ready)

            def lru():
                project("lgate", lambda k, b: act.activation(lr["gate"][:, at(k), :], ps[:, b:b + 1, 0:T], ACT.Gelu))
                project("lrec", lambda k, b: act.copy(lr["rp"][:, at(k), 3:], ps[:, b:b + 1, 0:T]))
                seen(sp_a)
                seen.link(act.activation(lr["sp"][:, 1, :], lr["sp"][:, 0, :], ACT.Exp, scale=-1.0))
                act.activation(lr["sp"][:, 1, :], lr["sp"][:, 1, :], ACT.Ln, bias=ones[:, 0:1]).then_inc(sp_b, 1)
                seen(gates_mm)
                for c in range(DC):
                    bank, half = c // 2, slice((c % 2) * T, (c % 2 + 1) * T)
                    act.activation(lr["rg"][:, c, :], ps[:, bank, half], ACT.Sigmoid, bias=pcol("ba")[:, c:c + 1])
                    ins = act.activation(lr["ig"][:, c, :], ps[:, 4 + bank, half], ACT.Sigmoid,
                                         bias=pcol("bx")[:, c:c + 1])
                ins.then_inc(gates_out, 1)
                seen(la_ready)
                act.activation(lr["tau"], lr["la"], ACT.Tanh, scale=-1.0).then_inc(ea_ready, 1)
                act.activation(lr["a"], lr["la"], ACT.Exp).then_inc(ea_ready, 1)
                seen(beta_in)
                act.activation(lr["tau"], lr["tau"], ACT.Sqrt, scale=2.0).then_inc(beta, 1)
                split_upper(mix_ready)

            def attention():
                project("dkv", lambda k, b: act.copy(
                    ml["ck"][:, k, :] if k < 2 else ml["krz"][:, k - 2, :], ps[:, b, 0:T]))
                modulate_for("mix3")
                project("dq", lambda k, b: act.copy(ml["cq"][:, k, :], ps[:, b, 0:T]))
                seen(ang_ready, 2)
                act.activation(ml["cos"], ml["cos"], ACT.Sin)
                act.activation(ml["sin"], ml["sin"], ACT.Sin).then_inc(trig, 1)
                for _ in range(2):
                    seen(ms_ready)
                    act.activation(ml["rinv"], ml["rinv"], ACT.Sqrt).then_inc(root, 1)
                for h in range(AH):
                    seen(sc_ready)
                    for q in range(TT):
                        ins = act.activation(ml["p"][:, q, :], ml["s"][:, q, :], ACT.Exp, bias=ml["st"][:, q:q + 1],
                                             accum_out=ml["st"][:, 2 + q:3 + q])
                    ins.then_inc(exp_done, 1)
                split_upper(av_out, AH // 2)

            def modulate_for(which):
                norm()
                if which == "kv":
                    modulate(mod_kv[:, 0:8])
                else:
                    a = 0 if which.startswith("mix") else 24
                    modulate(mods[:, int(which[-1]) % 2, a:a + 8])

            def peer(l):
                project(f"q{l}", lambda k, b: act.copy(tk["q"][:, at(k), :], ps[:, b:b + 1, 0:T]))
                for tt in range(TT):
                    for b in range(4):
                        seen(score_mm)
                        act.copy(tk["sc"][:, tt, 4 * b:4 * b + 4, :].rearrange("p a k -> p (a k)"),
                                 ps[:, 2 + b, :]).then_inc(score_out, 1)
                name = f"u{l}"
                first = SEGS[name][0]

                def gelu(k, b):
                    act.activation(act_all[:, at(k), :], ps[:, b:b + 1, 0:T], ACT.Gelu).then_inc(taken, 1)

                def step(n, j, k, i):
                    upper(n, j, i, name)
                    gelu(k - 2, j % 2)
                upper(first, first, None, name)
                upper(first + 1, first + 1, None, name)
                a = 2
                for tt in range(TT):
                    b = STEPS * tt + SOFT + 3
                    in_loops(act, name, a, b, step)
                    a = b
                    seen(sm_in)
                    act.activation(tk["e"][:, 2], tk["e"][:, 2], ACT.Exp).then_inc(sm_exp, 1)
                in_loops(act, name, a, SC_SLOT + 2, step)
                seen(ranked)
                in_loops(act, name, SC_SLOT + 2, TK_SLOT + 2, step)
                act.wait_ge(sel_ready, TT * (l + 1))
                in_loops(act, name, TK_SLOT + 2, KEYS, step)
                for k in (KEYS - 2, KEYS - 1):
                    act.wait_ge(tile_used, first + k + 1)
                    gelu(k, (first + k) % 2)
                if l < 3:
                    rows(l + 1)
                name = f"v{l}"
                first = SEGS[name][0]
                act.wait_ge(gated, (T // 4) * (l + 1))

                def upper_gated(k, j):
                    act.copy(wa_hi[:, j % 4:j % 4 + 1, :], act_all[:, at(k), :]).then_inc(wah, 1)

                def step(n, j, k, i):
                    upper(n, j, i, name)
                    upper_gated(k + 1, j + 1)
                upper_gated(0, first)
                tiles_in_loops(act, first, KEYS - 1, step)
                upper(first + KEYS - 1, first + KEYS - 1, None, name)

            act.wait_ge(par_in, 32)
            act.activation(c_act[:, 0, :], pcol("c0"), ACT.Silu).then_inc(c_ready, 1)
            act.activation(c_act[:, 1, :], pcol("c1"), ACT.Silu).then_inc(c_ready, 1)
            rows(0)
            for l in range(4):
                if l == 3:
                    modulate_for("kv")
                    attention()
                else:
                    modulate_for(f"mix{l}")
                    if l < 2:
                        rwkv(l)
                    else:
                        lru()
                uppers(("out0", "out1", "lout", "wo")[l])
                modulate_for(f"ffn{l}")
                peer(l)
                if l % 2:
                    norm()

        @block.vector
        def _(dve):
            seen = Seen(dve, chains["dve"])
            link = seen.link
            tts, ts, stt, cp = dve.tensor_tensor, dve.tensor_scalar, dve.scalar_tensor_tensor, dve.tensor_copy

            def lower(n, j, name):
                dve.wait_ge(hi_done, n + (1 - WHOLE[name]))
                tts(t_lo[:, j % SPL, :], raw[:, j % RAW, :], t_hi[:, j % SPL, :].bitcast(F32),
                    ALU.subtract).then_inc(lo_done, 1)

            def lowers(name):
                tiles_in_loops(dve, *SEGS[name][:2], lambda n, j, k, i: lower(n, j, name))

            def at(k):
                return bass.ds(k, 1) if not isinstance(k, int) else slice(k, k + 1)

            def add_products(name, gate):
                first, count = SEGS[name][:2]
                lower(first, first, name)
                lower(first + 1, first + 1, name)

                def take_out(k, b):
                    return stt(x[:, k, :], ps[:, b, 0:T], gate[:, k:k + 1], x[:, k, :], ALU.mult, ALU.add)

                for k in range(2, count):
                    lower(first + k, first + k, name)
                    take_out(k - 2, (first + k) % 2).then_inc(taken, 1)
                for k in (count - 2, count - 1):
                    dve.wait_ge(tile_used, first + k + 1)
                    take_out(k, (first + k) % 2).then_inc(taken, 1)
                dve.wait_ge(taken, TAKEN[name] + count)

            def modulation(l):
                dve.wait_ge(row_turned, ROWS[l] + SEGS[f"ada{l}"][1] // 8)
                if l == 3:
                    tts(mod_kv[:, :], ps[:, 5, 48:64], pcol("kv_ada_b"), ALU.add)
                link(tts(mods[:, l % 2, :], ps[:, 5, 0:48], pcol(f"ada_b{l}"), ALU.add), mod_ready)

            def norm_x():
                tts(wide, x[:, :, :], x[:, :, :], ALU.mult).then_inc(squares, 1)
                seen(sumsq)
                ts(ms_all, ps[:, 2, 0:T], 1.0 / D, EPS, ALU.mult, ALU.add).then_inc(ms_ready, 1)
                seen(root)
                link(dve.reciprocal(rinv_all, rinv_all))
                return tts(wide, x[:, :, :], rinv_all.unsqueeze(1).broadcast_to([P, DC, T]), ALU.mult)

            def norm(g, scale):
                link(stt(gain[:, :], scale, 1.0, g, ALU.add, ALU.mult))
                norm_x().then_inc(normed, 1)
                split_lower()

            def split_lower():
                seen(h_up)
                tts(h_lo[:, :, :], wide, h_hi[:, :, :].bitcast(F32), ALU.subtract).then_inc(h_split, 1)

            def rwkv(l):
                z, rw, kk, kp, a, v = rk["z"], rk["rw"], rk["kk"], rk["kp"], rk["a"], rk["rw"][:, 8:12, :]
                r, k, tmp, tmp2 = rw[:, 0:4, :], rw[:, 4:8, :], rk["tmp"], rk["d1"]
                name = f"in{l}"
                first, count = SEGS[name][:2]
                link(dve.memset(z[:, :, 0:1], 0.0))
                lowers(name)
                dve.wait_ge(taken, TAKEN[name] + count)
                link(tts(rw[:, 0:14, :], z[:, 0:14, 0:T], z[:, 0:14, 1:T + 1], ALU.subtract), z_free)
                if l:
                    link(tts(rw[:, 14, :], z[:, 18, 0:T], z[:, 18, 1:T + 1], ALU.subtract))
                for m in range(14 + l):
                    ins = stt(rw[:, m, :], rw[:, m, :], pcol(f"mu{l}")[:, m:m + 1], z[:, m + 4 * (m == 14), 1:],
                              ALU.mult, ALU.add)
                link(ins, shifted)
                if not l:
                    cp(v_first[:, :, :], v)
                for g in range(G4):
                    ins = ts(kk[:, g, :], k[:, g, :], pcol(f"k_k{l}")[:, g:g + 1], None, ALU.mult)
                link(ins)
                seen(lora_out)
                if l:
                    link(tts(v_first[:, :, :], v_first[:, :, :], v, ALU.subtract))
                    link(tts(v_first[:, :, :], v_first[:, :, :], tmp, ALU.mult))
                    link(tts(v, v, v_first[:, :, :], ALU.add))
                tts(tmp2, kk, kk, ALU.mult).then_inc(hsum_in, 1)
                link(ts(gain[:, 0:4], pcol(f"k_a{l}"), -1.0, 1.0, ALU.mult, ALU.add))
                for g in range(G4):
                    ins = ts(kp[:, g, :], a[:, g, :], pcol(f"k_a{l}")[:, g:g + 1], gain[:, g:g + 1], ALU.mult, ALU.add)
                link(ins)
                link(tts(kp, kp, k, ALU.mult))
                dec, Pc, Pinv, Pprev = rk["dec"], rk["Pc"], rk["Pinv"], rk["Pprev"]
                starts = lambda b: b.rearrange("p g (c t) -> p (g c) t", t=CH)
                seen(hsum)
                link(dve.memset(tmp2, 0.0))
                link(cp(starts(tmp2)[:, :, 0:1], starts(dec)[:, :, 0:1]))
                link(dve.memset(starts(dec)[:, :, 0:1], 0.0))
                flat = lambda b: b.rearrange("p g t -> p (g t)")
                link(dve.tensor_tensor_scan(flat(Pc), flat(dec), flat(tmp2), 0.0, ALU.mult, ALU.add))
                link(dve.reciprocal(Pinv, Pc))
                dve.memset(starts(Pprev)[:, :, 0:1], 1.0)
                link(cp(starts(Pprev)[:, :, 1:], starts(Pc)[:, :, 0:CH - 1]))
                seen(hroot)
                link(ts(tmp, tmp, 1e-12, None, ALU.max))
                link(dve.reciprocal(tmp, tmp))
                link(tts(kk, kk, tmp, ALU.mult))
                link(tts(rk["R"], r, kp, ALU.mult))
                for g in range(G4):
                    ins = ts(tmp[:, g, :], rk["R"][:, g, :], pcol(f"r_k{l}")[:, g:g + 1], None, ALU.mult)
                ins.then_inc(hsum_in, 1)
                link(stt(rk["A"], kk, -1.0, Pprev, ALU.mult, ALU.mult))
                link(tts(rk["B"], kk, a, ALU.mult))
                link(tts(rk["B"], rk["B"], Pinv, ALU.mult))
                link(tts(rk["K"], kp, Pinv, ALU.mult))
                link(tts(rk["R"], r, Pc, ALU.mult))
                seen(hsum)
                link(tts(rk["bonus"].rearrange("p (b g) t -> p b (g t)", b=2), ps[:, 4:6, :],
                         v.rearrange("p (b g) t -> p b (g t)", b=2), ALU.mult))
                dve.wait_ge(pool_ready, l + 1)
                c_ = chunk_at
                for n in ("Abd", "Bbd", "Kbd", "Rbd", "Vbd", "S0"):
                    ins = dve.memset(c_[n], 0.0)
                link(ins)
                masks = rk["masks"]
                SU, SL, IU, M1T, M1 = (masks[:, k, :] for k in range(5))
                bc = lambda m: m.unsqueeze(1).broadcast_to([P, G4, P])
                out4 = lambda b: ps[:, b, :].rearrange("p (g k) -> p g k", g=4)
                with seen.loop(NCH, {chains["dve"]: 2, pe_blk: CHUNK_STEPS, blocks_in: 1, blk_out: CHUNK_OUTS}) as c:
                    tok = bass.ds(c * CH, CH)
                    pairs = (("Abd", rk["A"]), ("Bbd", rk["B"]), ("Kbd", rk["K"]), ("Rbd", rk["R"]), ("Vbd", v))
                    for n, src in pairs:
                        cp(c_[n][0:64, :, 0:64], src[0:64, :, tok])
                        ins = cp(c_[n][64:128, :, 64:128], src[64:128, :, tok])
                    link(ins, blocks_in)

                    def out_of(bank, dst, mask=None, plus=None):
                        seen(pe_blk)
                        if mask is not None:
                            return tts(dst, out4(bank), bc(mask), ALU.mult)
                        if plus is not None:
                            return tts(dst, out4(bank), plus, ALU.add)
                        return cp(dst, out4(bank))

                    def done(ins):
                        link(ins, blk_out)

                    done(out_of(2, c_["LT"], SU))
                    done(out_of(3, c_["X0"], M1))
                    done(out_of(4, c_["L2T"], SU))
                    done(out_of(5, c_["T1T"], IU))
                    done(out_of(6, c_["T2T"], IU))
                    done(out_of(7, c_["At"]))
                    done(out_of(2, c_["Bt"]))
                    done(out_of(3, c_["Kt"]))
                    done(out_of(4, c_["Vt"]))
                    link(tts(c_["XT0"], c_["LT"], bc(M1T), ALU.mult))
                    link(tts(c_["X0"], c_["X0"], bc(ident), ALU.add))
                    done(tts(c_["XT0"], c_["XT0"], bc(ident), ALU.add))
                    for lev in range(5):
                        cur, nxt = lev % 2, (lev + 1) % 2
                        done(out_of(5, c_["Z"], masks[:, 5 + lev, :]))
                        done(out_of(6, c_[f"X{nxt}"], plus=c_[f"X{cur}"]))
                        done(out_of(7, c_[f"XT{nxt}"], plus=c_[f"XT{cur}"]))
                    done(out_of(2, c_["Gm"]))
                    done(out_of(3, c_["XA"]))
                    done(out_of(4, c_["U0"]))
                    done(out_of(5, c_["RpT"], plus=c_["Rbd"]))
                    done(out_of(6, c_["Q"]))
                    seen(pe_blk)
                    cp(rk["y"][0:64, :, tok], out4(7)[0:64, :, 0:64])
                    done(cp(rk["y"][64:128, :, tok], out4(7)[64:128, :, 64:128]))
                    seen(pe_blk)
                    end = rk["Pc"].rearrange("p g (c t) -> p g c t", t=CH)[:, :, bass.ds(c, 1), CH - 1]
                    done(tts(c_["S0"], out4(2), end.broadcast_to([P, G4, P]), ALU.mult))
                y = rk["y"]
                seen(hsum)
                halves = lambda b: b.rearrange("p (b g) t -> p b (g t)", b=2)
                link(stt(halves(y), ps[:, 2:4, :], -1.0 / 64, halves(y), ALU.mult, ALU.add))
                tts(tmp, y, y, ALU.mult).then_inc(hsum_in, 1)
                seen(hsum)
                ts(halves(tmp), ps[:, 4:6, :], 1.0 / 64, GN_EPS, ALU.mult, ALU.add).then_inc(hsum_in, 1)
                seen(hroot)
                link(dve.reciprocal(tmp, tmp))
                link(tts(y, y, tmp, ALU.mult))
                for g in range(G4):
                    ins = ts(y[:, g, :], y[:, g, :], pcol(f"lnx_g{l}")[:, g:g + 1], pcol(f"lnx_b{l}")[:, g:g + 1],
                             ALU.mult, ALU.add)
                link(ins)
                link(tts(y, y, rk["bonus"], ALU.add))
                tts(wide[:, 0:4, :], y, rk["gate"], ALU.mult)
                seen(pool_mm)
                for g in range(G4):
                    ins = ts(wide[:, 4 + g, :], ps[:, 6 + g // 2, (g % 2) * T:(g % 2 + 1) * T],
                             pcol(f"pool_scale{l}")[:, g:g + 1], None, ALU.mult)
                ins.then_inc(mix_ready, 1)
                split_lower()

            def lru():
                rp, xc = lr["rp"], lr["xc"]
                lowers("lgate")
                link(dve.memset(rp[:, :, 0:3], 0.0))
                lowers("lrec")
                link(ts(lr["sp"][:, 0, :], pcol("lam"), -1.0, None, ALU.mult))
                tts(lr["sp"][:, 0, :], lr["sp"][:, 0, :], pcol("lam"), ALU.max).then_inc(sp_a, 1)
                dve.wait_ge(taken, TAKEN["lrec"] + 8)
                w = lambda k, c: pcol("conv_w")[:, 8 * k + c:8 * k + c + 1]
                for c in range(DC):
                    ins = ts(xc[:, c, :], rp[:, c, 0:T], w(0, c), pcol("conv_b")[:, c:c + 1], ALU.mult, ALU.add)
                link(ins)
                for k in range(1, 4):
                    for c in range(DC):
                        ins = stt(xc[:, c, :], rp[:, c, k:k + T], w(k, c), xc[:, c, :], ALU.mult, ALU.add)
                    if k < 3:
                        link(ins)
                ins.then_inc(xc_ready, 1)
                link(ts(lr["sp"][:, 2, :], pcol("lam"), -1.0, 0.0, ALU.mult, ALU.max))
                seen(sp_b)
                link(tts(lr["sp"][:, 2, :], lr["sp"][:, 2, :], lr["sp"][:, 1, :], ALU.add))
                link(ts(lr["sp"][:, 3, :], lr["sp"][:, 2, :], -8.0, None, ALU.mult))
                seen(gates_out)
                for c in range(DC):
                    ins = ts(lr["la"][:, c, :], lr["rg"][:, c, :], lr["sp"][:, 3, c:c + 1], None, ALU.mult)
                ins.then_inc(la_ready, 1)
                link(tts(lr["ig"], lr["ig"], xc, ALU.mult))
                seen(ea_ready)
                link(ts(lr["rg"], lr["tau"], 1.0, None, ALU.add))
                link(dve.reciprocal(lr["rg"], lr["rg"]))
                tts(lr["tau"], lr["tau"], lr["rg"], ALU.mult).then_inc(beta_in, 1)
                seen(beta)
                link(tts(lr["ig"], lr["ig"], lr["tau"], ALU.mult))
                seen(ea_ready)
                for c in range(DC):
                    ins = dve.tensor_tensor_scan(lr["hs"][:, c, :], lr["a"][:, c, :], lr["ig"][:, c, :], 0.0,
                                                 ALU.mult, ALU.add)
                link(ins)
                tts(wide, lr["gate"], lr["hs"], ALU.mult).then_inc(mix_ready, 1)
                split_lower()

            def attention():
                lowers("dkv")
                norm(pcol("mix_g3"), mods[:, 1, 8:16])
                lowers("dq")
                dve.wait_ge(taken, TAKEN["dq"] + 3)
                dve.wait_ge(small_in, SMALL["mix3"])
                posf, ang, cos, sin, tmp = ml["posf"], ml["ang"], ml["cos"], ml["sin"], ml["tmp"]
                cp(ml["posq"], ml["posqi"].bitcast(I32))
                link(cp(posf, ml["posi"].bitcast(I32)))
                for tt in range(TT):
                    ins = ts(ml["mask"][:, tt, :], posf, ml["posq"][:, tt:tt + 1], None, ALU.is_le)
                link(ins)
                link(ts(ml["mbias"], ml["mask"], -1.0, -NEG, ALU.add, ALU.mult))
                link(ts(ang, posf, pcol("freq"), None, ALU.mult))
                MAGIC = 12582912.0
                C1, C2 = 6.28125, 0.0019350051879882812
                C3 = 2.0 * np.pi - C1 - C2
                for dst, quarter, add in ((sin, 0.0, 0.0), (cos, 0.25, float(np.pi / 2))):
                    link(ts(tmp[:, 0, :], ang, float(1 / (2 * np.pi)), quarter, ALU.mult, ALU.add))
                    link(ts(tmp[:, 1, :], tmp[:, 0, :], MAGIC, None, ALU.add))
                    link(ts(tmp[:, 1, :], tmp[:, 1, :], MAGIC, None, ALU.subtract))
                    link(stt(dst, tmp[:, 1, :], -C1, ang, ALU.mult, ALU.add))
                    link(stt(dst, tmp[:, 1, :], -C2, dst, ALU.mult, ALU.add))
                    link(stt(dst, tmp[:, 1, :], -float(C3), dst, ALU.mult, ALU.add))
                    if add:
                        link(ts(dst, dst, add, None, ALU.add))
                    link(ts(dst, dst, 3.1415925, -3.1415925, ALU.min, ALU.max), ang_ready)
                seen(trig)
                link(ts(sin, sin, pcol("sign"), None, ALU.mult))
                for lat, n, g in (("ck", 2, "ckv_g"), ("cq", 3, "cq_g")):
                    tts(ml["sq"][:, 0:n, :], ml[lat], ml[lat], ALU.mult).then_inc(squares, 1)
                    seen(sumsq)
                    ts(ml["rinv"], ps[:, 2, 0:T], 1.0 / (n * P), EPS, ALU.mult, ALU.add).then_inc(ms_ready, 1)
                    seen(root)
                    link(dve.reciprocal(ml["rinv"], ml["rinv"]))
                    for c in range(n):
                        ins = stt(ml[lat][:, c, :], ml[lat][:, c, :], pcol(g)[:, c:c + 1], ml["rinv"], ALU.mult, ALU.mult)
                    link(ins)
                link(tts(ml["kr"], ml["krz"][:, 0, :], cos, ALU.mult))
                link(tts(tmp[:, 0, :], ml["krz"][:, 1, :], sin, ALU.mult))
                link(tts(ml["kr"], ml["kr"], tmp[:, 0, :], ALU.add))
                link(dve.memset(ml["vpad"], 0.0), lat_in)
                pair = lambda v, a: v[:, a:a + 2, :].rearrange("p a t -> p (a t)")
                dsts = [pair(ml["kn"], a) for a in (0, 2, 4, 6)] + [pair(ml["qn"], a) for a in (0, 2, 4, 6)] \
                    + [pair(ml["qr"], a) for a in (0, 2)] + [pair(ml["qs"], a) for a in (0, 2)]
                for n, dst in enumerate(dsts):
                    seen(kv_mm)
                    link(cp(dst, ps[:, n % 8, :]), kv_out)
                for kt in range(TT):
                    for half in range(2):
                        seen(kv_mm)
                        src = ps[:, 4 + 2 * kt + half, :].rearrange("p (h two k) -> p h two k", two=2, k=64)
                        dst = ml["vpad"][:, kt, 8 * half:8 * half + 8, :].rearrange("p (h two) k -> p h two k", two=2)
                        cp(dst[:, :, 0, 0:64], src[:, :, 0, :])
                        link(cp(dst[:, :, 1, 64:128], src[:, :, 1, :]), kv_out)
                bc4 = lambda v: v.unsqueeze(1).broadcast_to([P, 4, T])
                link(tts(ml["qr"], ml["qr"], bc4(cos), ALU.mult))
                link(tts(ml["qs"], ml["qs"], bc4(sin), ALU.mult))
                link(tts(ml["qr"], ml["qr"], ml["qs"], ALU.add), lat_in)
                s, p, st = ml["s"], ml["p"], ml["st"]
                for h in range(AH):
                    seen(sc_mm)
                    link(stt(s, ps[:, 2 + h % 2, :].rearrange("p (q k) -> p q k", q=2), ATT_SCALE, ml["mask"],
                             ALU.mult, ALU.mult))
                    link(tts(s, s, ml["mbias"], ALU.add))
                    link(dve.tensor_reduce(st[:, 4:6], s, AX.X, ALU.max))
                    ts(st[:, 0:2], st[:, 4:6], -1.0, None, ALU.mult).then_inc(sc_ready, 1)
                    seen(exp_done)
                    link(dve.reciprocal(st[:, 6:8], st[:, 2:4]))
                    for q in range(TT):
                        ins = ts(p[:, q, :], p[:, q, :], st[:, 6 + q:7 + q], None, ALU.mult)
                    ins.then_inc(p_ready, 1)
                    seen(pt_mm)
                    cp(ml["pT"].rearrange("p a t -> p (a t)"), ps[:, 4 + h % 2, :]).then_inc(pt_out, 1)
                    if h % 2:
                        seen(av_mm)
                        cp(wide[:, h // 2, :], ps[:, 6, 0:T]).then_inc(av_out, 1)
                split_lower()

            def first8(src, other, val, idx):
                link(dve.max(val[:, 0:8], src))
                dve.max_index(idx[:, 0:8], val[:, 0:8], src)
                return dve.match_replace(other, val[:, 0:8], src, LOWEST)

            def next8(other, val, idx):
                link(dve.max(val[:, 8:16], other))
                return dve.max_index(idx[:, 8:16], val[:, 8:16], other)

            val, idx, idf, cs, ci = tk["val"], tk["idx"].bitcast(U32), tk["idf"], tk["cs"], tk["ci"].bitcast(U32)
            hat, hatu, e, eq = tk["hat"], tk["hatu"].bitcast(U32), tk["e"], tk["eq"]
            half_shape = [P, HEADS // 2, TOPK, TOPK]

            def two(v, w, h=slice(0, HEADS)):
                return v.rearrange("p (h two) k -> p two h k", two=2)[:, w, h]

            def pair_sums(part):
                h = slice(4 * part, 4 * part + 4)
                return tts(tk["cand"][:, h].rearrange("p h (i j) -> p h i j", i=TOPK),
                           two(val, 0, h).unsqueeze(3).broadcast_to(half_shape),
                           two(val, 1, h).unsqueeze(2).broadcast_to(half_shape), ALU.add)

            def look_up(w, part, step):
                h = slice(4 * part, 4 * part + 4)
                if step == 0:
                    return tts(eq, hat[:, w, h].unsqueeze(3).broadcast_to(half_shape),
                               iota[:, 0:TOPK].unsqueeze(1).unsqueeze(1).broadcast_to(half_shape), ALU.is_equal)
                if step == 1:
                    return tts(eq, eq, two(idf, w, h).unsqueeze(2).broadcast_to(half_shape), ALU.mult)
                return dve.tensor_reduce(e[:, w, h], eq, AX.X, ALU.add)

            def choose(l):
                name = f"u{l}"
                first = SEGS[name][0]

                def sel_out(tt):
                    seen(chosen_t)
                    cp(sel[:, :, tt * P:(tt + 1) * P], ps[:, 6 + tt, 0:3 * P].rearrange("p (w t) -> p w t", w=3))\
                        .then_inc(sel_ready, 1)

                for tt in range(TT):
                    for k in range(STEPS):
                        lower(first + STEPS * tt + k, first + STEPS * tt + k, name)
                        if k < PAIRS:
                            if k % 4 == 0:
                                seen(score_out)
                            src = tk["sc"][:, tt, k, :]
                            link(first8(src, tk["s2"], val[:, k, :], idx[:, k, :]))
                            link(next8(tk["s2"], val[:, k, :], idx[:, k, :]), *([ranked] if tt and k == 15 else []))
                            if tt and k == 4:
                                sel_out(0)
                        elif k < RANK_PAIRS:
                            if k == PAIRS:
                                link(cp(idf, idx))
                            link(pair_sums(k - PAIRS))
                        elif k < SOFT:
                            h, second = divmod(k - RANK_PAIRS, 2)
                            link(next8(tk["c2"], cs[:, h, :], ci[:, h, :]) if second
                                 else first8(tk["cand"][:, h, :], tk["c2"], cs[:, h, :], ci[:, h, :]))
                        elif k == SOFT:
                            tts(e[:, 2], cs, cs[:, :, 0:1].broadcast_to([P, HEADS, TOPK]), ALU.subtract)\
                                .then_inc(sm_in, 1)
                            ts(hatu[:, 0], ci, 4, None, ALU.logical_shift_right)
                            link(ts(hatu[:, 1], ci, TOPK - 1, None, ALU.bitwise_and))
                            link(cp(hat, hatu))
                        elif k < CHOSEN:
                            part, step = divmod(k - LOOK_UP, 3)
                            link(look_up(part // 2, part % 2, step))
                        else:
                            seen(sm_exp)
                            link(dve.tensor_reduce(tk["den"][:, 0, :], e[:, 2], AX.X, ALU.add))
                            link(dve.reciprocal(tk["den"][:, 1, :], tk["den"][:, 0, :]))
                            tts(e[:, 2], e[:, 2], tk["den"][:, 1, :].unsqueeze(2).broadcast_to([P, HEADS, TOPK]),
                                ALU.mult).then_inc(chosen, 1)
                a = TT * STEPS
                for k in range(a, a + 4):
                    lower(first + k, first + k, name)
                sel_out(1)
                in_loops(dve, name, a + 4, KEYS, lambda n, j, k, i: lower(n, j, name))

            def gates(l):
                def hots(g, b):
                    cols = bass.ds(g * 4, 4) if not isinstance(g, int) else slice(4 * g, 4 * g + 4)
                    tts(oh1[:, b], iota.unsqueeze(1).broadcast_to([P, 4, P]),
                        sel[:, 0, cols].unsqueeze(2).broadcast_to([P, 4, P]), ALU.is_equal)
                    for q in range(4):
                        col = lambda w: sel[:, w, bass.ds(g * 4 + q, 1)] if not isinstance(g, int) \
                            else sel[:, w, 4 * g + q:4 * g + q + 1]
                        ins = ts(oh2[:, b, q, :], iota, col(1), col(2), ALU.is_equal, ALU.mult)
                    ins.then_inc(hot, 1)

                def gate(g, b):
                    view = act_all[:, :, bass.ds(g * 4, 4)] if not isinstance(g, int) else act_all[:, :, 4 * g:4 * g + 4]
                    view = view.rearrange("p e t -> p t e")
                    return tts(view, ps[:, b, :].rearrange("p (t e) -> p t e", t=4), view, ALU.mult).then_inc(gated, 1)

                dve.wait_ge(sel_ready, TT * (l + 1))
                dve.wait_ge(taken, TAKEN[f"u{l}"] + KEYS)
                n = T // 4
                hots(0, 0)
                with seen.loop(n // 2 - 1, {gates_t: 2}) as i:
                    hots(i * 2 + 1, 1)
                    seen(gates_t)
                    gate(i * 2, 0)
                    hots(i * 2 + 2, 0)
                    seen(gates_t)
                    gate(i * 2 + 1, 1)
                hots(n - 1, 1)
                seen(gates_t)
                gate(n - 2, 0)
                seen(gates_t)
                gate(n - 1, 1)

            def experts_out(l):
                name = f"v{l}"
                first = SEGS[name][0]
                g2 = mods[:, l % 2, 40:48]

                def lower_gated(k, j):
                    dve.wait_ge(wah, k + (1 + KEYS * l))
                    tts(wa_lo[:, j % 4:j % 4 + 1, :], act_all[:, at(k), :], wa_hi[:, j % 4:j % 4 + 1, :].bitcast(F32),
                        ALU.subtract).then_inc(wal, 1)

                def step(n, j, k, i):
                    lower(n, j, name)
                    lower_gated(k + 1, j + 1)
                lower_gated(0, first)
                tiles_in_loops(dve, first, KEYS - 1, step)
                lower(first + KEYS - 1, first + KEYS - 1, name)
                dve.wait_ge(tile_used, first + KEYS)
                for tt in range(TT):
                    for half in range(2):
                        ins = cp(sum_sb[:, tt, half * 512:(half + 1) * 512], ps[:, 2 + 2 * tt + half, :])
                ins.then_inc(moe_out, 1)
                for m in range(4):
                    seen(moe_t)
                    for c in range(2):
                        ins = stt(x[:, 2 * m + c, :], ps[:, [6, 7, 0, 1][m], c * T:(c + 1) * T], g2[:, 2 * m + c:2 * m + c + 1],
                                  x[:, 2 * m + c, :], ALU.mult, ALU.add)
                if l in (1, 3):
                    link(ins)
                return ins

            dve.wait_ge(par_in, 32)
            modulation(0)
            for l in range(4):
                if l == 0:
                    dve.wait_ge(x_in, 16)
                if l == 3:
                    norm(pcol("kv_g"), mod_kv[:, 8:16])
                    attention()
                else:
                    norm(pcol(f"mix_g{l}"), mods[:, l % 2, 8:16])
                    if l < 2:
                        rwkv(l)
                    else:
                        lru()
                add_products(("out0", "out1", "lout", "wo")[l], mods[:, l % 2, 16:24])
                norm(pcol(f"ffn_g{l}"), mods[:, l % 2, 32:40])
                lowers(f"q{l}")
                choose(l)
                gates(l)
                if l < 3:
                    modulation(l + 1)
                ins = experts_out(l)
                if l == 1 or l == 3:
                    link(norm_x())
                    g = pcol("lnf_g" if l == 1 else "final_g")
                    for c in range(DC):
                        dst = x if l == 1 else wide
                        ins = ts(dst[:, c, :], wide[:, c, :], g[:, c:c + 1], None, ALU.mult)
                link(ins, arena_free if l < 3 else fin)

        @block.tensor
        def _(pe):
            seen = Seen(pe, None)
            mm = pe.matmul

            def products(name, a=0, b=None):
                first, count = SEGS[name][:2]

                def step(n, j, k, i):
                    pe.wait_ge(lo_done, n + (1 - WHOLE[name]))
                    if not (TAKEN[name] == 0 and i is None and k < 2):
                        pe.wait_ge(taken, k + (TAKEN[name] - 1))
                    o = ps[:, j % 2, 0:T]
                    hi = t_hi[:, j % SPL, :].rearrange("p (c m) -> p c m", c=DC)
                    lo = t_lo[:, j % SPL, :].rearrange("p (c m) -> p c m", c=DC)
                    for c in range(DC):
                        mm(o, hi[:, c, :], h_hi[:, c, :], start=(c == 0), stop=False)
                        mm(o, hi[:, c, :], h_lo[:, c, :], start=False, stop=False)
                        ins = mm(o, lo[:, c, :], h_hi[:, c, :], start=False, stop=(c == DC - 1))
                    ins.then_inc(tile_used, 1)
                if TAKEN[name] == 0:
                    step(first, first, 0, None)
                    step(first + 1, first + 1, 1, None)
                    a = 2
                in_loops(pe, name, a, b or count, step)

            def modulate(l, n, j, kc, g, i):
                turn = (j // RAW + 1) if i is None else i * 2 + (j // RAW + 1)
                pe.wait_ge(loaded[j % RAW], turn * 16)
                if kc == 0 and not (isinstance(g, int) and g == 0):
                    turn_row(l, g - 1)
                for half in range(2):
                    ins = mm(ps[0:1, 6 + half, :], c_act[:, l // 2, kc:kc + 1],
                             raw[:, j % RAW, half * 512:(half + 1) * 512], start=(kc == 0), stop=(kc == DC - 1))
                ins.then_inc(tile_used, 1)

            def turn_row(l, g):
                pe.wait_ge(row_out, g + (ROWS[l] + 1))
                for m in range(8):
                    o = ps[:, 5, 8 * g + m:8 * g + m + 1] if isinstance(g, int) else ps[:, 5, bass.ds(g * 8 + m, 1)]
                    ins = mm(o, mod_row[0:1, m * P:(m + 1) * P], ones[0:1, 0:1], start=True, stop=True)
                ins.then_inc(row_turned, 1)

            def sum_squares(src, n):
                seen(squares)
                for c in range(n):
                    ins = mm(ps[:, 2, 0:T], ones, src[:, c, :], start=(c == 0), stop=(c == n - 1))
                ins.then_inc(sumsq, 1)

            def head_sum(src, bank, wait=True):
                if wait:
                    seen(hsum_in)
                for b in range(2):
                    ins = mm(ps[:, bank + b, :], head_ones, src[:, 2 * b:2 * b + 2, :].rearrange("p g t -> p (g t)"),
                             start=True, stop=True)
                ins.then_inc(hsum, 1)

            def rwkv(l):
                rw, lw = rk["rw"], rk["lora"]
                products(f"in{l}")
                pe.wait_ge(small_in, SMALL[f"mix{l}"])
                seen(lora_in, 2)
                for m in range(8):
                    mm(ps[:, 2 + m // 2, (m % 2) * T:(m % 2 + 1) * T], lw[:, m, :], rw[:, 12, :], start=True, stop=True)
                for m in range(4):
                    ins = mm(ps[:, 6 + m // 2, (m % 2) * T:(m % 2 + 1) * T], lw[:, 8 + m, :], rw[:, 13, :],
                             start=True, stop=True)
                if l:
                    pe.wait_ge(taken, TAKEN["in1"] + 19)
                    for m in range(4):
                        ins = mm(ps[:, m // 2, (m % 2) * T:(m % 2 + 1) * T], lw[:, 12 + m, :], rw[:, 14, :],
                                 start=True, stop=True)
                ins.then_inc(lora_mm, 1)
                head_sum(rk["d1"], 2)
                head_sum(rk["tmp"], 4)
                c_ = chunk_at
                out4 = lambda b, g: ps[:, b, g * P:(g + 1) * P]
                with seen.loop(NCH, {blocks_in: 1, blk_out: CHUNK_OUTS}) as c:
                    def four(bank, *terms):
                        for g in range(G4):
                            for n, (lhs, rhs) in enumerate(terms):
                                lhs_ = lhs[:, g, :] if not lhs is ident else ident
                                ins = mm(out4(bank, g), lhs_, rhs[:, g, :], start=(n == 0), stop=(n == len(terms) - 1))
                        ins.then_inc(pe_blk, 1)

                    def turn(bank, src):
                        for g in range(G4):
                            ins = pe.transpose(out4(bank, g), src[:, g, :], ident)
                        ins.then_inc(pe_blk, 1)

                    A, B, K, R = c_["Abd"], c_["Bbd"], c_["Kbd"], c_["Rbd"]
                    seen(blocks_in)
                    four(2, (B, A))
                    four(3, (A, B))
                    four(4, (K, A))
                    four(5, (B, R))
                    four(6, (K, R))
                    turn(7, A)
                    seen(blk_out)
                    turn(2, B)
                    seen(blk_out)
                    turn(3, K)
                    seen(blk_out)
                    turn(4, c_["Vbd"])
                    seen(blk_out, 7)
                    for lev in range(5):
                        cur = lev % 2
                        four(5, (c_["LT"], c_[f"X{cur}"]))
                        seen(blk_out)
                        four(6, (c_[f"XT{cur}"], c_["Z"]))
                        four(7, (c_["Z"], c_[f"XT{cur}"]))
                        seen(blk_out, 2)
                    XT = c_["XT1"]
                    four(2, (c_["L2T"], c_["Vt"]))
                    four(3, (XT, c_["At"]))
                    seen(blk_out)
                    four(4, (XT, c_["Gm"]))
                    seen(blk_out)
                    four(5, (c_["XA"], c_["T1T"]))
                    four(6, (c_["XA"], c_["Bt"]))
                    seen(blk_out, 3)
                    S = c_["S0"]
                    four(7, (c_["U0"], c_["T1T"]), (c_["Vt"], c_["T2T"]), (S, c_["RpT"]))
                    four(2, (c_["Bt"], c_["U0"]), (c_["Kt"], c_["Vt"]), (c_["Q"], S), (ident, S))
                    seen(blk_out, 2)
                head_sum(rk["y"], 2, wait=False)
                head_sum(rk["tmp"], 4)
                seen(hsum_in)
                pe.wait_ge(pool_ready, l + 1)
                for g in range(G4):
                    src = rk["pb"] if g % 2 == 0 else rk["pa"]
                    ins = mm(ps[:, 6 + g // 2, (g % 2) * T:(g % 2 + 1) * T], lw[:, 16 + g, :], src[:, g, 16:],
                             start=True, stop=True)
                ins.then_inc(pool_mm, 1)

            def lru():
                products("lgate")
                products("lrec")
                pe.wait_ge(small_in, SMALL["mix2"])
                seen(xc_ready)
                pe.wait_ge(taken, TAKEN["lrec"] + 8)
                for gate in range(2):
                    for h in range(4):
                        for jt in range(2):
                            c = 2 * h + jt
                            for ic in range(2):
                                ins = mm(ps[:, 4 * gate + c // 2, (c % 2) * T:(c % 2 + 1) * T],
                                         lr["wts"][:, ((gate * 4 + h) * 2 + ic) * 2 + jt, :], lr["xc"][:, 2 * h + ic, :],
                                         start=(ic == 0), stop=(ic == 1))
                ins.then_inc(gates_mm, 1)

            def attention():
                products("dkv")
                sum_squares(wide, DC)
                seen(h_split)
                products("dq")
                sum_squares(ml["sq"], 2)
                sum_squares(ml["sq"], 3)
                pe.wait_ge(small_in, SMALL["mix3"])
                seen(lat_in)
                pe.wait_ge(taken, TAKEN["dq"] + 3)
                jobs = [(ml["uk"], 2, ml["ck"], m) for m in range(8)] + [(ml["uq"], 3, ml["cq"], m) for m in range(16)]
                for n in range(0, len(jobs), 2):
                    bank = (n // 2) % 8
                    if n // 2 >= 8:
                        seen(kv_out)
                    for half in range(2):
                        w, kc, rhs, m = jobs[n + half]
                        for c in range(kc):
                            ins = mm(ps[:, bank, half * T:(half + 1) * T], w[:, m * kc + c, :], rhs[:, c, :],
                                     start=(c == 0), stop=(c == kc - 1))
                    ins.then_inc(kv_mm, 1)
                for kt in range(TT):
                    for half in range(2):
                        seen(kv_out)
                        for c in range(2):
                            ins = mm(ps[:, 4 + 2 * kt + half, :], ml["ck"][:, c, kt * P:(kt + 1) * P],
                                     ml["uv"][:, c, half * 512:(half + 1) * 512], start=(c == 0), stop=(c == 1))
                        ins.then_inc(kv_mm, 1)
                seen(kv_out, 8)
                seen(lat_in)
                for h in range(AH):
                    a, r = 64 * (h % 2), 32 * (h % 4)
                    for q in range(TT):
                        o = ps[:, 2 + h % 2, q * T:(q + 1) * T]
                        mm(o, ml["qn"][a:a + 64, h // 2, q * P:(q + 1) * P], ml["kn"][a:a + 64, h // 2, :],
                           start=True, stop=False)
                        ins = mm(o, ml["qr"][r:r + 32, h // 4, q * P:(q + 1) * P], ml["kr"][r:r + 32, :],
                                 start=False, stop=True)
                    ins.then_inc(sc_mm, 1)
                    seen(p_ready)
                    for kt in range(TT):
                        for q in range(TT):
                            ins = pe.transpose(ps[:, 4 + h % 2, kt * T + q * P:kt * T + (q + 1) * P],
                                               ml["p"][:, q, kt * P:(kt + 1) * P], ident)
                    ins.then_inc(pt_mm, 1)
                    seen(pt_out)
                    if h % 2 == 0 and h:
                        seen(av_out)
                    for kt in range(TT):
                        ins = mm(ps[:, 6, 0:T], ml["vpad"][:, kt, h, :], ml["pT"][:, kt, :],
                                 start=(h % 2 == 0 and kt == 0), stop=(h % 2 == 1 and kt == 1))
                    if h % 2:
                        ins.then_inc(av_mm, 1)

            def peer(l):
                products(f"q{l}")
                pe.wait_ge(keys_in, 16 * (l + 1))
                pe.wait_ge(taken, TAKEN[f"q{l}"] + 16)
                for tt in range(TT):
                    for b in range(4):
                        if tt:
                            seen(score_out)
                        for k in range(4):
                            hp = 4 * b + k
                            ins = mm(ps[:, 2 + b, k * P:(k + 1) * P], tk["q"][:, hp, tt * P:(tt + 1) * P],
                                     tk["keys"][:, hp, :], start=True, stop=True)
                        ins.then_inc(score_mm, 1)
                seen(score_out, 4)
                a = 0
                for tt in range(TT):
                    b = STEPS * tt + CHOSEN + 2
                    products(f"u{l}", a, b)
                    a = b
                    seen(chosen)
                    for w in range(3):
                        ins = pe.transpose(ps[:, 6 + tt, w * P:(w + 1) * P], tk["e"][:, w].rearrange("p h k -> p (h k)"), ident)
                    ins.then_inc(chosen_t, 1)
                products(f"u{l}", a)
                pe.wait_ge(taken, TAKEN[f"u{l}"] + KEYS)
                turns = T // 32
                ada, tiles = SEGS[f"ada{l + 1}"][:2] if l < 3 else (0, 0)

                def gate(b):
                    for q in range(4):
                        ins = mm(ps[:, b, q * P:(q + 1) * P], oh1[:, b, q, :], oh2[:, b, q, :], start=True, stop=True)
                    ins.then_inc(gates_t, 1)

                for q in range(8):
                    seen(hot)
                    if q >= 2:
                        seen(gated)
                    gate(q % 2)
                    if tiles:
                        modulate(l + 1, ada + q, ada + q, q, 0, None)
                with_tiles = tiles // 8 - 1 if tiles else 0
                for n, some in ((with_tiles, True), (turns - 1 - with_tiles, False)):
                    if n == 0:
                        continue
                    with seen.loop(n, {hot: 8, gated: 8}) as i:
                        for q in range(8):
                            seen(hot)
                            seen(gated)
                            gate(q % 2)
                            if some:
                                modulate(l + 1, ada + 8 + q + i * 8, ada + 8 + q, q, i + 1, i)
                seen(gated, 2)
                if tiles:
                    turn_row(l + 1, tiles // 8 - 1)
                    pe.wait_ge(mod_ready, l + 2)
                first = SEGS[f"v{l}"][0]

                def step(n, j, k, i):
                    pe.wait_ge(lo_done, n + (1 - WHOLE[f"v{l}"]))
                    pe.wait_ge(wal, k + (1 + KEYS * l))
                    b = j % 4
                    one, last = (i is None and k == 0), (i is None and k == KEYS - 1)
                    for tt in range(TT):
                        up = wa_hi[:, b, tt * P:(tt + 1) * P]
                        down = wa_lo[:, b, tt * P:(tt + 1) * P]
                        for half in range(2):
                            cols = slice(half * 512, (half + 1) * 512)
                            o = ps[:, 2 + 2 * tt + half, :]
                            mm(o, up, t_hi[:, j % SPL, cols], start=one, stop=False)
                            mm(o, up, t_lo[:, j % SPL, cols], start=False, stop=False)
                            ins = mm(o, down, t_hi[:, j % SPL, cols], start=False, stop=last)
                    ins.then_inc(tile_used, 1)
                step(first, first, 0, None)
                tiles_in_loops(pe, first + 1, KEYS - 1, lambda n, j, k, i: step(n, j, k + 1, i))
                seen(moe_out)
                for m in range(4):
                    for c in range(2):
                        for tt in range(TT):
                            ins = pe.transpose(ps[:, [6, 7, 0, 1][m], c * T + tt * P:c * T + (tt + 1) * P],
                                               sum_sb[:, tt, (2 * m + c) * P:(2 * m + c + 1) * P], ident)
                    ins.then_inc(moe_t, 1)

            pe.wait_ge(par_in, 32)
            seen(c_ready, 2)
            for k in range(8):
                modulate(0, k, k, k, 0, None)
            with pe.Fori(0, 5) as i:
                for k in range(8):
                    modulate(0, 8 + k + i * 8, 8 + k, k, i + 1, i)
            turn_row(0, 5)
            for l in range(4):
                sum_squares(wide, DC)
                seen(h_split)
                if l < 2:
                    rwkv(l)
                elif l == 2:
                    lru()
                else:
                    attention()
                seen(h_split)
                products(("out0", "out1", "lout", "wo")[l])
                sum_squares(wide, DC)
                seen(h_split)
                peer(l)
                if l % 2:
                    sum_squares(wide, DC)


def _by_chunk(a, n):
    a = np.asarray(a)
    return np.moveaxis(a.reshape(*a.shape[:-1], n, P), -1, 0)


def _tiles(w, pad=0):
    w = np.asarray(w)
    if pad:
        w = np.concatenate([w, np.zeros((w.shape[0], pad), w.dtype)], axis=1)
    m = w.shape[1] // P
    return w.reshape(DC, P, m, P).transpose(2, 1, 0, 3).reshape(m, P, D)


def _row_tiles(w):
    w = np.asarray(w)
    m = w.shape[1] // D
    return w.reshape(DC, P, m, D).transpose(2, 0, 1, 3).reshape(m * DC, P, D)


def _constants():
    i = np.arange(P)
    row, col = i[:, None], i[None, :]
    same = row // 64 == col // 64
    out = [row == col, np.ones((P, P)), same, np.broadcast_to(col, (P, P)),
           same & (row < col), same & (row > col), same & (row <= col),
           (row // 2 == col // 2) & (row < col), (row // 2 == col // 2) & (row > col)]
    for n in (2, 4, 8, 16, 32):
        out.append((row // (2 * n) == col // (2 * n)) & (row // n > col // n))
    return np.stack([np.asarray(m, np.float32) for m in out], axis=1)


def _layout(i):
    f = np.float32
    par = np.zeros((P, NPAR), f)

    def put(name, v):
        a, n = PCOLS[name]
        par[:, a:a + n] = np.asarray(v).reshape(P, n)

    put("c0", _by_chunk(i["c"], 8))
    put("c1", _by_chunk(i["c_2"], 8))
    for l in range(4):
        b = l // 2
        put(f"ada_b{l}", _by_chunk(i["ada_b_2" if b else "ada_b"][l % 2], 48))
        put(f"mix_g{l}", _by_chunk(i["norm_mix_g_2" if b else "ln1_g"][l % 2], 8))
        put(f"ffn_g{l}", _by_chunk(i["norm_ffn_g_2" if b else "ln2_g"][l % 2], 8))
    for l in range(2):
        mu = np.zeros((15 * P,), f)
        mu[:14 * P] = i["mu_shift"][l]
        if l:
            mu[14 * P:14 * P + 32] = i["vres_mu"][0]
        put(f"mu{l}", _by_chunk(mu, 15))
        for n in ("w0", "a0", "k_k", "k_a", "lnx_g", "lnx_b", "pool_scale"):
            put(f"{n}{l}", _by_chunk(i[n][l], 4))
        put(f"r_k{l}", _by_chunk(np.asarray(i["r_k"][l]).reshape(-1), 4))
    put("vres_v0", _by_chunk(i["vres_v0"][0], 4))
    put("lnf_g", _by_chunk(i["lnf_g"], 8))
    put("conv_w", _by_chunk(i["lru_conv_w_2"][0], 8))
    for n, src in (("conv_b", "lru_conv_b_2"), ("ba", "lru_ba_2"), ("bx", "lru_bx_2"), ("lam", "lru_lambda_2")):
        put(n, _by_chunk(i[src][0], 8))
    put("kv_g", _by_chunk(i["kv_norm_g_2"], 8))
    put("final_g", _by_chunk(i["final_g_2"], 8))
    put("kv_ada_b", _by_chunk(i["kv_ada_b_2"], 16))
    put("ckv_g", _by_chunk(i["mla_kv_latent_g_2"], 2))
    put("cq_g", _by_chunk(i["mla_q_latent_g_2"][0], 3))
    freq = np.float32(10000.0) ** (-np.arange(16, dtype=f) / np.float32(16))
    put("freq", freq[np.arange(P) % 16])
    put("sign", np.where(np.arange(P) % 32 < 16, -1.0, 1.0).astype(f))

    swap = np.r_[16:32, 0:16]
    kr = np.asarray(i["mla_w_kr_2"])
    w = []
    for l in range(4):
        if l == 0:
            w.append(_row_tiles(i["ada_w"][0]))
        if l == 0:
            w += [_tiles(i["w_in"][0]), _tiles(i["w_out"][0])]
        elif l == 1:
            w += [_tiles(i["w_in"][1]), _tiles(i["vres_down"][0], pad=96), _tiles(i["w_out"][1])]
        elif l == 2:
            w += [_tiles(i["lru_w_in_2"][0]), _tiles(i["lru_w_out_2"][0])]
        else:
            w += [_tiles(i["mla_w_dkv_2"]), _tiles(np.tile(kr, (1, 4))),
                  _tiles(np.tile(kr[:, swap], (1, 4))), _tiles(i["mla_w_dq_2"][0]), _tiles(i["mla_w_o_2"][0])]
        w.append(_tiles(i["peer_w_q_2" if l > 1 else "peer_q"][l % 2]))
        if l < 3:
            w.append(_row_tiles(i["ada_w_2" if l > 0 else "ada_w"][(l + 1) % 2]))
        if l == 2:
            w.append(_row_tiles(i["kv_ada_w_2"]))
    w = np.concatenate(w)

    u = np.concatenate([np.asarray(i[n][l]).reshape(KEYS, KEYS, DC, P).transpose(1, 3, 2, 0).reshape(KEYS, P, D)
                        for n in ("peer_u", "peer_u_2") for l in range(2)])
    v = np.concatenate([np.asarray(i[n]).reshape(2, KEYS, KEYS, D) for n in ("peer_v", "peer_v_2")])

    lora = np.zeros((2, P, 20, P), f)
    for l in range(2):
        lora[l, :64, 0:4] = np.asarray(i["w_up"][l]).reshape(64, 4, P)
        lora[l, 64:, 4:8] = np.asarray(i["a_up"][l]).reshape(64, 4, P)
        lora[l, :, 8:12] = np.asarray(i["g_up"][l]).reshape(P, 4, P)
        if l:
            lora[l, :32, 12:16] = np.asarray(i["vres_up"][0]).reshape(32, 4, P)
        lora[l, :, 16:20] = np.asarray(i["pool_w"][l]).transpose(1, 0, 2)

    lru = np.stack([np.asarray(i[n][0]).reshape(4, 2, P, 2, P) for n in ("lru_wa_2", "lru_wx_2")])
    lru = lru.transpose(3, 0, 1, 2, 4, 5).reshape(P, 32, P)

    uq = np.asarray(i["mla_w_uq_2"][0]).reshape(3, P, AH, 96)
    rope = uq[..., 64:]
    parts = [uq[..., :64].reshape(3, P, 8, P), rope.reshape(3, P, 4, P), rope[..., swap].reshape(3, P, 4, P)]
    uq = np.concatenate(parts, axis=2).transpose(1, 2, 0, 3).reshape(P, 48, P)
    uk = np.asarray(i["mla_w_uk_2"]).reshape(2, P, 8, P).transpose(1, 2, 0, 3).reshape(P, 16, P)
    mla = np.concatenate([uq, uk], axis=1)
    uv = np.asarray(i["mla_w_uv_2"]).reshape(2, P, D).transpose(1, 0, 2)

    keys = np.concatenate([np.asarray(i[n]) for n in ("peer_keys", "peer_sub_keys_2")])
    keys = keys.reshape(4, 16, KEYS, P).transpose(0, 3, 1, 2)

    pos = np.arange(1, T + 1, dtype=f)
    inv = np.stack([1.0 / np.minimum(pos, f(win)) for win in WINDOWS]).astype(f)
    inv = np.broadcast_to(inv, (P, 4, T))
    xt = _by_chunk(i["x"][0], 8).transpose(0, 2, 1)
    return {"x_in": xt, "w_tiles": w, "u_tiles": u, "v_tiles": v, "params": par, "consts": _constants(),
            "lora": lora, "lru_w": lru, "mla_w": mla, "mla_uv": uv, "keys_t": keys, "pool_inv": inv,
            "positions": np.asarray(i["positions_2"])}


def kernel(**inputs):
    import concourse.bacc as bacc
    from concourse.bass_utils import run_bass_kernel_spmd as run

    arrays = {n: np.ascontiguousarray(a) for n, a in _layout({n: np.asarray(a) for n, a in inputs.items()}).items()}
    nc = bacc.Bacc("TRN2", target_bir_lowering=False, num_devices=1)
    args = [nc.dram_tensor(n, a.shape, mybir.dt.from_np(a.dtype), kind="ExternalInput").ap() for n, a in arrays.items()]
    out = nc.dram_tensor("out_xt", (P, DC, T), F32, kind="ExternalOutput").ap()
    build(nc, *args, out)
    r = run(nc, [arrays], core_ids=[0])
    got = np.asarray(r.results[0]["out_xt"])
    return np.ascontiguousarray(got.transpose(2, 1, 0)).reshape(1, T, D)
```

```python
from contextlib import ExitStack, contextmanager

import numpy as np

import concourse.bass as bass
from concourse import mybir

F32 = mybir.dt.float32
F32R = mybir.dt.float32r
U32 = mybir.dt.uint32
I32 = mybir.dt.int32
ALU = mybir.AluOpType
ACT = mybir.ActivationFunctionType
AX = mybir.AxisListType

P = 128
T = 256
D = 1024
DC = D // P
TT = T // P
RW = 512
G4 = RW // P
CH = 64
NCH = T // CH
HEADS = 8
TOPK = 16
KEYS = 128
EXPERTS = KEYS * KEYS
GN_EPS = 64e-5
EPS = 1e-6
DECAY = float(np.exp(-0.5))
WINDOWS = (2, 4, 8, 16)
AH = 16
ATT_SCALE = 1.0 / float(np.sqrt(96.0))
NEG = -1e30
LOWEST = -3.0e38

RAW = 4
SPL = 2

PCOLS = {}


def _cols(name, n):
    PCOLS[name] = (sum(k for _, k in PCOLS.values()), n)


_cols("c0", 8)
_cols("c1", 8)
for _l in range(4):
    _cols(f"ada_b{_l}", 48)
    _cols(f"mix_g{_l}", 8)
    _cols(f"ffn_g{_l}", 8)
for _l in range(2):
    _cols(f"mu{_l}", 15)
    for _n in ("w0", "a0", "k_k", "k_a", "r_k", "lnx_g", "lnx_b", "pool_scale"):
        _cols(f"{_n}{_l}", 4)
_cols("vres_v0", 4)
_cols("lnf_g", 8)
_cols("conv_w", 32)
for _n in ("conv_b", "ba", "bx", "lam", "kv_g", "final_g"):
    _cols(_n, 8)
_cols("kv_ada_b", 16)
_cols("ckv_g", 2)
_cols("cq_g", 3)
_cols("freq", 1)
_cols("sign", 1)
NPAR = sum(k for _, k in PCOLS.values())

SEGS = {}


def _plan():
    n = w = 0
    for l in range(4):
        mix = [[("in0", 18), ("out0", 8)], [("in1", 19), ("out1", 8)],
               [("lgate", 8), ("lrec", 8), ("lout", 8)],
               [("dkv", 4), ("dq", 3), ("wo", 8)]][l]
        for name, count in [("ada0", 48)] * (l == 0) + mix + [(f"q{l}", 16)]:
            SEGS[name] = (n, count, "w", w)
            n, w = n + count, w + count
        SEGS[f"u{l}"] = (n, KEYS, "u", l)
        n += KEYS
        if l < 3:
            count = 48 + 16 * (l == 2)
            SEGS[f"ada{l + 1}"] = (n, count, "w", w)
            n, w = n + count, w + count
        SEGS[f"v{l}"] = (n, KEYS, "v", l)
        n += KEYS
    return w


NW = _plan()
TAKEN = {}
WHOLE = {}
_e = _w = 0
for _name in SEGS:
    TAKEN[_name], WHOLE[_name] = _e, _w
    if _name.startswith("ada"):
        _w += SEGS[_name][1]
    elif _name[0] != "v":
        _e += SEGS[_name][1]
RANK_KEYS, PAIRS, RANK_PAIRS, SOFT, LOOK_UP, CHOSEN = 0, 16, 18, 34, 35, 47
STEPS = 48
ROWS = [0, 6, 12, 18]

SMALL = {"mix0": 48, "mix1": 96, "mix2": 112, "mix3": 192}
HSPLIT = {"ffn0": 3, "ffn1": 6, "ffn2": 9, "ffn3": 13}
STEPS2 = 60
OUTS2 = 40
COPIES2 = 16
BLOCKS2 = 10
MASKS = 10


def in_loops(eng, name, a, b, body):
    tiles_in_loops(eng, SEGS[name][0] + a, b - a, lambda n, j, k, i: body(n, j, k + a, i))


def tiles_in_loops(eng, first, count, body):
    k = 0
    while k < count and first + k < RAW:
        body(first + k, first + k, k, None)
        k += 1
    turns = (count - k) // 4
    if turns >= 2:
        with eng.Fori(0, turns) as i:
            for j in range(4):
                body(first + k + j + i * 4, first + k + j, k + j + i * 4, i)
        k += 4 * turns
    while k < count:
        body(first + k, first + k, k, None)
        k += 1


class Seen:

    def __init__(self, eng, chain):
        self.eng, self.chain_sem, self.base, self.here = eng, chain, {}, None

    def __call__(self, sem, k=1):
        if self.here is None:
            self.base[sem.name] = self.base.get(sem.name, 0) + k
            self.eng.wait_ge(sem, self.base[sem.name])
        else:
            i, per, got = self.here
            got[sem.name] = got.get(sem.name, 0) + k
            at = self.base.get(sem.name, 0) + got[sem.name]
            self.eng.wait_ge(sem, at if i is None else i * per[sem.name] + at)

    def skip(self, sem, k):
        if self.here is None:
            self.base[sem.name] = self.base.get(sem.name, 0) + k
        else:
            self.here[2][sem.name] = self.here[2].get(sem.name, 0) + k

    def link(self, ins, sem=None):
        sem = sem or self.chain_sem
        ins.then_inc(sem, 1)
        self(sem)

    @contextmanager
    def loop(self, turns, per):
        per = {s.name: k for s, k in per.items()}
        with self.eng.Fori(0, turns) as i:
            self.here = (i, per, {})
            yield i
            got = self.here[2]
        assert got == per, (got, per)
        self.here = None
        for s, k in per.items():
            self.base[s] = self.base.get(s, 0) + turns * k


def build(nc, x_in_dram, w_tiles, u_tiles, v_tiles, params, consts, lora, lru_w, mla_w, mla_uv, keys_t, pool_inv,
          positions, out):
    with ExitStack() as ctx:
        def sb(name, shape, dt=F32):
            return ctx.enter_context(nc.sbuf_tensor(name, shape, dt))

        def sem(name):
            return ctx.enter_context(nc.semaphore(name))

        arena = sb("arena", [P, KEYS * T])
        raw = sb("raw", [P, RAW, D])
        t_hi = sb("t_hi", [P, SPL, D], F32R)
        t_lo = sb("t_lo", [P, SPL, D], F32R)
        x = sb("x", [P, DC, T])
        h_hi = sb("h_hi", [P, DC, T], F32R)
        h_lo = sb("h_lo", [P, DC, T], F32R)
        par = sb("par", [P, NPAR])
        cst = sb("cst", [P, 4, P])
        mods = sb("mods", [P, 2, 48])
        mod_kv = sb("mod_kv", [P, 16])
        gain = sb("gain", [P, DC])
        c_act = sb("c_act", [P, 2, DC])
        mod_row = sb("mod_row", [1, D])
        v_first = sb("v_first", [P, G4, T])
        sel = sb("sel", [P, 3, T])
        ps = ctx.enter_context(nc.psum_tensor("ps", [P, 8, 512], F32))

        ident, ones, head_ones, iota = (cst[:, k, :] for k in range(4))

        def pcol(name):
            a, n = PCOLS[name]
            return par[:, a:a + n]

        def carve(spec):
            at, got = 0, {}
            for name, shape in spec:
                size = int(np.prod(shape))
                v = arena[:, at:at + size]
                if len(shape) > 1:
                    names = " ".join(f"a{k}" for k in range(len(shape)))
                    v = v.rearrange(f"p ({names}) -> p {names}", **{f"a{k}": s for k, s in enumerate(shape)})
                got[name] = v
                at += size
            assert at <= KEYS * T, at
            return got

        act_all = arena[:, :].rearrange("p (e t) -> p e t", t=T)
        quad = (G4, T)
        rk = carve([("A", quad), ("B", quad), ("z", (19, T + 1)), ("rw", (15, T)), ("dec", quad), ("d1", quad),
                    ("Pinv", quad), ("Pprev", quad), ("kk", quad), ("kp", quad), ("tmp", quad), ("Pc", quad),
                    ("a", quad), ("gate", quad), ("K", quad), ("R", quad), ("bonus", quad), ("y", quad),
                    ("lora", (20, P)), ("masks", (MASKS, P)), ("pa", (4, T + 16)), ("pb", (4, T + 16)),
                    ("inv", quad)])
        wide = carve([("w", (DC, T))])["w"]
        chunk_at = [{}, {}]
        at_rw = 2048 + 19 * (T + 1)
        at_dec = at_rw + 15 * T
        at_lora = at_dec + 14 * G4 * T
        free = [(2048, 9), (at_rw, 4), (at_rw + 12 * T, 1), (at_dec, 14), (at_dec + 8 * G4 * T, 2), (at_lora, 4)]
        free = [a + 512 * k for a, n in free for k in range(n)]
        four_blocks = [arena[:, a:a + 512].rearrange("p (g k) -> p g k", g=4) for a in free]
        lr = carve([("w", (DC, T)), ("gate", (DC, T)), ("rp", (DC, T + 3)), ("xc", (DC, T)), ("rg", (DC, T)),
                    ("ig", (DC, T)), ("la", (DC, T)), ("a", (DC, T)), ("tau", (DC, T)), ("hs", (DC, T)),
                    ("wts", (32, P)), ("sp", (4, DC))])
        ml = carve([("w", (DC, T)), ("ck", (2, T)), ("krz", (2, T)), ("cq", (3, T)), ("uq", (48, P)),
                    ("uk", (16, P)), ("uv", (2, D)), ("kn", (DC, T)), ("kr", (T,)), ("qn", (DC, T)),
                    ("qr", (4, T)), ("qs", (4, T)), ("cos", (T,)), ("sin", (T,)), ("ang", (T,)), ("tmp", (4, T)),
                    ("vpad", (TT, AH, P)), ("mask", (TT, T)), ("mbias", (TT, T)), ("s", (2, TT, T)),
                    ("p", (2, TT, T)), ("pT", (2, TT, T)), ("posi", (T,)), ("posf", (T,)), ("posq", (TT,)),
                    ("posqi", (TT,)), ("st", (2, 8)), ("sq", (3, T)), ("rinv", (T,))])
        def ml_at(name):
            return {"uq": DC * T + 7 * T}[name]

        choice = [("s2", (P,)), ("cand", (HEADS, 256)), ("c2", (256,)), ("eq", (HEADS // 2, TOPK, TOPK)),
                  ("val", (16, TOPK)), ("idx", (16, TOPK)), ("idf", (16, TOPK)), ("cs", (HEADS, TOPK)),
                  ("ci", (HEADS, TOPK)), ("hat", (2, HEADS, TOPK)), ("hatu", (2, HEADS, TOPK)),
                  ("e", (3, HEADS, TOPK)), ("den", (2, HEADS))]
        TK_SLOT = KEYS - -(-sum(int(np.prod(shape)) for _, shape in choice) // T)
        SC_SLOT = TK_SLOT - TT * 16 * P // T
        assert SC_SLOT > STEPS + PAIRS + 2 and TK_SLOT > TT * STEPS + 6
        tk = carve([("w", (DC, T)), ("keys", (16, P)), ("q", (16, T)), ("gap", (SC_SLOT * T - 8192,)),
                    ("sc", (TT, 16, P)), *choice])
        sum_sb = carve([("w", (DC, T)), ("keys", (16, P)), ("sum", (TT, D))])["sum"]
        oh1 = sb("oh1", [P, 2, 4, P])
        ms_all = oh1[:, 0, 0:2, :].rearrange("p a k -> p (a k)")
        rinv_all = oh1[:, 0, 2:4, :].rearrange("p a k -> p (a k)")
        oh2 = sb("oh2", [P, 2, 4, P])
        four_blocks += [oh1[:, 0], oh1[:, 1], oh2[:, 0], oh2[:, 1]]
        for name in ("Abd", "Bbd", "Kbd", "Rbd", "Vbd", "LT", "L2T", "T1T", "T2T", "At", "Bt", "Kt", "Vt",
                     "X0", "X1", "XT0", "XT1", "Z"):
            for c in chunk_at:
                c[name] = four_blocks.pop(0)
        for c in chunk_at:
            c.update(Gm=c["LT"], U0=c["Z"], XA=c["X0"], RpT=c["XT0"], Q=c["L2T"])
        states = [four_blocks.pop(0) for _ in range(2)]
        wa_hi, wa_lo = h_hi, h_lo

        def four_of(bank):
            return ps[:, bank, :].rearrange("p (g k) -> p g k", g=4)

        loaded = [sem(f"loaded{k}") for k in range(RAW)]
        hi_done = sem("hi_done")
        lo_done = sem("lo_done")
        tile_used = sem("tile_used")
        taken = sem("taken")
        par_in = sem("par_in")
        x_in = sem("x_in")
        small_in = sem("small_in")
        c_ready = sem("c_ready")
        row_out = sem("row_out")
        row_turned = sem("row_turned")
        mod_ready = sem("mod_ready")
        chains = {e: sem(f"chain_{e}") for e in ("act", "dve", "pool")}
        squares = sem("squares")
        sumsq = sem("sumsq")
        ms_ready = sem("ms_ready")
        root = sem("root")
        normed = sem("normed")
        h_up = sem("h_up")
        h_split = sem("h_split")
        arena_free = sem("arena_free")
        shifted = sem("shifted")
        lora_in = sem("lora_in")
        lora_mm = sem("lora_mm")
        lora_out = sem("lora_out")
        hsum_in = sem("hsum_in")
        hsum = sem("hsum")
        hroot = sem("hroot")
        blocks_in = sem("blocks_in")
        pe_blk = sem("pe_blk")
        blk_out = sem("blk_out")
        blk_copied = sem("blk_copied")
        state_out = sem("state_out")
        pool_ready = sem("pool_ready")
        pool_mm = sem("pool_mm")
        z_free = sem("z_free")
        mix_ready = sem("mix_ready")
        xc_ready = sem("xc_ready")
        gates_mm = sem("gates_mm")
        gates_out = sem("gates_out")
        la_ready = sem("la_ready")
        ea_ready = sem("ea_ready")
        beta_in = sem("beta_in")
        beta = sem("beta")
        sp_a = sem("sp_a")
        sp_b = sem("sp_b")
        ang_ready = sem("ang_ready")
        trig = sem("trig")
        lat_in = sem("lat_in")
        kv_mm = sem("kv_mm")
        kv_out = sem("kv_out")
        sc_mm = sem("sc_mm")
        sc_ready = sem("sc_ready")
        exp_done = sem("exp_done")
        p_ready = sem("p_ready")
        pt_mm = sem("pt_mm")
        pt_out = sem("pt_out")
        av_mm = sem("av_mm")
        av_out = sem("av_out")
        keys_in = sem("keys_in")
        score_mm = sem("score_mm")
        score_out = sem("score_out")
        sm_in = sem("sm_in")
        sm_exp = sem("sm_exp")
        chosen = sem("chosen")
        chosen_t = sem("chosen_t")
        sel_ready = sem("sel_ready")
        ranked = sem("ranked")
        hot = sem("hot")
        gates_t = sem("gates_t")
        gated = sem("gated")
        wah = sem("wah")
        wal = sem("wal")
        moe_out = sem("moe_out")
        moe_t = sem("moe_t")
        fin = sem("fin")
        out_done = sem("out_done")

        block = ctx.enter_context(nc.Block())

        @block.sync
        def _(sp):
            sp.dma_start(par[:, :], params).then_inc(par_in, 16)
            sp.dma_start(cst[:, :, :], consts[:, 0:4, :]).then_inc(par_in, 16)
            sp.dma_start(x[:, :, :], x_in_dram).then_inc(x_in, 16)
            for name, (first, count, source, s0) in SEGS.items():
                def load(n, j, k, i, name=name, source=source, s0=s0):
                    if j >= RAW:
                        last = name
                        if i is None and n - RAW < SEGS[name][0]:
                            last = [s for s in SEGS if SEGS[s][0] <= n - RAW][-1]
                        if last.startswith("ada"):
                            sp.wait_ge(tile_used, n - RAW + 1)
                        else:
                            sp.wait_ge(lo_done, n + (1 - RAW - WHOLE[last]))
                    slot = j % RAW
                    if source == "w":
                        src = w_tiles[bass.ds(s0 + k, 1)].rearrange("a p n -> p (a n)")
                    elif source == "u":
                        src = u_tiles[bass.ds(s0 * KEYS + k, 1)].rearrange("a p n -> p (a n)")
                    else:
                        src = v_tiles[s0, :, bass.ds(k, 1), :].rearrange("p a n -> p (a n)")
                    sp.dma_start(raw[:, slot, :], src).then_inc(loaded[slot], 16)
                for k in range(min(RAW, count)):
                    load(first + k, first + k, k, None)
                if count > RAW:
                    in_loops(sp, name, RAW, count, load)
            sp.wait_ge(fin, 1)
            sp.dma_start(out, wide).then_inc(out_done, 16)
            sp.wait_ge(out_done, 16)

        @block.gpsimd
        def _(pool):
            seen = Seen(pool, chains["pool"])

            def pooling(l):
                pool.wait_ge(small_in, SMALL[f"mix{l}"])
                seen(z_free)
                pa, pb, z = rk["pa"], rk["pb"], rk["z"]
                seen.link(pool.memset(pa[:, :, 0:16], 0.0))
                seen.link(pool.memset(pb[:, :, 0:16], 0.0))
                seen.link(pool.tensor_copy(pa[:, :, 16:], z[:, 14:18, 1:]))
                bufs = [pa, pb]
                for k, win in enumerate(WINDOWS):
                    src, dst, back = bufs[k % 2], bufs[(k + 1) % 2], win // 2
                    seen.link(pool.tensor_tensor(dst[:, k:, 16:], src[:, k:, 16:], src[:, k:, 16 - back:16 + T - back],
                                                 ALU.add))
                    seen.link(pool.tensor_tensor(dst[:, k, 16:], dst[:, k, 16:], rk["inv"][:, k, :], ALU.mult))
                    last = pool.tensor_tensor(dst[:, k, 16:], dst[:, k, 16:], z[:, 14 + k, 1:], ALU.subtract)
                    if k < len(WINDOWS) - 1:
                        seen.link(last)
                last.then_inc(pool_ready, 1)

            for l in range(4):
                if l:
                    seen(arena_free)
                if l < 2:
                    pool.dma_start(rk["lora"], lora[l]).then_inc(small_in, 16)
                    pool.dma_start(rk["masks"], consts[:, 4:4 + MASKS, :]).then_inc(small_in, 16)
                    pool.dma_start(rk["inv"], pool_inv).then_inc(small_in, 16)
                    pooling(l)
                elif l == 2:
                    pool.dma_start(lr["wts"], lru_w).then_inc(small_in, 16)
                else:
                    a = ml_at("uq")
                    pool.dma_start(arena[:, a:a + 64 * P].rearrange("p (m k) -> p m k", k=P), mla_w).then_inc(small_in, 16)
                    pool.dma_start(ml["uv"], mla_uv).then_inc(small_in, 16)
                    pool.dma_start(ml["posi"].bitcast(I32), positions[0:1, :].broadcast_to([P, T])).then_inc(small_in, 16)
                    for tt in range(TT):
                        pool.dma_start(ml["posqi"][:, tt:tt + 1].bitcast(I32),
                                       positions[0:1, tt * P:(tt + 1) * P].rearrange("a p -> p a")).then_inc(small_in, 16)
                pool.wait_ge(h_split, HSPLIT[f"ffn{l}"])
                pool.dma_start(tk["keys"], keys_t[l]).then_inc(keys_in, 16)

        @block.scalar
        def _(act):
            seen = Seen(act, chains["act"])

            def upper(n, j, i, name):
                turn = (j // RAW + 1) if i is None else i + (j // RAW + 1)
                act.wait_ge(loaded[j % RAW], turn * 16)
                if j >= SPL:
                    act.wait_ge(tile_used, n - SPL + 1)
                act.copy(t_hi[:, j % SPL, :], raw[:, j % RAW, :]).then_inc(hi_done, 1)

            def uppers(name):
                tiles_in_loops(act, *SEGS[name][:2], lambda n, j, k, i: upper(n, j, i, name))

            def project(name, take_out):
                first, count = SEGS[name][:2]
                upper(first, first, None, name)
                upper(first + 1, first + 1, None, name)

                def step(n, j, k, i):
                    upper(n, j, i, name)
                    take_out(k, j % 2).then_inc(taken, 1)
                tiles_in_loops(act, first + 2, count - 2, step)
                for k in (count - 2, count - 1):
                    act.wait_ge(tile_used, first + k + 1)
                    take_out(k, (first + k) % 2).then_inc(taken, 1)

            def at(k):
                return bass.ds(k, 1) if not isinstance(k, int) else slice(k, k + 1)

            def rows(l):
                first, count = SEGS[f"ada{l}"][:2]

                def take_out(g):
                    act.wait_ge(tile_used, first + 8 + g * 8)
                    if not (l == 0 and isinstance(g, int)):
                        act.wait_ge(row_turned, g + ROWS[l])
                    act.copy(mod_row[0:1, :], ps[0:1, 6:8, :].rearrange("p a k -> p (a k)")).then_inc(row_out, 1)
                take_out(0)
                with act.Fori(1, count // 8) as g:
                    take_out(g)

            def norm():
                seen(ms_ready)
                act.activation(rinv_all, ms_all, ACT.Sqrt).then_inc(root, 1)

            def modulate(shift):
                seen(normed)
                for c in range(DC):
                    ins = act.activation(wide[:, c, :], wide[:, c, :], ACT.Identity, bias=shift[:, c:c + 1],
                                         scale=gain[:, c:c + 1])
                seen.link(ins)
                ins = act.copy(h_hi[:, :, :], wide)
                ins.then_inc(h_up, 1)

            def split_upper(ready, k=1):
                seen(ready, k)
                act.copy(h_hi[:, :, :], wide).then_inc(h_up, 1)

            def rwkv(l):
                rw = rk["rw"]
                project(f"in{l}", lambda k, b: act.copy(rk["z"][:, at(k), 1:], ps[:, b:b + 1, 0:T]))
                seen(shifted)
                act.activation(rw[0:64, 12, :], rw[0:64, 12, :], ACT.Tanh).then_inc(lora_in, 1)
                act.activation(rw[:, 13, :], rw[:, 13, :], ACT.Sigmoid).then_inc(lora_in, 1)
                seen(lora_mm)
                for g in range(G4):
                    lo, hi = ps[:, 2 + g // 2, (g % 2) * T:(g % 2 + 1) * T], ps[:, 4 + g // 2, (g % 2) * T:(g % 2 + 1) * T]
                    d = act.activation(rk["dec"][:, g, :], lo, ACT.Sigmoid, bias=pcol(f"w0{l}")[:, g:g + 1])
                    act.activation(rk["a"][:, g, :], hi, ACT.Sigmoid, bias=pcol(f"a0{l}")[:, g:g + 1])
                for g in range(G4):
                    ins = act.copy(rk["gate"][:, g, :], ps[:, 6 + g // 2, (g % 2) * T:(g % 2 + 1) * T])
                if l:
                    for g in range(G4):
                        ins = act.activation(rk["tmp"][:, g, :], ps[:, g // 2, (g % 2) * T:(g % 2 + 1) * T], ACT.Sigmoid,
                                             bias=pcol("vres_v0")[:, g:g + 1])
                seen.link(ins)
                act.activation(rk["dec"], rk["dec"], ACT.Exp, scale=-DECAY).then_inc(lora_out, 1)
                seen(hsum)
                act.activation(rk["tmp"].rearrange("p (b g) t -> p b (g t)", b=2), ps[:, 2:4, :], ACT.Sqrt)\
                    .then_inc(hroot, 1)
                chunks()
                seen(hsum_in, 4)
                act.activation(rk["tmp"], rk["tmp"], ACT.Sqrt).then_inc(hroot, 1)
                seen(hsum, 3)
                split_upper(mix_ready)

            def chunks():
                seen(blk_out)
                with seen.loop(NCH // 2, {pe_blk: STEPS2, blk_out: OUTS2}) as pair:
                    seen(blk_out, 0)
                    blocks = lambda n, src: [(c[n], src, pair * 2 * CH + k * CH) for k, c in enumerate(chunk_at)]
                    ab = [blocks("Abd", rk["A"]), blocks("Bbd", rk["B"])]
                    for dst, src, at in (ab[0][0], ab[1][0], ab[0][1], ab[1][1], *blocks("Kbd", rk["K"]),
                                         *blocks("Rbd", rk["R"]), *blocks("Vbd", rk["rw"][:, 8:12, :])):
                        act.copy(dst[0:64, :, 0:64], src[0:64, :, bass.ds(at, CH)])
                        act.copy(dst[64:128, :, 64:128], src[64:128, :, bass.ds(at, CH)]).then_inc(blocks_in, 1)

                    def out_of(first, name):
                        for k in range(2):
                            seen(pe_blk)
                            act.copy(chunk_at[k][name], four_of((first + k) % 8)).then_inc(blk_copied, 1)

                    seen.skip(pe_blk, 10)
                    out_of(10, "At")
                    out_of(12, "Bt")
                    out_of(14, "Kt")
                    out_of(16, "Vt")
                    seen.skip(pe_blk, 28)
                    out_of(46, "Gm")
                    out_of(48, "XA")
                    out_of(50, "U0")
                    seen.skip(pe_blk, 2)
                    out_of(54, "Q")
                    seen.skip(pe_blk, 4)
                    seen.skip(blk_out, OUTS2)

            def lru():
                project("lgate", lambda k, b: act.activation(lr["gate"][:, at(k), :], ps[:, b:b + 1, 0:T], ACT.Gelu))
                project("lrec", lambda k, b: act.copy(lr["rp"][:, at(k), 3:], ps[:, b:b + 1, 0:T]))
                seen(sp_a)
                seen.link(act.activation(lr["sp"][:, 1, :], lr["sp"][:, 0, :], ACT.Exp, scale=-1.0))
                act.activation(lr["sp"][:, 1, :], lr["sp"][:, 1, :], ACT.Ln, bias=ones[:, 0:1]).then_inc(sp_b, 1)
                seen(gates_mm)
                for c in range(DC):
                    bank, half = c // 2, slice((c % 2) * T, (c % 2 + 1) * T)
                    act.activation(lr["rg"][:, c, :], ps[:, bank, half], ACT.Sigmoid, bias=pcol("ba")[:, c:c + 1])
                    ins = act.activation(lr["ig"][:, c, :], ps[:, 4 + bank, half], ACT.Sigmoid,
                                         bias=pcol("bx")[:, c:c + 1])
                ins.then_inc(gates_out, 1)
                seen(la_ready)
                act.activation(lr["tau"], lr["la"], ACT.Tanh, scale=-1.0).then_inc(ea_ready, 1)
                act.activation(lr["a"], lr["la"], ACT.Exp).then_inc(ea_ready, 1)
                seen(beta_in)
                act.activation(lr["tau"], lr["tau"], ACT.Sqrt, scale=2.0).then_inc(beta, 1)
                split_upper(mix_ready)

            def attention():
                project("dkv", lambda k, b: act.copy(
                    ml["ck"][:, k, :] if k < 2 else ml["krz"][:, k - 2, :], ps[:, b, 0:T]))
                modulate_for("mix3")
                project("dq", lambda k, b: act.copy(ml["cq"][:, k, :], ps[:, b, 0:T]))
                seen(ang_ready, 2)
                act.activation(ml["cos"], ml["cos"], ACT.Sin)
                act.activation(ml["sin"], ml["sin"], ACT.Sin).then_inc(trig, 1)
                for _ in range(2):
                    seen(ms_ready)
                    act.activation(ml["rinv"], ml["rinv"], ACT.Sqrt).then_inc(root, 1)
                for h in range(AH):
                    seen(sc_ready)
                    if h >= 2:
                        seen(pt_mm)
                    s, p, st = (ml[n][:, h % 2] for n in ("s", "p", "st"))
                    for q in range(TT):
                        ins = act.activation(p[:, q, :], s[:, q, :], ACT.Exp, bias=st[:, q:q + 1],
                                             accum_out=st[:, 2 + q:3 + q])
                    ins.then_inc(exp_done, 1)
                split_upper(av_out, AH // 2)

            def modulate_for(which):
                norm()
                if which == "kv":
                    modulate(mod_kv[:, 0:8])
                else:
                    a = 0 if which.startswith("mix") else 24
                    modulate(mods[:, int(which[-1]) % 2, a:a + 8])

            def peer(l):
                project(f"q{l}", lambda k, b: act.copy(tk["q"][:, at(k), :], ps[:, b:b + 1, 0:T]))
                for tt in range(TT):
                    for b in range(4):
                        seen(score_mm)
                        act.copy(tk["sc"][:, tt, 4 * b:4 * b + 4, :].rearrange("p a k -> p (a k)"),
                                 ps[:, 2 + b, :]).then_inc(score_out, 1)
                name = f"u{l}"
                first = SEGS[name][0]

                def gelu(k, b):
                    act.activation(act_all[:, at(k), :], ps[:, b:b + 1, 0:T], ACT.Gelu).then_inc(taken, 1)

                def step(n, j, k, i):
                    upper(n, j, i, name)
                    gelu(k - 2, j % 2)
                upper(first, first, None, name)
                upper(first + 1, first + 1, None, name)
                a = 2
                for tt in range(TT):
                    b = STEPS * tt + SOFT + 3
                    in_loops(act, name, a, b, step)
                    a = b
                    seen(sm_in)
                    act.activation(tk["e"][:, 2], tk["e"][:, 2], ACT.Exp).then_inc(sm_exp, 1)
                in_loops(act, name, a, SC_SLOT + 2, step)
                seen(ranked)
                in_loops(act, name, SC_SLOT + 2, TK_SLOT + 2, step)
                act.wait_ge(sel_ready, TT * (l + 1))
                in_loops(act, name, TK_SLOT + 2, KEYS, step)
                for k in (KEYS - 2, KEYS - 1):
                    act.wait_ge(tile_used, first + k + 1)
                    gelu(k, (first + k) % 2)
                if l < 3:
                    rows(l + 1)
                name = f"v{l}"
                first = SEGS[name][0]
                act.wait_ge(gated, (T // 4) * (l + 1))

                def upper_gated(k, j):
                    act.copy(wa_hi[:, j % 4:j % 4 + 1, :], act_all[:, at(k), :]).then_inc(wah, 1)

                def step(n, j, k, i):
                    upper(n, j, i, name)
                    upper_gated(k + 1, j + 1)
                upper_gated(0, first)
                tiles_in_loops(act, first, KEYS - 1, step)
                upper(first + KEYS - 1, first + KEYS - 1, None, name)

            act.wait_ge(par_in, 32)
            act.activation(c_act[:, 0, :], pcol("c0"), ACT.Silu).then_inc(c_ready, 1)
            act.activation(c_act[:, 1, :], pcol("c1"), ACT.Silu).then_inc(c_ready, 1)
            rows(0)
            for l in range(4):
                if l == 3:
                    modulate_for("kv")
                    attention()
                else:
                    modulate_for(f"mix{l}")
                    if l < 2:
                        rwkv(l)
                    else:
                        lru()
                uppers(("out0", "out1", "lout", "wo")[l])
                modulate_for(f"ffn{l}")
                peer(l)
                if l % 2:
                    norm()

        @block.vector
        def _(dve):
            seen = Seen(dve, chains["dve"])
            link = seen.link
            tts, ts, stt, cp = dve.tensor_tensor, dve.tensor_scalar, dve.scalar_tensor_tensor, dve.tensor_copy

            def lower(n, j, name):
                dve.wait_ge(hi_done, n + (1 - WHOLE[name]))
                tts(t_lo[:, j % SPL, :], raw[:, j % RAW, :], t_hi[:, j % SPL, :].bitcast(F32),
                    ALU.subtract).then_inc(lo_done, 1)

            def lowers(name):
                tiles_in_loops(dve, *SEGS[name][:2], lambda n, j, k, i: lower(n, j, name))

            def at(k):
                return bass.ds(k, 1) if not isinstance(k, int) else slice(k, k + 1)

            def add_products(name, gate):
                first, count = SEGS[name][:2]
                lower(first, first, name)
                lower(first + 1, first + 1, name)

                def take_out(k, b):
                    return stt(x[:, k, :], ps[:, b, 0:T], gate[:, k:k + 1], x[:, k, :], ALU.mult, ALU.add)

                for k in range(2, count):
                    lower(first + k, first + k, name)
                    take_out(k - 2, (first + k) % 2).then_inc(taken, 1)
                for k in (count - 2, count - 1):
                    dve.wait_ge(tile_used, first + k + 1)
                    take_out(k, (first + k) % 2).then_inc(taken, 1)
                dve.wait_ge(taken, TAKEN[name] + count)

            def modulation(l):
                dve.wait_ge(row_turned, ROWS[l] + SEGS[f"ada{l}"][1] // 8)
                if l == 3:
                    tts(mod_kv[:, :], ps[:, 5, 48:64], pcol("kv_ada_b"), ALU.add)
                link(tts(mods[:, l % 2, :], ps[:, 5, 0:48], pcol(f"ada_b{l}"), ALU.add), mod_ready)

            def norm_x():
                tts(wide, x[:, :, :], x[:, :, :], ALU.mult).then_inc(squares, 1)
                seen(sumsq)
                ts(ms_all, ps[:, 2, 0:T], 1.0 / D, EPS, ALU.mult, ALU.add).then_inc(ms_ready, 1)
                seen(root)
                link(dve.reciprocal(rinv_all, rinv_all))
                return tts(wide, x[:, :, :], rinv_all.unsqueeze(1).broadcast_to([P, DC, T]), ALU.mult)

            def norm(g, scale):
                link(stt(gain[:, :], scale, 1.0, g, ALU.add, ALU.mult))
                norm_x().then_inc(normed, 1)
                split_lower()

            def split_lower():
                seen(h_up)
                tts(h_lo[:, :, :], wide, h_hi[:, :, :].bitcast(F32), ALU.subtract).then_inc(h_split, 1)

            def rwkv(l):
                z, rw, kk, kp, a, v = rk["z"], rk["rw"], rk["kk"], rk["kp"], rk["a"], rk["rw"][:, 8:12, :]
                r, k, tmp, tmp2 = rw[:, 0:4, :], rw[:, 4:8, :], rk["tmp"], rk["d1"]
                name = f"in{l}"
                first, count = SEGS[name][:2]
                link(dve.memset(z[:, :, 0:1], 0.0))
                lowers(name)
                dve.wait_ge(taken, TAKEN[name] + count)
                link(tts(rw[:, 0:14, :], z[:, 0:14, 0:T], z[:, 0:14, 1:T + 1], ALU.subtract), z_free)
                if l:
                    link(tts(rw[:, 14, :], z[:, 18, 0:T], z[:, 18, 1:T + 1], ALU.subtract))
                for m in range(14 + l):
                    ins = stt(rw[:, m, :], rw[:, m, :], pcol(f"mu{l}")[:, m:m + 1], z[:, m + 4 * (m == 14), 1:],
                              ALU.mult, ALU.add)
                link(ins, shifted)
                if not l:
                    cp(v_first[:, :, :], v)
                for g in range(G4):
                    ins = ts(kk[:, g, :], k[:, g, :], pcol(f"k_k{l}")[:, g:g + 1], None, ALU.mult)
                link(ins)
                seen(lora_out)
                if l:
                    link(tts(v_first[:, :, :], v_first[:, :, :], v, ALU.subtract))
                    link(tts(v_first[:, :, :], v_first[:, :, :], tmp, ALU.mult))
                    link(tts(v, v, v_first[:, :, :], ALU.add))
                tts(tmp2, kk, kk, ALU.mult).then_inc(hsum_in, 1)
                link(ts(gain[:, 0:4], pcol(f"k_a{l}"), -1.0, 1.0, ALU.mult, ALU.add))
                for g in range(G4):
                    ins = ts(kp[:, g, :], a[:, g, :], pcol(f"k_a{l}")[:, g:g + 1], gain[:, g:g + 1], ALU.mult, ALU.add)
                link(ins)
                link(tts(kp, kp, k, ALU.mult))
                dec, Pc, Pinv, Pprev = rk["dec"], rk["Pc"], rk["Pinv"], rk["Pprev"]
                starts = lambda b: b.rearrange("p g (c t) -> p (g c) t", t=CH)
                seen(hsum)
                link(dve.memset(tmp2, 0.0))
                link(cp(starts(tmp2)[:, :, 0:1], starts(dec)[:, :, 0:1]))
                link(dve.memset(starts(dec)[:, :, 0:1], 0.0))
                flat = lambda b: b.rearrange("p g t -> p (g t)")
                link(dve.tensor_tensor_scan(flat(Pc), flat(dec), flat(tmp2), 0.0, ALU.mult, ALU.add))
                link(dve.reciprocal(Pinv, Pc))
                dve.memset(starts(Pprev)[:, :, 0:1], 1.0)
                link(cp(starts(Pprev)[:, :, 1:], starts(Pc)[:, :, 0:CH - 1]))
                seen(hroot)
                link(ts(tmp, tmp, 1e-12, None, ALU.max))
                link(dve.reciprocal(tmp, tmp))
                link(tts(kk, kk, tmp, ALU.mult))
                link(tts(rk["R"], r, kp, ALU.mult))
                for g in range(G4):
                    ins = ts(tmp[:, g, :], rk["R"][:, g, :], pcol(f"r_k{l}")[:, g:g + 1], None, ALU.mult)
                ins.then_inc(hsum_in, 1)
                link(stt(rk["A"], kk, -1.0, Pprev, ALU.mult, ALU.mult))
                link(tts(rk["B"], kk, a, ALU.mult))
                link(tts(rk["B"], rk["B"], Pinv, ALU.mult))
                link(tts(rk["K"], kp, Pinv, ALU.mult))
                link(tts(rk["R"], r, Pc, ALU.mult))
                seen(hsum)
                link(tts(rk["bonus"].rearrange("p (b g) t -> p b (g t)", b=2), ps[:, 4:6, :],
                         v.rearrange("p (b g) t -> p b (g t)", b=2), ALU.mult))
                dve.wait_ge(pool_ready, l + 1)
                for c in chunk_at:
                    for n in ("Abd", "Bbd", "Kbd", "Rbd", "Vbd"):
                        dve.memset(c[n], 0.0)
                link(dve.memset(states[0], 0.0), blk_out)
                masks = rk["masks"]
                SU, SL, IU, M1T, M1 = (masks[:, k, :] for k in range(5))
                bc = lambda m: m.unsqueeze(1).broadcast_to([P, G4, P])
                both = (0, 1)
                with seen.loop(NCH // 2, {chains["dve"]: 2, pe_blk: STEPS2, blk_out: OUTS2}) as pair:

                    def out_of(n, k, name, mask=None, plus=None, out=blk_out):
                        seen(pe_blk)
                        if mask is not None:
                            ins = tts(chunk_at[k][name], four_of(n % 8), bc(mask), ALU.mult)
                        else:
                            ins = tts(chunk_at[k][name], four_of(n % 8), chunk_at[k][plus], ALU.add)
                        return ins.then_inc(out, 1) if out else ins

                    for k in both:
                        out_of(0 + k, k, "LT", SU)
                    for k in both:
                        c = chunk_at[k]
                        out_of(2 + k, k, "X0", M1, out=None)
                        seen(blk_out)
                        link(tts(c["XT0"], c["LT"], bc(M1T), ALU.mult))
                        tts(c["X0"], c["X0"], bc(ident), ALU.add)
                        tts(c["XT0"], c["XT0"], bc(ident), ALU.add).then_inc(blk_out, 1)
                    for n, name, mask in ((4, "L2T", SU), (6, "T1T", IU), (8, "T2T", IU)):
                        for k in both:
                            out_of(n + k, k, name, mask)
                    seen.skip(blk_out, OUTS2 - 2)
                    seen.skip(pe_blk, 8)
                    n = 18
                    for lev in range(5):
                        cur, nxt = lev % 2, (lev + 1) % 2
                        for k in both:
                            out_of(n + k, k, "Z", masks[:, 5 + lev, :])
                        n += 2
                        for k in both:
                            if lev < 4:
                                out_of(n, k, f"X{nxt}", plus=f"X{cur}")
                                n += 1
                            out_of(n, k, f"XT{nxt}", plus=f"XT{cur}")
                            n += 1
                    seen.skip(pe_blk, 6)
                    for k in both:
                        out_of(52 + k, k, "RpT", plus="Rbd")
                    seen.skip(pe_blk, 2)
                    for k in both:
                        seen(pe_blk)
                        end = rk["Pc"].rearrange("p g (c t) -> p g c t", t=CH)[:, :, bass.ds(pair * 2 + k, 1), CH - 1]
                        tts(states[1 - k], four_of((56 + 2 * k) % 8), end.broadcast_to([P, G4, P]), ALU.mult)\
                            .then_inc(state_out, 1)
                        seen(pe_blk)
                        tok = bass.ds(pair * 2 * CH + k * CH, CH)
                        y_blocks = four_of((57 + 2 * k) % 8)
                        cp(rk["y"][0:64, :, tok], y_blocks[0:64, :, 0:64])
                        cp(rk["y"][64:128, :, tok], y_blocks[64:128, :, 64:128]).then_inc(state_out, 1)
                y = rk["y"]
                seen(hsum)
                halves = lambda b: b.rearrange("p (b g) t -> p b (g t)", b=2)
                link(stt(halves(y), ps[:, 2:4, :], -1.0 / 64, halves(y), ALU.mult, ALU.add))
                tts(tmp, y, y, ALU.mult).then_inc(hsum_in, 1)
                seen(hsum)
                ts(halves(tmp), ps[:, 4:6, :], 1.0 / 64, GN_EPS, ALU.mult, ALU.add).then_inc(hsum_in, 1)
                seen(hroot)
                link(dve.reciprocal(tmp, tmp))
                link(tts(y, y, tmp, ALU.mult))
                for g in range(G4):
                    ins = ts(y[:, g, :], y[:, g, :], pcol(f"lnx_g{l}")[:, g:g + 1], pcol(f"lnx_b{l}")[:, g:g + 1],
                             ALU.mult, ALU.add)
                link(ins)
                link(tts(y, y, rk["bonus"], ALU.add))
                tts(wide[:, 0:4, :], y, rk["gate"], ALU.mult)
                seen(pool_mm)
                for g in range(G4):
                    ins = ts(wide[:, 4 + g, :], ps[:, 6 + g // 2, (g % 2) * T:(g % 2 + 1) * T],
                             pcol(f"pool_scale{l}")[:, g:g + 1], None, ALU.mult)
                ins.then_inc(mix_ready, 1)
                split_lower()

            def lru():
                rp, xc = lr["rp"], lr["xc"]
                lowers("lgate")
                link(dve.memset(rp[:, :, 0:3], 0.0))
                lowers("lrec")
                link(ts(lr["sp"][:, 0, :], pcol("lam"), -1.0, None, ALU.mult))
                tts(lr["sp"][:, 0, :], lr["sp"][:, 0, :], pcol("lam"), ALU.max).then_inc(sp_a, 1)
                dve.wait_ge(taken, TAKEN["lrec"] + 8)
                w = lambda k, c: pcol("conv_w")[:, 8 * k + c:8 * k + c + 1]
                for c in range(DC):
                    ins = ts(xc[:, c, :], rp[:, c, 0:T], w(0, c), pcol("conv_b")[:, c:c + 1], ALU.mult, ALU.add)
                link(ins)
                for k in range(1, 4):
                    for c in range(DC):
                        ins = stt(xc[:, c, :], rp[:, c, k:k + T], w(k, c), xc[:, c, :], ALU.mult, ALU.add)
                    if k < 3:
                        link(ins)
                ins.then_inc(xc_ready, 1)
                link(ts(lr["sp"][:, 2, :], pcol("lam"), -1.0, 0.0, ALU.mult, ALU.max))
                seen(sp_b)
                link(tts(lr["sp"][:, 2, :], lr["sp"][:, 2, :], lr["sp"][:, 1, :], ALU.add))
                link(ts(lr["sp"][:, 3, :], lr["sp"][:, 2, :], -8.0, None, ALU.mult))
                seen(gates_out)
                for c in range(DC):
                    ins = ts(lr["la"][:, c, :], lr["rg"][:, c, :], lr["sp"][:, 3, c:c + 1], None, ALU.mult)
                ins.then_inc(la_ready, 1)
                link(tts(lr["ig"], lr["ig"], xc, ALU.mult))
                seen(ea_ready)
                link(ts(lr["rg"], lr["tau"], 1.0, None, ALU.add))
                link(dve.reciprocal(lr["rg"], lr["rg"]))
                tts(lr["tau"], lr["tau"], lr["rg"], ALU.mult).then_inc(beta_in, 1)
                seen(beta)
                link(tts(lr["ig"], lr["ig"], lr["tau"], ALU.mult))
                seen(ea_ready)
                for c in range(DC):
                    ins = dve.tensor_tensor_scan(lr["hs"][:, c, :], lr["a"][:, c, :], lr["ig"][:, c, :], 0.0,
                                                 ALU.mult, ALU.add)
                link(ins)
                tts(wide, lr["gate"], lr["hs"], ALU.mult).then_inc(mix_ready, 1)
                split_lower()

            def attention():
                lowers("dkv")
                norm(pcol("mix_g3"), mods[:, 1, 8:16])
                lowers("dq")
                dve.wait_ge(taken, TAKEN["dq"] + 3)
                dve.wait_ge(small_in, SMALL["mix3"])
                posf, ang, cos, sin, tmp = ml["posf"], ml["ang"], ml["cos"], ml["sin"], ml["tmp"]
                cp(ml["posq"], ml["posqi"].bitcast(I32))
                link(cp(posf, ml["posi"].bitcast(I32)))
                for tt in range(TT):
                    ins = ts(ml["mask"][:, tt, :], posf, ml["posq"][:, tt:tt + 1], None, ALU.is_le)
                link(ins)
                link(ts(ml["mbias"], ml["mask"], -1.0, -NEG, ALU.add, ALU.mult))
                link(ts(ang, posf, pcol("freq"), None, ALU.mult))
                MAGIC = 12582912.0
                C1, C2 = 6.28125, 0.0019350051879882812
                C3 = 2.0 * np.pi - C1 - C2
                for dst, quarter, add in ((sin, 0.0, 0.0), (cos, 0.25, float(np.pi / 2))):
                    link(ts(tmp[:, 0, :], ang, float(1 / (2 * np.pi)), quarter, ALU.mult, ALU.add))
                    link(ts(tmp[:, 1, :], tmp[:, 0, :], MAGIC, None, ALU.add))
                    link(ts(tmp[:, 1, :], tmp[:, 1, :], MAGIC, None, ALU.subtract))
                    link(stt(dst, tmp[:, 1, :], -C1, ang, ALU.mult, ALU.add))
                    link(stt(dst, tmp[:, 1, :], -C2, dst, ALU.mult, ALU.add))
                    link(stt(dst, tmp[:, 1, :], -float(C3), dst, ALU.mult, ALU.add))
                    if add:
                        link(ts(dst, dst, add, None, ALU.add))
                    link(ts(dst, dst, 3.1415925, -3.1415925, ALU.min, ALU.max), ang_ready)
                seen(trig)
                link(ts(sin, sin, pcol("sign"), None, ALU.mult))
                for lat, n, g in (("ck", 2, "ckv_g"), ("cq", 3, "cq_g")):
                    tts(ml["sq"][:, 0:n, :], ml[lat], ml[lat], ALU.mult).then_inc(squares, 1)
                    seen(sumsq)
                    ts(ml["rinv"], ps[:, 2, 0:T], 1.0 / (n * P), EPS, ALU.mult, ALU.add).then_inc(ms_ready, 1)
                    seen(root)
                    link(dve.reciprocal(ml["rinv"], ml["rinv"]))
                    for c in range(n):
                        ins = stt(ml[lat][:, c, :], ml[lat][:, c, :], pcol(g)[:, c:c + 1], ml["rinv"], ALU.mult, ALU.mult)
                    link(ins)
                link(tts(ml["kr"], ml["krz"][:, 0, :], cos, ALU.mult))
                link(tts(tmp[:, 0, :], ml["krz"][:, 1, :], sin, ALU.mult))
                link(tts(ml["kr"], ml["kr"], tmp[:, 0, :], ALU.add))
                link(dve.memset(ml["vpad"], 0.0), lat_in)
                pair = lambda v, a: v[:, a:a + 2, :].rearrange("p a t -> p (a t)")
                dsts = [pair(ml["kn"], a) for a in (0, 2, 4, 6)] + [pair(ml["qn"], a) for a in (0, 2, 4, 6)] \
                    + [pair(ml["qr"], a) for a in (0, 2)] + [pair(ml["qs"], a) for a in (0, 2)]
                for n, dst in enumerate(dsts):
                    seen(kv_mm)
                    link(cp(dst, ps[:, n % 8, :]), kv_out)
                for kt in range(TT):
                    for half in range(2):
                        seen(kv_mm)
                        src = ps[:, 4 + 2 * kt + half, :].rearrange("p (h two k) -> p h two k", two=2, k=64)
                        dst = ml["vpad"][:, kt, 8 * half:8 * half + 8, :].rearrange("p (h two) k -> p h two k", two=2)
                        cp(dst[:, :, 0, 0:64], src[:, :, 0, :])
                        link(cp(dst[:, :, 1, 64:128], src[:, :, 1, :]), kv_out)
                bc4 = lambda v: v.unsqueeze(1).broadcast_to([P, 4, T])
                link(tts(ml["qr"], ml["qr"], bc4(cos), ALU.mult))
                link(tts(ml["qs"], ml["qs"], bc4(sin), ALU.mult))
                link(tts(ml["qr"], ml["qr"], ml["qs"], ALU.add), lat_in)

                def scaled(h):
                    s, st = ml["s"][:, h % 2], ml["st"][:, h % 2]
                    seen(sc_mm)
                    link(stt(s, ps[:, 2 + h % 2, :].rearrange("p (q k) -> p q k", q=2), ATT_SCALE, ml["mask"],
                             ALU.mult, ALU.mult))
                    link(tts(s, s, ml["mbias"], ALU.add))
                    link(dve.tensor_reduce(st[:, 4:6], s, AX.X, ALU.max))
                    ts(st[:, 0:2], st[:, 4:6], -1.0, None, ALU.mult).then_inc(sc_ready, 1)

                def weights(h):
                    p, st = ml["p"][:, h % 2], ml["st"][:, h % 2]
                    seen(exp_done)
                    link(dve.reciprocal(st[:, 6:8], st[:, 2:4]))
                    for q in range(TT):
                        ins = ts(p[:, q, :], p[:, q, :], st[:, 6 + q:7 + q], None, ALU.mult)
                    ins.then_inc(p_ready, 1)

                def turned(h):
                    seen(pt_mm)
                    cp(ml["pT"][:, h % 2].rearrange("p a t -> p (a t)"), ps[:, 4 + h % 2, :]).then_inc(pt_out, 1)

                def attended(pair):
                    seen(av_mm)
                    cp(wide[:, pair, :], ps[:, 6 + pair % 2, 0:T]).then_inc(av_out, 1)

                scaled(0)
                for h in range(AH):
                    if h + 1 < AH:
                        scaled(h + 1)
                    weights(h)
                    if h >= 1:
                        turned(h - 1)
                    if h >= 3 and h % 2:
                        attended((h - 3) // 2)
                turned(AH - 1)
                attended(AH // 2 - 1)
                split_lower()

            def first8(src, other, val, idx):
                link(dve.max(val[:, 0:8], src))
                dve.max_index(idx[:, 0:8], val[:, 0:8], src)
                return dve.match_replace(other, val[:, 0:8], src, LOWEST)

            def next8(other, val, idx):
                link(dve.max(val[:, 8:16], other))
                return dve.max_index(idx[:, 8:16], val[:, 8:16], other)

            val, idx, idf, cs, ci = tk["val"], tk["idx"].bitcast(U32), tk["idf"], tk["cs"], tk["ci"].bitcast(U32)
            hat, hatu, e, eq = tk["hat"], tk["hatu"].bitcast(U32), tk["e"], tk["eq"]
            half_shape = [P, HEADS // 2, TOPK, TOPK]

            def two(v, w, h=slice(0, HEADS)):
                return v.rearrange("p (h two) k -> p two h k", two=2)[:, w, h]

            def pair_sums(part):
                h = slice(4 * part, 4 * part + 4)
                return tts(tk["cand"][:, h].rearrange("p h (i j) -> p h i j", i=TOPK),
                           two(val, 0, h).unsqueeze(3).broadcast_to(half_shape),
                           two(val, 1, h).unsqueeze(2).broadcast_to(half_shape), ALU.add)

            def look_up(w, part, step):
                h = slice(4 * part, 4 * part + 4)
                if step == 0:
                    return tts(eq, hat[:, w, h].unsqueeze(3).broadcast_to(half_shape),
                               iota[:, 0:TOPK].unsqueeze(1).unsqueeze(1).broadcast_to(half_shape), ALU.is_equal)
                if step == 1:
                    return tts(eq, eq, two(idf, w, h).unsqueeze(2).broadcast_to(half_shape), ALU.mult)
                return dve.tensor_reduce(e[:, w, h], eq, AX.X, ALU.add)

            def choose(l):
                name = f"u{l}"
                first = SEGS[name][0]

                def sel_out(tt):
                    seen(chosen_t)
                    cp(sel[:, :, tt * P:(tt + 1) * P], ps[:, 6 + tt, 0:3 * P].rearrange("p (w t) -> p w t", w=3))\
                        .then_inc(sel_ready, 1)

                for tt in range(TT):
                    for k in range(STEPS):
                        lower(first + STEPS * tt + k, first + STEPS * tt + k, name)
                        if k < PAIRS:
                            if k % 4 == 0:
                                seen(score_out)
                            src = tk["sc"][:, tt, k, :]
                            link(first8(src, tk["s2"], val[:, k, :], idx[:, k, :]))
                            link(next8(tk["s2"], val[:, k, :], idx[:, k, :]), *([ranked] if tt and k == 15 else []))
                            if tt and k == 4:
                                sel_out(0)
                        elif k < RANK_PAIRS:
                            if k == PAIRS:
                                link(cp(idf, idx))
                            link(pair_sums(k - PAIRS))
                        elif k < SOFT:
                            h, second = divmod(k - RANK_PAIRS, 2)
                            link(next8(tk["c2"], cs[:, h, :], ci[:, h, :]) if second
                                 else first8(tk["cand"][:, h, :], tk["c2"], cs[:, h, :], ci[:, h, :]))
                        elif k == SOFT:
                            tts(e[:, 2], cs, cs[:, :, 0:1].broadcast_to([P, HEADS, TOPK]), ALU.subtract)\
                                .then_inc(sm_in, 1)
                            ts(hatu[:, 0], ci, 4, None, ALU.logical_shift_right)
                            link(ts(hatu[:, 1], ci, TOPK - 1, None, ALU.bitwise_and))
                            link(cp(hat, hatu))
                        elif k < CHOSEN:
                            part, step = divmod(k - LOOK_UP, 3)
                            link(look_up(part // 2, part % 2, step))
                        else:
                            seen(sm_exp)
                            link(dve.tensor_reduce(tk["den"][:, 0, :], e[:, 2], AX.X, ALU.add))
                            link(dve.reciprocal(tk["den"][:, 1, :], tk["den"][:, 0, :]))
                            tts(e[:, 2], e[:, 2], tk["den"][:, 1, :].unsqueeze(2).broadcast_to([P, HEADS, TOPK]),
                                ALU.mult).then_inc(chosen, 1)
                a = TT * STEPS
                for k in range(a, a + 4):
                    lower(first + k, first + k, name)
                sel_out(1)
                in_loops(dve, name, a + 4, KEYS, lambda n, j, k, i: lower(n, j, name))

            def gates(l):
                def hots(g, b):
                    cols = bass.ds(g * 4, 4) if not isinstance(g, int) else slice(4 * g, 4 * g + 4)
                    tts(oh1[:, b], iota.unsqueeze(1).broadcast_to([P, 4, P]),
                        sel[:, 0, cols].unsqueeze(2).broadcast_to([P, 4, P]), ALU.is_equal)
                    for q in range(4):
                        col = lambda w: sel[:, w, bass.ds(g * 4 + q, 1)] if not isinstance(g, int) \
                            else sel[:, w, 4 * g + q:4 * g + q + 1]
                        ins = ts(oh2[:, b, q, :], iota, col(1), col(2), ALU.is_equal, ALU.mult)
                    ins.then_inc(hot, 1)

                def gate(g, b):
                    view = act_all[:, :, bass.ds(g * 4, 4)] if not isinstance(g, int) else act_all[:, :, 4 * g:4 * g + 4]
                    view = view.rearrange("p e t -> p t e")
                    return tts(view, ps[:, b, :].rearrange("p (t e) -> p t e", t=4), view, ALU.mult).then_inc(gated, 1)

                dve.wait_ge(sel_ready, TT * (l + 1))
                dve.wait_ge(taken, TAKEN[f"u{l}"] + KEYS)
                n = T // 4
                hots(0, 0)
                with seen.loop(n // 2 - 1, {gates_t: 2}) as i:
                    hots(i * 2 + 1, 1)
                    seen(gates_t)
                    gate(i * 2, 0)
                    hots(i * 2 + 2, 0)
                    seen(gates_t)
                    gate(i * 2 + 1, 1)
                hots(n - 1, 1)
                seen(gates_t)
                gate(n - 2, 0)
                seen(gates_t)
                gate(n - 1, 1)

            def experts_out(l):
                name = f"v{l}"
                first = SEGS[name][0]
                g2 = mods[:, l % 2, 40:48]

                def lower_gated(k, j):
                    dve.wait_ge(wah, k + (1 + KEYS * l))
                    tts(wa_lo[:, j % 4:j % 4 + 1, :], act_all[:, at(k), :], wa_hi[:, j % 4:j % 4 + 1, :].bitcast(F32),
                        ALU.subtract).then_inc(wal, 1)

                def step(n, j, k, i):
                    lower(n, j, name)
                    lower_gated(k + 1, j + 1)
                lower_gated(0, first)
                tiles_in_loops(dve, first, KEYS - 1, step)
                lower(first + KEYS - 1, first + KEYS - 1, name)
                dve.wait_ge(tile_used, first + KEYS)
                for tt in range(TT):
                    for half in range(2):
                        ins = cp(sum_sb[:, tt, half * 512:(half + 1) * 512], ps[:, 2 + 2 * tt + half, :])
                ins.then_inc(moe_out, 1)
                for m in range(4):
                    seen(moe_t)
                    for c in range(2):
                        ins = stt(x[:, 2 * m + c, :], ps[:, [6, 7, 0, 1][m], c * T:(c + 1) * T], g2[:, 2 * m + c:2 * m + c + 1],
                                  x[:, 2 * m + c, :], ALU.mult, ALU.add)
                if l in (1, 3):
                    link(ins)
                return ins

            dve.wait_ge(par_in, 32)
            modulation(0)
            for l in range(4):
                if l == 0:
                    dve.wait_ge(x_in, 16)
                if l == 3:
                    norm(pcol("kv_g"), mod_kv[:, 8:16])
                    attention()
                else:
                    norm(pcol(f"mix_g{l}"), mods[:, l % 2, 8:16])
                    if l < 2:
                        rwkv(l)
                    else:
                        lru()
                add_products(("out0", "out1", "lout", "wo")[l], mods[:, l % 2, 16:24])
                norm(pcol(f"ffn_g{l}"), mods[:, l % 2, 32:40])
                lowers(f"q{l}")
                choose(l)
                gates(l)
                if l < 3:
                    modulation(l + 1)
                ins = experts_out(l)
                if l == 1 or l == 3:
                    link(norm_x())
                    g = pcol("lnf_g" if l == 1 else "final_g")
                    for c in range(DC):
                        dst = x if l == 1 else wide
                        ins = ts(dst[:, c, :], wide[:, c, :], g[:, c:c + 1], None, ALU.mult)
                link(ins, arena_free if l < 3 else fin)

        @block.tensor
        def _(pe):
            seen = Seen(pe, None)
            mm = pe.matmul

            def products(name, a=0, b=None):
                first, count = SEGS[name][:2]

                def step(n, j, k, i):
                    pe.wait_ge(lo_done, n + (1 - WHOLE[name]))
                    if not (TAKEN[name] == 0 and i is None and k < 2):
                        pe.wait_ge(taken, k + (TAKEN[name] - 1))
                    o = ps[:, j % 2, 0:T]
                    hi = t_hi[:, j % SPL, :].rearrange("p (c m) -> p c m", c=DC)
                    lo = t_lo[:, j % SPL, :].rearrange("p (c m) -> p c m", c=DC)
                    for c in range(DC):
                        mm(o, hi[:, c, :], h_hi[:, c, :], start=(c == 0), stop=False)
                        mm(o, hi[:, c, :], h_lo[:, c, :], start=False, stop=False)
                        ins = mm(o, lo[:, c, :], h_hi[:, c, :], start=False, stop=(c == DC - 1))
                    ins.then_inc(tile_used, 1)
                if TAKEN[name] == 0:
                    step(first, first, 0, None)
                    step(first + 1, first + 1, 1, None)
                    a = 2
                in_loops(pe, name, a, b or count, step)

            def modulate(l, n, j, kc, g, i):
                turn = (j // RAW + 1) if i is None else i * 2 + (j // RAW + 1)
                pe.wait_ge(loaded[j % RAW], turn * 16)
                if kc == 0 and not (isinstance(g, int) and g == 0):
                    turn_row(l, g - 1)
                for half in range(2):
                    ins = mm(ps[0:1, 6 + half, :], c_act[:, l // 2, kc:kc + 1],
                             raw[:, j % RAW, half * 512:(half + 1) * 512], start=(kc == 0), stop=(kc == DC - 1))
                ins.then_inc(tile_used, 1)

            def turn_row(l, g):
                pe.wait_ge(row_out, g + (ROWS[l] + 1))
                for m in range(8):
                    o = ps[:, 5, 8 * g + m:8 * g + m + 1] if isinstance(g, int) else ps[:, 5, bass.ds(g * 8 + m, 1)]
                    ins = mm(o, mod_row[0:1, m * P:(m + 1) * P], ones[0:1, 0:1], start=True, stop=True)
                ins.then_inc(row_turned, 1)

            def sum_squares(src, n):
                seen(squares)
                for c in range(n):
                    ins = mm(ps[:, 2, 0:T], ones, src[:, c, :], start=(c == 0), stop=(c == n - 1))
                ins.then_inc(sumsq, 1)

            def head_sum(src, bank, wait=True):
                if wait:
                    seen(hsum_in)
                for b in range(2):
                    ins = mm(ps[:, bank + b, :], head_ones, src[:, 2 * b:2 * b + 2, :].rearrange("p g t -> p (g t)"),
                             start=True, stop=True)
                ins.then_inc(hsum, 1)

            def rwkv(l):
                rw, lw = rk["rw"], rk["lora"]
                products(f"in{l}")
                pe.wait_ge(small_in, SMALL[f"mix{l}"])
                seen(lora_in, 2)
                for m in range(8):
                    mm(ps[:, 2 + m // 2, (m % 2) * T:(m % 2 + 1) * T], lw[:, m, :], rw[:, 12, :], start=True, stop=True)
                for m in range(4):
                    ins = mm(ps[:, 6 + m // 2, (m % 2) * T:(m % 2 + 1) * T], lw[:, 8 + m, :], rw[:, 13, :],
                             start=True, stop=True)
                if l:
                    pe.wait_ge(taken, TAKEN["in1"] + 19)
                    for m in range(4):
                        ins = mm(ps[:, m // 2, (m % 2) * T:(m % 2 + 1) * T], lw[:, 12 + m, :], rw[:, 14, :],
                                 start=True, stop=True)
                ins.then_inc(lora_mm, 1)
                head_sum(rk["d1"], 2)
                head_sum(rk["tmp"], 4)
                both = (0, 1)
                seen(blk_out)
                with seen.loop(NCH // 2, {blocks_in: BLOCKS2, blk_out: OUTS2, blk_copied: COPIES2,
                                          state_out: 4}) as pair:
                    def four(n, *terms):
                        for g in range(G4):
                            for m, (lhs, rhs) in enumerate(terms):
                                ins = mm(ps[:, n % 8, g * P:(g + 1) * P], lhs if lhs is ident else lhs[:, g, :],
                                         rhs[:, g, :], start=(m == 0), stop=(m == len(terms) - 1))
                        ins.then_inc(pe_blk, 1)

                    def turn(n, src):
                        for g in range(G4):
                            ins = pe.transpose(ps[:, n % 8, g * P:(g + 1) * P], src[:, g, :], ident)
                        ins.then_inc(pe_blk, 1)

                    for k in both:
                        seen(blocks_in, 2)
                        four(0 + k, (chunk_at[k]["Bbd"], chunk_at[k]["Abd"]))
                    for k in both:
                        four(2 + k, (chunk_at[k]["Abd"], chunk_at[k]["Bbd"]))
                    for k in both:
                        seen(blocks_in)
                        four(4 + k, (chunk_at[k]["Kbd"], chunk_at[k]["Abd"]))
                    for k in both:
                        seen(blocks_in)
                        four(6 + k, (chunk_at[k]["Bbd"], chunk_at[k]["Rbd"]))
                    for k in both:
                        seen(blk_out)
                        four(8 + k, (chunk_at[k]["Kbd"], chunk_at[k]["Rbd"]))
                    for m, name in enumerate(("Abd", "Bbd", "Kbd", "Vbd")):
                        for k in both:
                            if name == "Vbd":
                                seen(blocks_in)
                            seen(blk_out)
                            turn(10 + 2 * m + k, chunk_at[k][name])
                    n = 18
                    for lev in range(5):
                        cur = lev % 2
                        for k in both:
                            if lev == 0:
                                seen(blk_copied)
                            else:
                                seen(blk_out, 1 if k == 0 else 2)
                            four(n + k, (chunk_at[k]["LT"], chunk_at[k][f"X{cur}"]))
                        n += 2
                        for k in both:
                            if lev == 0:
                                seen(blk_copied, 2)
                                seen(blk_out)
                            elif k == 0:
                                seen(blk_out, 2)
                            else:
                                seen(blk_out)
                            if lev < 4:
                                four(n, (chunk_at[k][f"XT{cur}"], chunk_at[k]["Z"]))
                                n += 1
                            four(n, (chunk_at[k]["Z"], chunk_at[k][f"XT{cur}"]))
                            n += 1
                        if lev == 0:
                            seen(blk_copied, 2)
                    for k in both:
                        four(46 + k, (chunk_at[k]["L2T"], chunk_at[k]["Vt"]))
                    for k in both:
                        seen(blk_out)
                        four(48 + k, (chunk_at[k]["XT1"], chunk_at[k]["At"]))
                    for k in both:
                        seen(blk_copied)
                        four(50 + k, (chunk_at[k]["XT1"], chunk_at[k]["Gm"]))
                    for k in both:
                        seen(blk_copied)
                        four(52 + k, (chunk_at[k]["XA"], chunk_at[k]["T1T"]))
                    for k in both:
                        four(54 + k, (chunk_at[k]["XA"], chunk_at[k]["Bt"]))
                    seen(blk_copied, 2)
                    seen(blk_out, 2)
                    for k in both:
                        seen(blk_copied)
                        if k:
                            seen(state_out)
                        c, S = chunk_at[k], states[k]
                        four(56 + 2 * k, (c["Bt"], c["U0"]), (c["Kt"], c["Vt"]), (c["Q"], S), (ident, S))
                        four(57 + 2 * k, (c["U0"], c["T1T"]), (c["Vt"], c["T2T"]), (S, c["RpT"]))
                    seen(state_out, 3)
                head_sum(rk["y"], 2, wait=False)
                head_sum(rk["tmp"], 4)
                seen(hsum_in)
                pe.wait_ge(pool_ready, l + 1)
                for g in range(G4):
                    src = rk["pb"] if g % 2 == 0 else rk["pa"]
                    ins = mm(ps[:, 6 + g // 2, (g % 2) * T:(g % 2 + 1) * T], lw[:, 16 + g, :], src[:, g, 16:],
                             start=True, stop=True)
                ins.then_inc(pool_mm, 1)

            def lru():
                products("lgate")
                products("lrec")
                pe.wait_ge(small_in, SMALL["mix2"])
                seen(xc_ready)
                pe.wait_ge(taken, TAKEN["lrec"] + 8)
                for gate in range(2):
                    for h in range(4):
                        for jt in range(2):
                            c = 2 * h + jt
                            for ic in range(2):
                                ins = mm(ps[:, 4 * gate + c // 2, (c % 2) * T:(c % 2 + 1) * T],
                                         lr["wts"][:, ((gate * 4 + h) * 2 + ic) * 2 + jt, :], lr["xc"][:, 2 * h + ic, :],
                                         start=(ic == 0), stop=(ic == 1))
                ins.then_inc(gates_mm, 1)

            def attention():
                products("dkv")
                sum_squares(wide, DC)
                seen(h_split)
                products("dq")
                sum_squares(ml["sq"], 2)
                sum_squares(ml["sq"], 3)
                pe.wait_ge(small_in, SMALL["mix3"])
                seen(lat_in)
                pe.wait_ge(taken, TAKEN["dq"] + 3)
                jobs = [(ml["uk"], 2, ml["ck"], m) for m in range(8)] + [(ml["uq"], 3, ml["cq"], m) for m in range(16)]
                for n in range(0, len(jobs), 2):
                    bank = (n // 2) % 8
                    if n // 2 >= 8:
                        seen(kv_out)
                    for half in range(2):
                        w, kc, rhs, m = jobs[n + half]
                        for c in range(kc):
                            ins = mm(ps[:, bank, half * T:(half + 1) * T], w[:, m * kc + c, :], rhs[:, c, :],
                                     start=(c == 0), stop=(c == kc - 1))
                    ins.then_inc(kv_mm, 1)
                for kt in range(TT):
                    for half in range(2):
                        seen(kv_out)
                        for c in range(2):
                            ins = mm(ps[:, 4 + 2 * kt + half, :], ml["ck"][:, c, kt * P:(kt + 1) * P],
                                     ml["uv"][:, c, half * 512:(half + 1) * 512], start=(c == 0), stop=(c == 1))
                        ins.then_inc(kv_mm, 1)
                seen(kv_out, 8)
                seen(lat_in)

                def scores(h):
                    a, r = 64 * (h % 2), 32 * (h % 4)
                    for q in range(TT):
                        o = ps[:, 2 + h % 2, q * T:(q + 1) * T]
                        mm(o, ml["qn"][a:a + 64, h // 2, q * P:(q + 1) * P], ml["kn"][a:a + 64, h // 2, :],
                           start=True, stop=False)
                        ins = mm(o, ml["qr"][r:r + 32, h // 4, q * P:(q + 1) * P], ml["kr"][r:r + 32, :],
                                 start=False, stop=True)
                    ins.then_inc(sc_mm, 1)

                def turn_weights(h):
                    seen(p_ready)
                    for kt in range(TT):
                        for q in range(TT):
                            ins = pe.transpose(ps[:, 4 + h % 2, kt * T + q * P:kt * T + (q + 1) * P],
                                               ml["p"][:, h % 2, q, kt * P:(kt + 1) * P], ident)
                    ins.then_inc(pt_mm, 1)

                def attend(h):
                    seen(pt_out)
                    if h % 2 == 0 and h >= 4:
                        seen(av_out)
                    for kt in range(TT):
                        ins = mm(ps[:, 6 + (h // 2) % 2, 0:T], ml["vpad"][:, kt, h, :], ml["pT"][:, h % 2, kt, :],
                                 start=(h % 2 == 0 and kt == 0), stop=(h % 2 == 1 and kt == 1))
                    if h % 2:
                        ins.then_inc(av_mm, 1)

                scores(0)
                for h in range(AH):
                    if h + 1 < AH:
                        scores(h + 1)
                    turn_weights(h)
                    if h >= 1:
                        attend(h - 1)
                attend(AH - 1)

            def peer(l):
                products(f"q{l}")
                pe.wait_ge(keys_in, 16 * (l + 1))
                pe.wait_ge(taken, TAKEN[f"q{l}"] + 16)
                for tt in range(TT):
                    for b in range(4):
                        if tt:
                            seen(score_out)
                        for k in range(4):
                            hp = 4 * b + k
                            ins = mm(ps[:, 2 + b, k * P:(k + 1) * P], tk["q"][:, hp, tt * P:(tt + 1) * P],
                                     tk["keys"][:, hp, :], start=True, stop=True)
                        ins.then_inc(score_mm, 1)
                seen(score_out, 4)
                a = 0
                for tt in range(TT):
                    b = STEPS * tt + CHOSEN + 2
                    products(f"u{l}", a, b)
                    a = b
                    seen(chosen)
                    for w in range(3):
                        ins = pe.transpose(ps[:, 6 + tt, w * P:(w + 1) * P], tk["e"][:, w].rearrange("p h k -> p (h k)"), ident)
                    ins.then_inc(chosen_t, 1)
                products(f"u{l}", a)
                pe.wait_ge(taken, TAKEN[f"u{l}"] + KEYS)
                turns = T // 32
                ada, tiles = SEGS[f"ada{l + 1}"][:2] if l < 3 else (0, 0)

                def gate(b):
                    for q in range(4):
                        ins = mm(ps[:, b, q * P:(q + 1) * P], oh1[:, b, q, :], oh2[:, b, q, :], start=True, stop=True)
                    ins.then_inc(gates_t, 1)

                for q in range(8):
                    seen(hot)
                    if q >= 2:
                        seen(gated)
                    gate(q % 2)
                    if tiles:
                        modulate(l + 1, ada + q, ada + q, q, 0, None)
                with_tiles = tiles // 8 - 1 if tiles else 0
                for n, some in ((with_tiles, True), (turns - 1 - with_tiles, False)):
                    if n == 0:
                        continue
                    with seen.loop(n, {hot: 8, gated: 8}) as i:
                        for q in range(8):
                            seen(hot)
                            seen(gated)
                            gate(q % 2)
                            if some:
                                modulate(l + 1, ada + 8 + q + i * 8, ada + 8 + q, q, i + 1, i)
                seen(gated, 2)
                if tiles:
                    turn_row(l + 1, tiles // 8 - 1)
                    pe.wait_ge(mod_ready, l + 2)
                first = SEGS[f"v{l}"][0]

                def step(n, j, k, i):
                    pe.wait_ge(lo_done, n + (1 - WHOLE[f"v{l}"]))
                    pe.wait_ge(wal, k + (1 + KEYS * l))
                    b = j % 4
                    one, last = (i is None and k == 0), (i is None and k == KEYS - 1)
                    for tt in range(TT):
                        up = wa_hi[:, b, tt * P:(tt + 1) * P]
                        down = wa_lo[:, b, tt * P:(tt + 1) * P]
                        for half in range(2):
                            cols = slice(half * 512, (half + 1) * 512)
                            o = ps[:, 2 + 2 * tt + half, :]
                            mm(o, up, t_hi[:, j % SPL, cols], start=one, stop=False)
                            mm(o, up, t_lo[:, j % SPL, cols], start=False, stop=False)
                            ins = mm(o, down, t_hi[:, j % SPL, cols], start=False, stop=last)
                    ins.then_inc(tile_used, 1)
                step(first, first, 0, None)
                tiles_in_loops(pe, first + 1, KEYS - 1, lambda n, j, k, i: step(n, j, k + 1, i))
                seen(moe_out)
                for m in range(4):
                    for c in range(2):
                        for tt in range(TT):
                            ins = pe.transpose(ps[:, [6, 7, 0, 1][m], c * T + tt * P:c * T + (tt + 1) * P],
                                               sum_sb[:, tt, (2 * m + c) * P:(2 * m + c + 1) * P], ident)
                    ins.then_inc(moe_t, 1)

            pe.wait_ge(par_in, 32)
            seen(c_ready, 2)
            for k in range(8):
                modulate(0, k, k, k, 0, None)
            with pe.Fori(0, 5) as i:
                for k in range(8):
                    modulate(0, 8 + k + i * 8, 8 + k, k, i + 1, i)
            turn_row(0, 5)
            for l in range(4):
                sum_squares(wide, DC)
                seen(h_split)
                if l < 2:
                    rwkv(l)
                elif l == 2:
                    lru()
                else:
                    attention()
                seen(h_split)
                products(("out0", "out1", "lout", "wo")[l])
                sum_squares(wide, DC)
                seen(h_split)
                peer(l)
                if l % 2:
                    sum_squares(wide, DC)


def _by_chunk(a, n):
    a = np.asarray(a)
    return np.moveaxis(a.reshape(*a.shape[:-1], n, P), -1, 0)


def _tiles(w, pad=0):
    w = np.asarray(w)
    if pad:
        w = np.concatenate([w, np.zeros((w.shape[0], pad), w.dtype)], axis=1)
    m = w.shape[1] // P
    return w.reshape(DC, P, m, P).transpose(2, 1, 0, 3).reshape(m, P, D)


def _row_tiles(w):
    w = np.asarray(w)
    m = w.shape[1] // D
    return w.reshape(DC, P, m, D).transpose(2, 0, 1, 3).reshape(m * DC, P, D)


def _constants():
    i = np.arange(P)
    row, col = i[:, None], i[None, :]
    same = row // 64 == col // 64
    out = [row == col, np.ones((P, P)), same, np.broadcast_to(col, (P, P)),
           same & (row < col), same & (row > col), same & (row <= col),
           (row // 2 == col // 2) & (row < col), (row // 2 == col // 2) & (row > col)]
    for n in (2, 4, 8, 16, 32):
        out.append((row // (2 * n) == col // (2 * n)) & (row // n > col // n))
    return np.stack([np.asarray(m, np.float32) for m in out], axis=1)


def _layout(i):
    f = np.float32
    par = np.zeros((P, NPAR), f)

    def put(name, v):
        a, n = PCOLS[name]
        par[:, a:a + n] = np.asarray(v).reshape(P, n)

    put("c0", _by_chunk(i["c"], 8))
    put("c1", _by_chunk(i["c_2"], 8))
    for l in range(4):
        b = l // 2
        put(f"ada_b{l}", _by_chunk(i["ada_b_2" if b else "ada_b"][l % 2], 48))
        put(f"mix_g{l}", _by_chunk(i["norm_mix_g_2" if b else "ln1_g"][l % 2], 8))
        put(f"ffn_g{l}", _by_chunk(i["norm_ffn_g_2" if b else "ln2_g"][l % 2], 8))
    for l in range(2):
        mu = np.zeros((15 * P,), f)
        mu[:14 * P] = i["mu_shift"][l]
        if l:
            mu[14 * P:14 * P + 32] = i["vres_mu"][0]
        put(f"mu{l}", _by_chunk(mu, 15))
        for n in ("w0", "a0", "k_k", "k_a", "lnx_g", "lnx_b", "pool_scale"):
            put(f"{n}{l}", _by_chunk(i[n][l], 4))
        put(f"r_k{l}", _by_chunk(np.asarray(i["r_k"][l]).reshape(-1), 4))
    put("vres_v0", _by_chunk(i["vres_v0"][0], 4))
    put("lnf_g", _by_chunk(i["lnf_g"], 8))
    put("conv_w", _by_chunk(i["lru_conv_w_2"][0], 8))
    for n, src in (("conv_b", "lru_conv_b_2"), ("ba", "lru_ba_2"), ("bx", "lru_bx_2"), ("lam", "lru_lambda_2")):
        put(n, _by_chunk(i[src][0], 8))
    put("kv_g", _by_chunk(i["kv_norm_g_2"], 8))
    put("final_g", _by_chunk(i["final_g_2"], 8))
    put("kv_ada_b", _by_chunk(i["kv_ada_b_2"], 16))
    put("ckv_g", _by_chunk(i["mla_kv_latent_g_2"], 2))
    put("cq_g", _by_chunk(i["mla_q_latent_g_2"][0], 3))
    freq = np.float32(10000.0) ** (-np.arange(16, dtype=f) / np.float32(16))
    put("freq", freq[np.arange(P) % 16])
    put("sign", np.where(np.arange(P) % 32 < 16, -1.0, 1.0).astype(f))

    swap = np.r_[16:32, 0:16]
    kr = np.asarray(i["mla_w_kr_2"])
    w = []
    for l in range(4):
        if l == 0:
            w.append(_row_tiles(i["ada_w"][0]))
        if l == 0:
            w += [_tiles(i["w_in"][0]), _tiles(i["w_out"][0])]
        elif l == 1:
            w += [_tiles(i["w_in"][1]), _tiles(i["vres_down"][0], pad=96), _tiles(i["w_out"][1])]
        elif l == 2:
            w += [_tiles(i["lru_w_in_2"][0]), _tiles(i["lru_w_out_2"][0])]
        else:
            w += [_tiles(i["mla_w_dkv_2"]), _tiles(np.tile(kr, (1, 4))),
                  _tiles(np.tile(kr[:, swap], (1, 4))), _tiles(i["mla_w_dq_2"][0]), _tiles(i["mla_w_o_2"][0])]
        w.append(_tiles(i["peer_w_q_2" if l > 1 else "peer_q"][l % 2]))
        if l < 3:
            w.append(_row_tiles(i["ada_w_2" if l > 0 else "ada_w"][(l + 1) % 2]))
        if l == 2:
            w.append(_row_tiles(i["kv_ada_w_2"]))
    w = np.concatenate(w)

    u = np.concatenate([np.asarray(i[n][l]).reshape(KEYS, KEYS, DC, P).transpose(1, 3, 2, 0).reshape(KEYS, P, D)
                        for n in ("peer_u", "peer_u_2") for l in range(2)])
    v = np.concatenate([np.asarray(i[n]).reshape(2, KEYS, KEYS, D) for n in ("peer_v", "peer_v_2")])

    lora = np.zeros((2, P, 20, P), f)
    for l in range(2):
        lora[l, :64, 0:4] = np.asarray(i["w_up"][l]).reshape(64, 4, P)
        lora[l, 64:, 4:8] = np.asarray(i["a_up"][l]).reshape(64, 4, P)
        lora[l, :, 8:12] = np.asarray(i["g_up"][l]).reshape(P, 4, P)
        if l:
            lora[l, :32, 12:16] = np.asarray(i["vres_up"][0]).reshape(32, 4, P)
        lora[l, :, 16:20] = np.asarray(i["pool_w"][l]).transpose(1, 0, 2)

    lru = np.stack([np.asarray(i[n][0]).reshape(4, 2, P, 2, P) for n in ("lru_wa_2", "lru_wx_2")])
    lru = lru.transpose(3, 0, 1, 2, 4, 5).reshape(P, 32, P)

    uq = np.asarray(i["mla_w_uq_2"][0]).reshape(3, P, AH, 96)
    rope = uq[..., 64:]
    parts = [uq[..., :64].reshape(3, P, 8, P), rope.reshape(3, P, 4, P), rope[..., swap].reshape(3, P, 4, P)]
    uq = np.concatenate(parts, axis=2).transpose(1, 2, 0, 3).reshape(P, 48, P)
    uk = np.asarray(i["mla_w_uk_2"]).reshape(2, P, 8, P).transpose(1, 2, 0, 3).reshape(P, 16, P)
    mla = np.concatenate([uq, uk], axis=1)
    uv = np.asarray(i["mla_w_uv_2"]).reshape(2, P, D).transpose(1, 0, 2)

    keys = np.concatenate([np.asarray(i[n]) for n in ("peer_keys", "peer_sub_keys_2")])
    keys = keys.reshape(4, 16, KEYS, P).transpose(0, 3, 1, 2)

    pos = np.arange(1, T + 1, dtype=f)
    inv = np.stack([1.0 / np.minimum(pos, f(win)) for win in WINDOWS]).astype(f)
    inv = np.broadcast_to(inv, (P, 4, T))
    xt = _by_chunk(i["x"][0], 8).transpose(0, 2, 1)
    return {"x_in": xt, "w_tiles": w, "u_tiles": u, "v_tiles": v, "params": par, "consts": _constants(),
            "lora": lora, "lru_w": lru, "mla_w": mla, "mla_uv": uv, "keys_t": keys, "pool_inv": inv,
            "positions": np.asarray(i["positions_2"])}


def kernel(**inputs):
    import concourse.bacc as bacc
    from concourse.bass_utils import run_bass_kernel_spmd as run

    arrays = {n: np.ascontiguousarray(a) for n, a in _layout({n: np.asarray(a) for n, a in inputs.items()}).items()}
    nc = bacc.Bacc("TRN2", target_bir_lowering=False, num_devices=1)
    args = [nc.dram_tensor(n, a.shape, mybir.dt.from_np(a.dtype), kind="ExternalInput").ap() for n, a in arrays.items()]
    out = nc.dram_tensor("out_xt", (P, DC, T), F32, kind="ExternalOutput").ap()
    build(nc, *args, out)
    r = run(nc, [arrays], core_ids=[0])
    got = np.asarray(r.results[0]["out_xt"])
    return np.ascontiguousarray(got.transpose(2, 1, 0)).reshape(1, T, D)
```
